# Optimizing a Trainium2 kernel written in Bass

```python
import math
import jax, jax.numpy as jnp
from jax import lax
import numpy as np

D_MODEL = 1024
BATCH = 1
SEQ = 512
DEPTH = 2
DEC_BATCH = 8
DEC_SEQ = 1
PAST_LEN = 512
PAGE_SIZE = 128

N_EVEN = (DEPTH + 1) // 2
N_ODD = DEPTH // 2

POOL_WIDTH = D_MODEL // 2
POOL_WINDOWS = (2, 4, 8, 16)
POOL_GROUP = POOL_WIDTH // len(POOL_WINDOWS)
POOL_BUF = max(POOL_WINDOWS) - 1
DIFF_HEADS = 4
DIFF_HALF = 64
DIFF_HEAD_DIM = 2 * DIFF_HALF
DIFF_WIDTH = DIFF_HEADS * DIFF_HEAD_DIM
Q_BLOCK = 128
EVEN_IN = POOL_WIDTH + 3 * DIFF_WIDTH
EVEN_MIX = POOL_WIDTH + DIFF_WIDTH
REL_BUCKETS = 32
REL_MAX_DIST = 128
GDN_HEADS = 8
GDN_DK = 128
GDN_DV = 128
GDN_CONV = 4
GDN_CHUNK = 64
GDN_QKV = GDN_HEADS * (2 * GDN_DK + GDN_DV)
ODD_IN = GDN_QKV + GDN_HEADS * GDN_DV + 2 * GDN_HEADS
D_FF = -(-8 * D_MODEL // (3 * 256)) * 256
EPS = 1e-6

kernel_name = 'hybrid_pool_diffattn_gdn_decode_step'

def rms_norm(x, g):
    xf = x.astype(jnp.float32)
    y = xf * lax.rsqrt(jnp.mean(xf * xf, -1, keepdims=True) + EPS)
    return (y * g.astype(jnp.float32)).astype(x.dtype)

def l2_normalize(x):
    xf = x.astype(jnp.float32)
    return xf * lax.rsqrt(jnp.sum(xf * xf, -1, keepdims=True) + EPS)

def swiglu(h, w_gu, w_d):
    gu = h @ w_gu
    return (jax.nn.silu(gu[..., :D_FF]) * gu[..., D_FF:]) @ w_d

def pool_mix(u, buf, pos, pool_w, pool_scale):
    T = u.shape[1]
    ext = jnp.concatenate([buf, u.astype(buf.dtype)], axis=1)
    cs = jnp.pad(jnp.cumsum(ext.astype(jnp.float32), axis=1), ((0, 0), (1, 0), (0, 0)))
    uf = u.astype(jnp.float32)
    outs = []
    for g, w in enumerate(POOL_WINDOWS):
        sl = slice(g * POOL_GROUP, (g + 1) * POOL_GROUP)
        win = cs[:, POOL_BUF + 1:POOL_BUF + 1 + T, sl] - cs[:, POOL_BUF + 1 - w:POOL_BUF + 1 - w + T, sl]
        cnt = jnp.minimum(pos + 1, w).astype(jnp.float32)[None, :, None]
        d = win / cnt - uf[:, :, sl]
        outs.append(jnp.einsum('btc,cd->btd', d, pool_w[g].astype(jnp.float32)))
    y = jnp.concatenate(outs, -1) * pool_scale.astype(jnp.float32)
    return y.astype(u.dtype), ext[:, -POOL_BUF:]

def rel_bucket(n):
    max_exact = REL_BUCKETS // 2
    nf = jnp.maximum(n, 1).astype(jnp.float32)
    large = max_exact + (jnp.log(nf / max_exact) / math.log(REL_MAX_DIST / max_exact)
                         * (REL_BUCKETS - max_exact)).astype(jnp.int32)
    large = jnp.minimum(large, REL_BUCKETS - 1)
    return jnp.where(n < max_exact, n, large)

def diff_attention(q, k, v, q_pos, k_pos, rel_table, lam):
    B, T, H, Dq = q.shape
    qb = min(Q_BLOCK, T)
    nb = -(-T // qb)
    pad = nb * qb - T
    qp = jnp.pad(q, ((0, 0), (0, pad), (0, 0), (0, 0)))
    posp = jnp.pad(q_pos, (0, pad), mode='edge')
    q_blocks = jnp.moveaxis(qp.reshape(B, nb, qb, H, Dq), 1, 0)
    p_blocks = posp.reshape(nb, qb)
    kf = k.astype(jnp.float32)
    vf = v.astype(jnp.float32)
    k1, k2 = kf[..., :DIFF_HALF], kf[..., DIFF_HALF:]
    table = rel_table.astype(jnp.float32)
    scale = DIFF_HALF ** -0.5

    def block(args):
        q_blk, p_blk = args
        qf = q_blk.astype(jnp.float32)
        dist = p_blk[:, None] - k_pos[None, :]
        causal = (dist >= 0)[None, None]
        bias = jnp.transpose(table[rel_bucket(jnp.maximum(dist, 0))], (2, 0, 1))[None]

        def probs(qh, kh):
            s = jnp.einsum('bqhd,bkhd->bhqk', qh, kh) * scale + bias
            return jax.nn.softmax(jnp.where(causal, s, -jnp.inf), axis=-1)

        a = probs(qf[..., :DIFF_HALF], k1) - lam * probs(qf[..., DIFF_HALF:], k2)
        return jnp.einsum('bhqk,bkhd->bqhd', a, vf)

    out = lax.map(block, (q_blocks, p_blocks))
    return jnp.moveaxis(out, 0, 1).reshape(B, nb * qb, H, v.shape[-1])[:, :T]

def pool_diff_mixer(h, pool_buf, k_past, v_past, layer, rel_bias, w_in, pool_w, pool_scale,
                    lq1, lk1, lq2, lk2, subln_w, w_out):
    B, T, _ = h.shape
    P = k_past.shape[1]
    proj = h @ w_in
    u = proj[..., :POOL_WIDTH]
    o0 = POOL_WIDTH
    q = proj[..., o0:o0 + DIFF_WIDTH].reshape(B, T, DIFF_HEADS, DIFF_HEAD_DIM)
    k_new = proj[..., o0 + DIFF_WIDTH:o0 + 2 * DIFF_WIDTH].reshape(B, T, DIFF_HEADS, DIFF_HEAD_DIM)
    v_new = proj[..., o0 + 2 * DIFF_WIDTH:].reshape(B, T, DIFF_HEADS, DIFF_HEAD_DIM)
    q_pos = P + jnp.arange(T, dtype=jnp.int32)
    y_pool, new_buf = pool_mix(u, pool_buf, q_pos, pool_w, pool_scale)
    lam_init = 0.8 - 0.6 * math.exp(-0.3 * layer)
    f = lambda a: a.astype(jnp.float32)
    lam = jnp.exp(jnp.sum(f(lq1) * f(lk1))) - jnp.exp(jnp.sum(f(lq2) * f(lk2))) + lam_init
    k_all = jnp.concatenate([k_past, k_new.astype(k_past.dtype)], axis=1)
    v_all = jnp.concatenate([v_past, v_new.astype(v_past.dtype)], axis=1)
    k_pos = jnp.arange(P + T, dtype=jnp.int32)
    o = diff_attention(q, k_all, v_all, q_pos, k_pos, rel_bias, lam)
    o = rms_norm(o, subln_w) * (1.0 - lam_init)
    mixed = jnp.concatenate([y_pool, o.reshape(B, T, DIFF_WIDTH).astype(h.dtype)], axis=-1)
    return mixed @ w_out, new_buf, k_new, v_new

def _chunks(a, C, nc):
    B, T = a.shape[:2]
    a = jnp.pad(a.astype(jnp.float32), [(0, 0), (0, nc * C - T)] + [(0, 0)] * (a.ndim - 2))
    a = a.reshape((B, nc, C) + a.shape[2:])
    return jnp.moveaxis(jnp.moveaxis(a, 3, 2), 1, 0)

def gated_delta_rule(q, k, v, g, beta, S0):
    B, T, H, _ = q.shape
    DV = v.shape[-1]
    C = min(GDN_CHUNK, T)
    nc = -(-T // C)
    qc, kc, vc = _chunks(q, C, nc), _chunks(k, C, nc), _chunks(v, C, nc)
    gc, bc = _chunks(g, C, nc), _chunks(beta, C, nc)
    Gc = jnp.cumsum(gc, axis=-1)
    idx = jnp.arange(C)
    incl = idx[:, None] >= idx[None, :]
    strict = idx[:, None] > idx[None, :]
    decay = jnp.exp(jnp.where(incl, Gc[..., :, None] - Gc[..., None, :], -jnp.inf))
    kk = jnp.einsum('...id,...jd->...ij', kc, kc)
    M = jnp.eye(C, dtype=jnp.float32) + jnp.where(strict, bc[..., :, None] * kk * decay, 0.0)
    gam = jnp.exp(Gc)
    W = lax.linalg.triangular_solve(M, (bc * gam)[..., None] * kc, left_side=True, lower=True, unit_diagonal=True)
    U = lax.linalg.triangular_solve(M, bc[..., None] * vc, left_side=True, lower=True, unit_diagonal=True)
    qk = jnp.einsum('...id,...jd->...ij', qc, kc) * decay
    q_dec = gam[..., None] * qc
    k_dec = jnp.exp(Gc[..., -1:] - Gc)[..., None] * kc
    g_last = jnp.exp(Gc[..., -1])

    def step(S, xs):
        W_, U_, qk_, qd_, kd_, gl_ = xs
        u_ = U_ - jnp.einsum('bhck,bhkv->bhcv', W_, S)
        o_ = jnp.einsum('bhck,bhkv->bhcv', qd_, S) + jnp.einsum('bhij,bhjv->bhiv', qk_, u_)
        S = gl_[..., None, None] * S + jnp.einsum('bhck,bhcv->bhkv', kd_, u_)
        return S, o_

    S_fin, O = lax.scan(step, S0.astype(jnp.float32), (W, U, qk, q_dec, k_dec, g_last))
    O = jnp.transpose(O, (1, 0, 3, 2, 4)).reshape(B, nc * C, H, DV)[:, :T]
    return O, S_fin

def gdn_mixer(h, conv_buf, S0, w_in, conv_w, a_log, dt_bias, o_norm, w_out):
    B, T, _ = h.shape
    HK, HV = GDN_HEADS * GDN_DK, GDN_HEADS * GDN_DV
    proj = h @ w_in
    qkv = proj[..., :GDN_QKV]
    z = proj[..., GDN_QKV:GDN_QKV + HV]
    a = proj[..., GDN_QKV + HV:GDN_QKV + HV + GDN_HEADS]
    b = proj[..., GDN_QKV + HV + GDN_HEADS:]
    ext = jnp.concatenate([conv_buf, qkv.astype(conv_buf.dtype)], axis=1)
    cw = conv_w.astype(jnp.float32)
    conv = ext[:, 0:T].astype(jnp.float32) * cw[0]
    for i in range(1, GDN_CONV):
        conv = conv + ext[:, i:i + T].astype(jnp.float32) * cw[i]
    conv = jax.nn.silu(conv)
    q = l2_normalize(conv[..., :HK].reshape(B, T, GDN_HEADS, GDN_DK)) * (GDN_DK ** -0.5)
    k = l2_normalize(conv[..., HK:2 * HK].reshape(B, T, GDN_HEADS, GDN_DK))
    v = conv[..., 2 * HK:].reshape(B, T, GDN_HEADS, GDN_DV)
    g = -jnp.exp(a_log.astype(jnp.float32)) * jax.nn.softplus(a.astype(jnp.float32) + dt_bias.astype(jnp.float32))
    beta = jax.nn.sigmoid(b.astype(jnp.float32))
    o, S = gated_delta_rule(q, k, v, g, beta, S0)
    o = rms_norm(o, o_norm) * jax.nn.silu(z.astype(jnp.float32).reshape(B, T, GDN_HEADS, GDN_DV))
    y = o.reshape(B, T, HV).astype(h.dtype) @ w_out
    return y, ext[:, -(GDN_CONV - 1):], S.astype(S0.dtype)

def setup_inputs(seed: int = 0) -> dict:
    key = jax.random.key(seed)
    ks = jax.random.split(key, 32)
    f32 = jnp.float32

    def nrm(i, shape, scale):
        return jax.random.normal(ks[i], shape, f32) * scale

    n_pages = PAST_LEN // PAGE_SIZE
    n_used = DEC_BATCH * n_pages
    n_pool = n_used + -(-n_used // 4)
    perm = jax.random.permutation(ks[4], n_pool)
    page_table = perm[:n_used].reshape(DEC_BATCH, n_pages).astype(jnp.int32)
    dt = jnp.exp(jax.random.uniform(ks[24], (N_ODD, GDN_HEADS), f32, math.log(1e-3), math.log(1e-1)))
    return {
        'x_prompt': nrm(0, (BATCH, SEQ, D_MODEL), 1.0),
        'x_sample': nrm(1, (DEC_BATCH, DEC_SEQ, D_MODEL), 1.0),
        'cache_k': nrm(2, (n_pool, N_EVEN, PAGE_SIZE, DIFF_HEADS, DIFF_HEAD_DIM), 1.0),
        'cache_v': nrm(3, (n_pool, N_EVEN, PAGE_SIZE, DIFF_HEADS, DIFF_HEAD_DIM), 1.0),
        'page_table': page_table,
        'state_pool': nrm(5, (N_EVEN, DEC_BATCH, POOL_BUF, POOL_WIDTH), 1.0),
        'state_conv': nrm(6, (N_ODD, DEC_BATCH, GDN_CONV - 1, GDN_QKV), 1.0),
        'state_delta': nrm(7, (N_ODD, DEC_BATCH, GDN_HEADS, GDN_DK, GDN_DV), 0.5),
        'norm_mix': 1.0 + nrm(8, (DEPTH, D_MODEL), 0.02),
        'norm_ffn': 1.0 + nrm(9, (DEPTH, D_MODEL), 0.02),
        'norm_final': 1.0 + nrm(10, (D_MODEL,), 0.02),
        'rel_bias': nrm(11, (REL_BUCKETS, DIFF_HEADS), 0.5),
        'w_in_even': nrm(12, (N_EVEN, D_MODEL, EVEN_IN), D_MODEL ** -0.5),
        'pool_w': nrm(13, (N_EVEN, len(POOL_WINDOWS), POOL_GROUP, POOL_GROUP), POOL_GROUP ** -0.5),
        'pool_scale': 1.0 + nrm(14, (N_EVEN, POOL_WIDTH), 0.02),
        'lambda_q1': nrm(15, (N_EVEN, DIFF_HALF), 0.1),
        'lambda_k1': nrm(16, (N_EVEN, DIFF_HALF), 0.1),
        'lambda_q2': nrm(17, (N_EVEN, DIFF_HALF), 0.1),
        'lambda_k2': nrm(18, (N_EVEN, DIFF_HALF), 0.1),
        'subln_w': 1.0 + nrm(19, (N_EVEN, DIFF_HEAD_DIM), 0.02),
        'w_out_even': nrm(20, (N_EVEN, EVEN_MIX, D_MODEL), EVEN_MIX ** -0.5),
        'w_in_odd': nrm(21, (N_ODD, D_MODEL, ODD_IN), D_MODEL ** -0.5),
        'conv_w': nrm(22, (N_ODD, GDN_CONV, GDN_QKV), 0.5),
        'a_log': jnp.log(jax.random.uniform(ks[23], (N_ODD, GDN_HEADS), f32, 1.0, 16.0)),
        'dt_bias': dt + jnp.log(-jnp.expm1(-dt)),
        'o_norm': 1.0 + nrm(25, (N_ODD, GDN_DV), 0.02),
        'w_out_odd': nrm(26, (N_ODD, GDN_HEADS * GDN_DV, D_MODEL), (GDN_HEADS * GDN_DV) ** -0.5),
        'w_gate_up': nrm(27, (DEPTH, D_MODEL, 2 * D_FF), D_MODEL ** -0.5),
        'w_down': nrm(28, (DEPTH, D_FF, D_MODEL), D_FF ** -0.5),
    }

def reference(x_prompt, x_sample, cache_k, cache_v, page_table, state_pool, state_conv, state_delta,
              norm_mix, norm_ffn, norm_final, rel_bias,
              w_in_even, pool_w, pool_scale, lambda_q1, lambda_k1, lambda_q2, lambda_k2, subln_w, w_out_even,
              w_in_odd, conv_w, a_log, dt_bias, o_norm, w_out_odd,
              w_gate_up, w_down):
    hp, hs = x_prompt, x_sample
    bp, bs = hp.shape[0], hs.shape[0]
    n_pages = page_table.shape[1]
    k_p, v_p, k_s, v_s, pool_p, pool_s = [], [], [], [], [], []
    conv_p, conv_s, delta_p, delta_s = [], [], [], []
    for layer in range(DEPTH):
        j = layer // 2
        zp = rms_norm(hp, norm_mix[layer])
        zs = rms_norm(hs, norm_mix[layer])
        if layer % 2 == 0:
            wts = (rel_bias, w_in_even[j], pool_w[j], pool_scale[j], lambda_q1[j], lambda_k1[j],
                   lambda_q2[j], lambda_k2[j], subln_w[j], w_out_even[j])
            no_past = jnp.zeros((bp, 0, DIFF_HEADS, DIFF_HEAD_DIM), hp.dtype)
            yp, pb, kp, vp = pool_diff_mixer(zp, jnp.zeros((bp, POOL_BUF, POOL_WIDTH), hp.dtype),
                                             no_past, no_past, layer, *wts)
            k_past = cache_k[page_table, j].reshape(bs, n_pages * PAGE_SIZE, DIFF_HEADS, DIFF_HEAD_DIM)
            v_past = cache_v[page_table, j].reshape(bs, n_pages * PAGE_SIZE, DIFF_HEADS, DIFF_HEAD_DIM)
            ys, sb, ks_, vs_ = pool_diff_mixer(zs, state_pool[j], k_past, v_past, layer, *wts)
            k_p.append(kp); v_p.append(vp); k_s.append(ks_); v_s.append(vs_)
            pool_p.append(pb); pool_s.append(sb)
        else:
            wts = (w_in_odd[j], conv_w[j], a_log[j], dt_bias[j], o_norm[j], w_out_odd[j])
            yp, cb_p, S_p = gdn_mixer(zp, jnp.zeros((bp, GDN_CONV - 1, GDN_QKV), hp.dtype),
                                      jnp.zeros((bp, GDN_HEADS, GDN_DK, GDN_DV), hp.dtype), *wts)
            ys, cb_s, S_s = gdn_mixer(zs, state_conv[j], state_delta[j], *wts)
            conv_p.append(cb_p); conv_s.append(cb_s); delta_p.append(S_p); delta_s.append(S_s)
        hp = hp + yp
        hs = hs + ys
        hp = hp + swiglu(rms_norm(hp, norm_ffn[layer]), w_gate_up[layer], w_down[layer])
        hs = hs + swiglu(rms_norm(hs, norm_ffn[layer]), w_gate_up[layer], w_down[layer])
    y_prompt = rms_norm(hp, norm_final)
    y_sample = rms_norm(hs, norm_final)
    return (y_prompt, y_sample,
            jnp.stack(k_p, axis=1), jnp.stack(v_p, axis=1), jnp.stack(k_s, axis=1), jnp.stack(v_s, axis=1),
            jnp.stack(pool_p), jnp.stack(pool_s), jnp.stack(conv_p), jnp.stack(conv_s),
            jnp.stack(delta_p), jnp.stack(delta_s))


_drawn_inputs = setup_inputs


def setup_inputs(seed=0):
    import zlib

    import numpy as np

    out = dict(_drawn_inputs(seed))
    spreads = {}
    factors = {'norm_ffn': 3.006,
     'norm_final': 2.871,
     'pool_scale': 3.627,
     'lambda_k2': 2.798,
     'subln_w': 3.87,
     'o_norm': 6.942}
    for name, (base, spread) in spreads.items():
        noise = np.random.default_rng([zlib.crc32(name.encode()), seed]).standard_normal(out[name].shape)
        drawn = base * np.exp(spread * noise) if base else spread * noise
        out[name] = __import__('jax').numpy.asarray(drawn.astype(out[name].dtype))
    for name, factor in factors.items():
        out[name] = (out[name] * factor).astype(out[name].dtype)
    return out
```

```python
import concourse.bass as bass
from concourse import mybir
from contextlib import ExitStack

D, SEQ, NDEC, PAST, PAGE = 1024, 512, 8, 512, 128
T = SEQ + NDEC
CH = T // 2
KD = D // 128
H0, HALF = 4, 64
PW = (2, 4, 8, 16)
DFF = 2816
KF = DFF // 128
HG = 8
NPG = PAST // PAGE
WS = 64.0
EPS = 1e-6
LAM0 = 0.2
NEG = -1e30
NB = 640
SKEW = NB + 1

UNIT = KF * 128
PHASES = (("in0", 8, 2, KD * 256), ("out0", 4, 2, KD * 256), ("gu0", 22, 2, KD * 256), ("dn0", 8, 1, UNIT),
          ("in1", 16, 2, KD * 256), ("out1", 4, 2, KD * 256), ("gu1", 22, 2, KD * 256), ("dn1", 8, 1, UNIT))
FIRST_UNIT, FIRST_TILE, WORDS = {}, {}, []
_u = _t = 0
for _n, _c, _j, _w in PHASES:
    FIRST_UNIT[_n], FIRST_TILE[_n] = _u, _t
    _u, _t = _u + _c, _t + _c * _j
    WORDS += [_w] * _c
UNITS = _u
HEAD_TILES = {
    "pe": ["gb_ps", "qk_ps", "kk_ps", "tk_ps", "n_ps", "tkb_ps", "tv_ps", "d2_ps", "dt2_ps", "d4_ps", "dt4_ps", "y2_ps",
           "d8_ps", "y3_ps", "y4_ps"] + ["x_ps", "z_ps", "v_ps"] * 3 + ["w_ps", "u_ps", "ds_ps"] +
          ["ws_ps", "ds_ps"] * 3 + ["o_ps"],
    "act": ["gam", "gd", "et", "kd4", "nf", "kd", "d2", "bv", "d4", "dt4", "d8", "x", "x", "x", "w", "o"],
    "dve": ["kb", "ex", "bd", "vb", "nt", "dt", "at", "d", "y1", "dt2", "kp", "y2", "y3", "xt"] + ["z", "xt"] * 3 +
           ["u", "s"] * 4,
    "pool": ["selb", "ets", "eti", "kbg", "om", "om", "om", "qd"],
}
P_MIX, P_FFN, P_FIN, P_POOL, P_SUB, P_ONORM, P_N = 0, 16, 32, 40, 44, 45, 46


def hybrid_trunk(nc, xT, w_in0, w_out0, w_gu, w_dn, w_in1, w_out1, params, convw, wab, gates, cache_k, cache_v, pages,
                 pool_w, pool_state, conv_state, delta_state, rel_tab, onehot, lam_vec, sel64, invcnt, masks,
                 o_y, o_k, o_v, o_pp, o_ps, o_ct, o_cs, o_dp, o_ds):
    f32, f16, i32 = mybir.dt.float32, mybir.dt.float16, mybir.dt.int32
    ALU, ACT, AX = mybir.AluOpType, mybir.ActivationFunctionType, mybir.AxisListType
    MUL, ADD, SUB, MAX, MIN = ALU.mult, ALU.add, ALU.subtract, ALU.max, ALU.min

    ctx = ExitStack()
    with ctx:
        def sb(name, shape, dt=f32):
            return ctx.enter_context(nc.sbuf_tensor(name, shape, dt))

        def sem(name):
            return ctx.enter_context(nc.semaphore(name))

        hT = sb("hT", [128, KD, T])
        zh = sb("zh", [128, KD, T], f16)
        zl = sb("zl", [128, KD, T], f16)
        stage = sb("stage", [128, 2, UNIT])
        wh = sb("wh", [128, 2, UNIT], f16)
        wl = sb("wl", [128, 2, UNIT], f16)
        rstd = sb("rstd", [128, T])
        sq = sb("sq", [128, 2, T])
        ssq = sb("ssq", [128, T])
        par = sb("par", [128, P_N])
        ident = sb("ident", [128, 128])
        ones = sb("ones", [128, 128])
        onesD = sb("onesD", [128, 128])
        onesH = sb("onesH", [128, 128])
        epsc = sb("epsc", [128, 3])
        pt = sb("pt", [1, NDEC * NPG], i32)
        ARENA = 30900
        arena = sb("arena", [128, ARENA])
        P = ctx.enter_context(nc.psum_tensor("P", [128, 8, 512], f32))
        pm = [P[:, 2 * j:2 * j + 2, 0:CH] for j in range(2)]
        stat = P[:, 4:6, 0:CH]

        def carver():
            at = [0]

            def take(n, dt=f32):
                n32 = n if dt == f32 else n // 2
                at[0] += n32
                assert at[0] <= ARENA, at[0]
                v = arena[:, at[0] - n32:at[0]]
                return v if dt == f32 else v.bitcast(dt)
            return take

        a0 = carver()
        qkv = a0(12 * T).rearrange("p (a t) -> p a t", t=T)
        mix = a0(KD * T)
        mh = mix[:, 0:KD * T // 2].bitcast(f16).rearrange("p (a t) -> p a t", t=T)
        ml = mix[:, KD * T // 2:].bitcast(f16).rearrange("p (a t) -> p a t", t=T)
        UP = 16 + T
        upad = a0(4 * UP).rearrange("p (g t) -> p g t", t=UP)
        win = a0(2 * (16 + SEQ)).rearrange("p (a t) -> p a t", a=2)
        dT = a0(T)
        ext = a0(4 * NDEC * 16).rearrange("p (g b t) -> p g b t", g=4, b=NDEC)
        extsum = a0(4 * NDEC).rearrange("p (g b) -> p g b", g=4)
        inv = a0(15)
        vtok = a0(4 * 512).rearrange("p (c n) -> p c n", c=4)
        biasT = a0(4 * 512).rearrange("p (h n) -> p h n", h=4)
        pr = a0(2 * 512).rearrange("p (m n) -> p m n", m=2)
        am = a0(512)
        aT = a0(512)
        mx, nm, ls, rl = a0(2), a0(2), a0(2), a0(2)
        oT = a0(4 * T).rearrange("p (h t) -> p h t", t=T)
        NKV = 2
        kv = a0(NKV * NPG * 512).rearrange("p (s g n) -> p s g n", s=NKV, g=NPG)
        qpad = a0(NDEC * 264)
        poolw = a0(4 * 128).rearrange("p (g n) -> p g n", g=4)
        qk2 = a0(64)
        td = a0(PAST + 1)
        tsm = a0(8)
        comb = a0(32)
        pnew = a0(128)
        aD = a0(5 * 32)
        vn = a0(32)
        lamt = a0(4)
        lpr = a0(2)
        lame = a0(2)
        nlam = a0(1)
        subw = a0(1)
        sel = a0(34)
        tab = a0(4)
        tab64 = a0(64)
        oh = oT.rearrange("p h t -> p (h t)")[:, 0:NB + PAST + 1]
        tabB = am.rearrange("p (h n) -> p h n", h=4)
        strips = mix[:, 0:H0 * NB].rearrange("p (h n) -> p h n", h=H0)
        oy = pr.rearrange("p m n -> p (m n)")
        ors = [oy[:, 0:T], vtok.rearrange("p c n -> p (c n)")[:, 0:T]]
        yn = [biasT.rearrange("p h n -> p (h n)")[:, i * T:(i + 1) * T] for i in range(2)]

        a2 = carver()
        qkvc = a2(24 * T).rearrange("p (a t) -> p a t", t=T)
        sz = a2(HG * T).rearrange("p (a t) -> p a t", t=T)
        tail = a2(24 * 11).rearrange("p (a t) -> p a t", t=11)
        cext = a2(24 * NDEC * 4).rearrange("p (a b t) -> p a b t", a=24, b=NDEC)
        cw = a2(96).rearrange("p (i a) -> p i a", i=4)
        msk = a2(6 * 128).rearrange("p (m n) -> p m n", m=6)
        rows = a2(T)
        tokm = a2(4 * 40).rearrange("p (c n) -> p c n", c=4)
        selb = a2(2 * 2 * 128).rearrange("p (s m n) -> p s m n", s=2, m=2)
        gD, bD, qkD = (a2(64).rearrange("p (b h) -> p b h", b=NDEC) for _ in range(3))
        kq = a2(128).rearrange("p (b h m) -> p b h m", b=NDEC, m=2)
        qkp = a2(64)
        gate = a2(8)
        sall = a2(HG * 128).rearrange("p (h n) -> p h n", h=HG)
        sping = a2(2 * 128).rearrange("p (s n) -> p s n", s=2)
        d4, kd4 = a2(4), a2(4)
        mix1 = a2(KD * T)
        mh1 = mix1[:, 0:KD * T // 2].bitcast(f16).rearrange("p (a t) -> p a t", t=T)
        ml1 = mix1[:, KD * T // 2:].bitcast(f16).rearrange("p (a t) -> p a t", t=T)
        pre = a2(2 * 524).rearrange("p (s t) -> p s t", s=2)
        rest = a2(8 * 512)
        spots = [rest[:, i * 512:(i + 1) * 512] for i in range(8)] + [mix1[:, i * 512:(i + 1) * 512] for i in range(8)]
        spots += [pre.rearrange("p s t -> p (s t)")[:, i * 512:(i + 1) * 512] for i in range(2)]
        (et, ets_nf_u, gamB, kbg_w, nt_z, At, dd, ddt, off1, off2, off3, d2_8, dt2_x, ya, yb, Kd, Kp, bV) = spots
        offs = (off1, off2, off3)
        rs2 = rest[:, 0:2 * T].rearrange("p (s t) -> p s t", s=2)
        rowt = rest[:, 2 * T:6 * T].rearrange("p (s t) -> p s t", s=4)
        wabf = rest[:, 6 * T:6 * T + 320]
        wabh, wabl = (rest[:, 6 * T + 320 + 160 * i:6 * T + 480 + 160 * i].bitcast(f16).rearrange(
            "p (k n) -> p k n", k=KD) for i in range(2))
        ctmp = mix1[:, 0:64].rearrange("p (a b) -> p a b", a=8)
        dS = mix1[:, 0:2048].rearrange("p (s n) -> p s n", s=2)
        um = mix1[:, 2048:3072]
        ud, od, t8 = (mix1[:, 3072 + 64 * i:3136 + 64 * i].rearrange("p (b h) -> p b h", b=NDEC) for i in range(3))
        krow = mix1[:, 3264:3392]
        urow = mix1[:, 3392:3520]
        ors1 = [rest[:, i * T:(i + 1) * T] for i in range(2)]
        yn1 = [rest[:, (2 + i) * T:(3 + i) * T] for i in range(2)]

        a1 = carver()
        fh = a1(KF * T, f16).rearrange("p (a t) -> p a t", t=T)
        fl = a1(KF * T, f16).rearrange("p (a t) -> p a t", t=T)
        gt = a1(2 * T).rearrange("p (a t) -> p a t", t=T)
        ut = a1(2 * T).rearrange("p (a t) -> p a t", t=T)
        gu = a1(2 * T).rearrange("p (a t) -> p a t", t=T)
        yf = a1(2 * T).rearrange("p (a t) -> p a t", t=T)

        scratch = nc.dram_tensor("bias_scratch", (4, 128 * SKEW), f32).ap()

        x_in, c_in, aux_in = sem("x_in"), sem("c_in"), sem("aux_in")
        kv_in = [sem(f"kv_in{i}") for i in range(NKV)]
        w_in = [sem(f"w_in{i}") for i in range(2)]
        consts = sem("consts")
        hi_ready, lo_ready = sem("hi_ready"), sem("lo_ready")
        mm_done, pm_free = sem("mm_done"), sem("pm_free")
        z_hi, z_lo, sq_ready, ssq_ready, stat_ready = (sem("z_hi"), sem("z_lo"),
                                                                sem("sq_ready"), sem("ssq_ready"), sem("stat_ready"))
        ln_done, rstd_ready = sem("ln_done"), sem("rstd_ready")
        silu_done, prod_done, f_hi, f_lo = sem("silu_done"), sem("prod_done"), sem("f_hi"), sem("f_lo")
        outs, dve_step, pool_step, act_step = sem("outs"), sem("dve_step"), sem("pool_step"), sem("act_step")
        y_ready = sem("y_ready")
        y_out = [sem(f"y_out{i}") for i in range(2)]
        tabB_ready, strip_ps, strip_ready, strip_out, bias_in = (sem("tabB_ready"), sem("strip_ps"),
                                                                 sem("strip_ready"), sem("strip_out"), sem("bias_in"))
        lam_pr, lam_ps, lam_ready = sem("lam_pr"), sem("lam_ps"), sem("lam_ready")
        vt_ps, vt_done = sem("vt_ps"), sem("vt_done")
        qpad_ready, s_ready, s_read, nm_ready, exp_done, a_ready = (sem("qpad_ready"), sem("s_ready"), sem("s_read"),
                                                                    sem("nm_ready"), sem("exp_done"), sem("a_ready"))
        at_ps, at_done, pv_done, o_evac = sem("at_ps"), sem("at_done"), sem("pv_done"), sem("o_evac")
        kv_used, dp_ready, comb_ready, ad_ps, ad_done = (sem("kv_used"), sem("dp_ready"),
                                                         sem("comb_ready"), sem("ad_ps"), sem("ad_done"))
        dec_o = sem("dec_o")
        d_ready, pool_ps, m_hi, m_lo = sem("d_ready"), sem("pool_ps"), sem("m_hi"), sem("m_lo")
        osq, ostat, oln, ors_ready, yn_ready = (sem("osq"), sem("ostat"), sem("oln"), sem("ors_ready"),
                                                sem("yn_ready"))
        dext = sem("dext")
        l1_in, l1_free, ab_split, ab_ps, ab_step, rows_ready, tok_ps, tok_done = (
            sem("l1_in"), sem("l1_free"), sem("ab_split"), sem("ab_ps"), sem("ab_step"), sem("rows_ready"),
            sem("tok_ps"), sem("tok_done"))
        conv_done, tail_done, convd_done, csilu = (sem("conv_done"), sem("tail_done"), sem("convd_done"),
                                                   sem("csilu"))
        nsq, nstat, nln, nrs, nq = sem("nsq"), sem("nstat"), sem("nln"), sem("nrs"), sem("nq")
        head_done = {e: sem(f"head_{e}") for e in HEAD_TILES}
        S = {n: head_done[e] for e, tiles in HEAD_TILES.items() for n in tiles}

        def G(name, n):
            e = next(e for e, tiles in HEAD_TILES.items() if name in tiles)
            at = [i for i, t in enumerate(HEAD_TILES[e]) if t == name]
            h, i = divmod(n - 1, len(at))
            return head_done[e], len(HEAD_TILES[e]) * h + at[i] + 1
        st_in = [sem(f"st_in{i}") for i in range(2)]
        st_out = [sem(f"st_out{i}") for i in range(2)]
        dprep, qk_dps, kqs_ps, du, du_ps, krow_ps, krow_s, urow_s, um_s, outer_ps, sdec, snew, zsilu = (
            sem("dprep"), sem("qk_dps"), sem("kqs_ps"), sem("du"), sem("du_ps"), sem("krow_ps"), sem("krow_s"),
            sem("urow_s"), sem("um_s"), sem("outer_ps"), sem("sdec"), sem("snew"), sem("zsilu"))
        o1sq, o1stat, o1ln, o1rs, yo, yz, m1_hi, m1_lo = (sem("o1sq"), sem("o1stat"), sem("o1ln"), sem("o1rs"),
                                                          sem("yo"), sem("yz"), sem("m1_hi"), sem("m1_lo"))

        block = ctx.enter_context(nc.Block())

        def bh(i):
            return divmod(i, H0)

        def paired(ap):
            return ap.rearrange("p (c n) -> p c n", c=2)

        @block.sync
        def _(sp):
            def weights(src, u, j, index, words):
                if not isinstance(u, int) or u >= 2:
                    sp.wait_ge(hi_ready, u - 1)
                    sp.wait_ge(lo_ready, u - 1)
                sp.dma_start(stage[:, j, 0:words], src[index].rearrange("a p n -> (a p) n")
                             if not isinstance(index, int) else src[index]).then_inc(w_in[j], 16)

            def stream(src, name, skip=0):
                base = FIRST_UNIT[name]
                n, words = [(c, w) for a, c, _, w in PHASES if a == name][0]
                with sp.Fori(skip // 2, n // 2) as i:
                    for j in range(2):
                        weights(src, base + 2 * i + j, j, bass.ds(2 * i + j, 1), words)

            sp.dma_start(hT[:, :, :], xT).then_inc(x_in, 16)
            sp.dma_start(par[:, :], params).then_inc(x_in, 16)
            for u in range(2):
                weights(w_in0, u, u, u, WORDS[u])
            sp.dma_start(pt[:, :], pages).then_inc(c_in, 16)
            sp.dma_start(oh[0:33, :], onehot).then_inc(c_in, 16)
            sp.dma_start(tab[0:33, :], rel_tab).then_inc(c_in, 16)
            sp.dma_start(lamt[0:64, :], lam_vec).then_inc(c_in, 16)
            sp.dma_start(sel[0:64, :], sel64).then_inc(c_in, 16)
            sp.dma_start(inv, invcnt).then_inc(c_in, 16)
            sp.dma_start(poolw, pool_w).then_inc(c_in, 16)
            sp.dma_start(ext[:, :, :, 0:15], pool_state).then_inc(c_in, 16)

            sp.wait_ge(c_in, 16 * 8)
            with ExitStack() as es:
                def load_kv(n):
                    src, b, s = (cache_k, n, n % NKV) if n < NDEC else (cache_v, n - NDEC, n % NKV)
                    if n >= NKV:
                        sp.wait_ge(kv_used, n - NKV + 1)
                    for g in range(NPG):
                        i = b * NPG + g
                        page = sp.value_load(pt[0:1, i:i + 1], min_val=0, max_val=cache_k.shape[0] - 1)
                        sp.dma_start(kv[:, s, g, :], src[bass.ds(page, 1)].rearrange("a p n -> (a p) n")
                                     ).then_inc(kv_in[s], 16)

                for n in range(NKV):
                    load_kv(n)
                for u in range(2, 4):
                    weights(w_in0, u, u % 2, u, WORDS[u])
                sp.wait_ge(strip_ready, H0)
                sp.dma_start(scratch.rearrange("h (p m) -> p h m", m=SKEW)[:, :, 0:NB], strips).then_inc(strip_out, 16)
                sp.wait_ge(strip_out, 16)
                sp.dma_start(biasT, scratch[:, 127:127 + 128 * NB].rearrange("h (p c) -> p h c", c=NB)[:, :, 0:512]
                             ).then_inc(bias_in, 16)
                stream(w_in0, "in0", skip=4)
                for u in range(FIRST_UNIT["out0"], FIRST_UNIT["out0"] + 2):
                    weights(w_out0, u, u % 2, u - FIRST_UNIT["out0"], WORDS[u])
                sp.wait_ge(pm_free, FIRST_TILE["out0"])
                sp.dma_start(o_k, qkv[:, 4:8, :]).then_inc(outs, 16)
                sp.dma_start(o_v, qkv[:, 8:12, :]).then_inc(outs, 16)
                sp.dma_start(o_pp, upad[:, :, 16 + SEQ - 15:16 + SEQ]).then_inc(outs, 16)
                sp.wait_ge(dext, 1)
                sp.dma_start(o_ps, ext).then_inc(outs, 16)
                for n in range(NKV, 2 * NDEC):
                    load_kv(n)
            stream(w_out0, "out0", skip=2)
            stream(w_gu[0], "gu0")
            stream(w_dn[0], "dn0")
            for u in range(FIRST_UNIT["in1"], FIRST_UNIT["in1"] + 2):
                weights(w_in1, u, u % 2, u - FIRST_UNIT["in1"], WORDS[u])
            sp.wait_ge(pm_free, FIRST_TILE["in1"])
            sp.dma_start(wabf, wab.rearrange("p k n -> p (k n)")).then_inc(l1_in, 16)
            sp.dma_start(gate[0:8, 0:2], gates).then_inc(l1_in, 16)
            sp.dma_start(cw, convw).then_inc(l1_in, 16)
            sp.dma_start(msk, masks).then_inc(l1_in, 16)
            sp.dma_start(cext[:, :, :, 0:3], conv_state).then_inc(l1_in, 16)
            stream(w_in1, "in1", skip=2)
            for u in range(FIRST_UNIT["out1"], FIRST_UNIT["out1"] + 2):
                weights(w_out1, u, u % 2, u - FIRST_UNIT["out1"], WORDS[u])
            sp.wait_ge(convd_done, 3)
            sp.dma_start(o_ct, tail).then_inc(outs, 16)
            sp.dma_start(o_cs, cext).then_inc(outs, 16)
            sp.wait_ge(*G("o", HG))
            sp.wait_ge(*G("s", 4 * HG))
            sp.dma_start(o_dp, sall).then_inc(outs, 16)
            for b in range(NDEC):
                if b >= 2:
                    sp.wait_ge(st_out[b % 2], 16 * (b // 2))
                sp.dma_start(dS[:, b % 2, :], delta_state[b]).then_inc(st_in[b % 2], 16)
                if b >= 1:
                    sp.wait_ge(snew, b)
                    sp.dma_start(o_ds[b - 1], dS[:, (b - 1) % 2, :]).then_inc(st_out[(b - 1) % 2], 16)
            sp.wait_ge(snew, NDEC)
            sp.dma_start(o_ds[NDEC - 1], dS[:, 1, :]).then_inc(st_out[1], 16)
            stream(w_out1, "out1", skip=2)
            stream(w_gu[1], "gu1")
            stream(w_dn[1], "dn1")
            for k in range(KD):
                sp.wait_ge(y_ready, k + 1)
                sp.dma_start(o_y[:, k, :], yf[:, k % 2, :]).then_inc(y_out[k % 2], 16)
            sp.wait_ge(outs, 16 * 7)
            for j in range(2):
                sp.wait_ge(st_out[j], 16 * NDEC // 2)
            for j in range(2):
                sp.wait_ge(y_out[j], 16 * KD // 2)

        @block.gpsimd
        def _(pool):
            steps = [0]

            def link(ins):
                steps[0] += 1
                ins.then_inc(pool_step, 1)
                pool.wait_ge(pool_step, steps[0])

            link(nc.gpsimd.memset(ident[:, :], 0.0))
            link(nc.gpsimd.affine_select(out=ident[:, :], in_=ident[:, :], compare_op=ALU.not_equal, fill=1.0, base=0,
                                         pattern=[[-1, 128]], channel_multiplier=1))
            nc.gpsimd.memset(ones[:, :], 1.0)
            nc.gpsimd.memset(onesD[:, :], 1.0 / D)
            nc.gpsimd.memset(onesH[:, :], 1.0 / 128)
            nc.gpsimd.memset(epsc[:, 0:1], EPS * WS * WS)
            nc.gpsimd.memset(epsc[:, 1:2], EPS)
            nc.gpsimd.memset(epsc[:, 2:3], EPS * 128)
            nc.gpsimd.memset(upad[:, :, 0:16], 0.0)
            nc.gpsimd.memset(qk2, 0.0)
            link(nc.gpsimd.memset(qpad, 0.0))
            pool.nop().then_inc(consts, 1)
            pool.wait_ge(c_in, 16 * 8)
            for h in range(H0):
                link(nc.gpsimd.tensor_copy(tabB[0:33, h, :], tab[0:33, h:h + 1].to_broadcast([33, 128])))
            for m in range(2):
                link(nc.gpsimd.tensor_copy(tab64[0:33, :].rearrange("p (b h m) -> p b h m", b=NDEC, m=2)[:, :, :, m],
                                           tab[0:33, :].unsqueeze(1).to_broadcast([33, NDEC, H0])))
            pool.nop().then_inc(tabB_ready, 1)

            def sum_squares(b):
                for k in range(KD):
                    pool.wait_ge(sq_ready, KD * b + k + 1)
                    if k == 0:
                        if b > 0:
                            pool.wait_ge(stat_ready, b)
                        ins = nc.gpsimd.tensor_copy(ssq[:, :], sq[:, 0, :])
                    else:
                        ins = nc.gpsimd.tensor_tensor(ssq[:, :], ssq[:, :], sq[:, k % 2, :], ADD)
                    ins.then_inc(ssq_ready, 1)
                    pool.wait_ge(ssq_ready, KD * b + k + 1)

            sum_squares(0)

            pool.wait_ge(pm_free, 4)
            for g, w in enumerate(PW):
                src = upad[:, g, 0:16 + SEQ]
                for l in range(g + 1):
                    s, lo = 1 << l, (2 << l) - 1
                    dst = win[:, l % 2, :]
                    link(nc.gpsimd.tensor_tensor(dst[:, lo:], src[:, lo:], src[:, lo - s:16 + SEQ - s], ADD))
                    src = dst
                if g >= 1:
                    pool.wait_ge(pool_ps, g)
                link(nc.gpsimd.tensor_scalar(dT[:, 0:SEQ], src[:, 16:], 1.0 / w, None, MUL))
                link(nc.gpsimd.tensor_tensor(dT[:, 0:w - 1], src[:, 16:15 + w], inv[:, 0:w - 1], MUL))
                link(nc.gpsimd.tensor_tensor(dT[:, 0:SEQ], dT[:, 0:SEQ], upad[:, g, 16:16 + SEQ], SUB))
                if g == 0:
                    pool.wait_ge(dext, 1)
                link(nc.gpsimd.tensor_scalar(dT[:, SEQ:T], extsum[:, g, :], 1.0 / w, None, MUL))
                nc.gpsimd.tensor_tensor(dT[:, SEQ:T], dT[:, SEQ:T], ext[:, g, :, 15], SUB).then_inc(d_ready, 1)

            for h in range(H0):
                pool.wait_ge(m_hi, 4 + h + 1)
                nc.gpsimd.tensor_tensor(ml[:, 4 + h, :], yn[h % 2], mh[:, 4 + h, :], SUB).then_inc(m_lo, 1)
            sum_squares(1)

            def ffn_up(layer):
                name = f"gu{layer}"

                def body(i):
                    t = FIRST_TILE[name] + 4 * i
                    f = 2 * (11 * layer + i)
                    for j in range(2):
                        pool.wait_ge(silu_done, f + j + 1)
                        pool.wait_ge(pm_free, t + 2 + j + 1)
                        nc.gpsimd.tensor_tensor(gu[:, j, :], gt[:, j, :], ut[:, j, :], MUL).then_inc(prod_done, 1)
                    for j in range(2):
                        pool.wait_ge(f_hi, f + j + 1)
                        nc.gpsimd.tensor_tensor(fl[:, bass.ds(2 * i + j, 1), :], gu[:, j:j + 1, :],
                                                fh[:, bass.ds(2 * i + j, 1), :], SUB).then_inc(f_lo, 1)
                    pool.wait_ge(f_lo, f + 2)
                with pool.Fori(0, 11) as i:
                    body(i)

            ffn_up(0)
            sum_squares(2)

            pool.wait_ge(pm_free, FIRST_TILE["in1"])
            nc.gpsimd.memset(rows[0:40, :], 0.0)
            nc.gpsimd.memset(pre[:, :, 0:3], 0.0).then_inc(l1_free, 1)
            pool.wait_ge(l1_in, 16 * 5)

            def tail_of(t):
                pool.wait_ge(pm_free, FIRST_TILE["in1"] + t + 1)
                nc.gpsimd.tensor_copy(tail[:, t, :], pre[:, t % 2, SEQ:SEQ + 11]).then_inc(tail_done, 1)

            def decode_conv(grp):
                pool.wait_ge(tail_done, 8 * grp + 8)
                g8 = slice(8 * grp, 8 * grp + 8)
                link(nc.gpsimd.tensor_copy(cext[:, g8, :, 3], tail[:, g8, 3:11]))
                dst = qkvc[:, g8, SEQ:]
                for i in range(4):
                    wt = cw[:, i, g8].unsqueeze(2).to_broadcast([128, 8, NDEC])
                    link(nc.gpsimd.tensor_tensor(dst if i == 0 else ctmp, cext[:, g8, :, i], wt, MUL))
                    if i > 0:
                        link(nc.gpsimd.tensor_tensor(dst, dst, ctmp, ADD))
                pool.nop().then_inc(convd_done, 1)

            def square(m):
                pool.wait_ge(csilu, m + 1)
                if m >= 2:
                    pool.wait_ge(nstat, m - 1)
                nc.gpsimd.tensor_tensor(sq[:, m % 2, :], qkvc[:, m, :], qkvc[:, m, :], MUL).then_inc(nsq, 1)

            def normalize(m):
                pool.wait_ge(nrs, m + 1)
                nc.gpsimd.tensor_tensor(qkvc[:, m, :], qkvc[:, m, :], rs2[:, m % 2, :], MUL).then_inc(nq, 1)

            for t in range(8):
                tail_of(t)
            decode_conv(0)
            for grp in range(2):
                square(8 * grp)
                square(8 * grp + 1)
                for m in range(8 * grp, 8 * grp + 8):
                    normalize(m)
                    if m % 8 < 6:
                        square(m + 2)
                    tail_of(m + 8)
                decode_conv(grp + 1)

            def four(ap):
                return ap.rearrange("p (c n) -> p c n", c=4)

            def mask(i):
                return msk[:, i, :].unsqueeze(1).to_broadcast([128, 4, 128])

            for h in range(HG):
                if h >= 2:
                    pool.wait_ge(*G("gb_ps", h - 1))
                nc.gpsimd.tensor_copy(selb[0:40, h % 2, 0, :], ident[0:40, h:h + 1].to_broadcast([40, 128]))
                nc.gpsimd.tensor_copy(selb[0:40, h % 2, 1, :], ident[0:40, 32 + h:33 + h].to_broadcast([40, 128])
                                      ).then_inc(S["selb"], 1)
                pool.wait_ge(*G("et", h + 1))
                nc.gpsimd.tensor_tensor(four(ets_nf_u), four(et), mask(1), MUL).then_inc(S["ets"], 1)
                pool.wait_ge(*G("ets", h + 1))
                nc.gpsimd.tensor_tensor(four(et), four(et), mask(0), MUL).then_inc(S["eti"], 1)
                pool.wait_ge(*G("gam", h + 1))
                pool.wait_ge(*G("kk_ps", h + 1))
                nc.gpsimd.tensor_tensor(kbg_w, kbg_w, gamB, MUL).then_inc(S["kbg"], 1)
                pool.wait_ge(*G("nf", h + 1))
                for l in range(3):
                    nc.gpsimd.tensor_tensor(four(offs[l]), four(ets_nf_u), mask(3 + l), MUL).then_inc(S["om"], 1)
                pool.wait_ge(*G("qk_ps", h + 1))
                nc.gpsimd.tensor_tensor(qkvc[:, h, 0:SEQ], qkvc[:, h, 0:SEQ], gamB, MUL).then_inc(S["qd"], 1)

            for b in range(NDEC):
                pool.wait_ge(kqs_ps, b + 1)
                v = dS[:, b % 2, :].rearrange("p (h n) -> p h n", h=HG)
                nc.gpsimd.tensor_tensor(v, v, gD[:, b, :].unsqueeze(2).to_broadcast([128, HG, 128]), MUL
                                        ).then_inc(sdec, 1)
            for h in range(HG):
                pool.wait_ge(yo, h + 1)
                pool.wait_ge(zsilu, h + 1)
                nc.gpsimd.tensor_tensor(yn1[h % 2], yn1[h % 2], sz[:, h, :], MUL).then_inc(yz, 1)
                pool.wait_ge(m1_hi, h + 1)
                nc.gpsimd.tensor_tensor(ml1[:, h, :], yn1[h % 2], mh1[:, h, :], SUB).then_inc(m1_lo, 1)
            sum_squares(3)
            ffn_up(1)
            sum_squares(4)

        @block.scalar
        def _(act):
            def split_hi(u, j, words, used):
                act.wait_ge(w_in[j], 16 * (u // 2 + 1) if isinstance(u, int) else u)
                if used is not None:
                    act.wait_ge(mm_done, used)
                nc.scalar.activation(wh[:, j, 0:words], stage[:, j, 0:words], ACT.Copy, scale=WS).then_inc(hi_ready, 1)

            def next_split(name, i, j, n):
                base, per = FIRST_UNIT[name], [p for a, _, p, _ in PHASES if a == name][0]
                if isinstance(i, int) and base + 2 * i + j + 2 >= UNITS:
                    return
                words = WORDS[base + 2 * i + j + 2] if isinstance(i, int) else WORDS[base + j + 2]
                act.wait_ge(w_in[j], 16 * (base // 2 + i + 2))
                act.wait_ge(mm_done, FIRST_TILE[name] + per * (2 * i + j + 1))
                nc.scalar.activation(wh[:, j, 0:words], stage[:, j, 0:words], ACT.Copy, scale=WS).then_inc(hi_ready, 1)

            def norm_tile(b, k, name=None):
                if name is None:
                    act.wait_ge(x_in, 32)
                else:
                    act.wait_ge(pm_free, FIRST_TILE[name] + k + 1)
                if b < 4:
                    nc.scalar.activation(zh[:, k, :], hT[:, k, :], ACT.Copy,
                                         scale=par[:, NORM[b] + k:NORM[b] + k + 1]).then_inc(z_hi, 1)
                if KD * b + k >= 2:
                    act.wait_ge(ssq_ready, KD * b + k - 1)
                nc.scalar.activation(sq[:, k % 2, :], hT[:, k, :], ACT.Square).then_inc(sq_ready, 1)

            def norm_factor(b):
                act.wait_ge(stat_ready, b + 1)
                c = epsc[:, 0:1] if b < 4 else epsc[:, 1:2]
                nc.scalar.activation(paired(rstd[:, :]), stat, ACT.Ln, scale=WS * WS if b < 4 else 1.0, bias=c
                                     ).then_inc(ln_done, 1)
                act.wait_ge(ln_done, b + 1)
                nc.scalar.activation(rstd[:, :], rstd[:, :], ACT.Exp, scale=-0.5).then_inc(rstd_ready, 1)

            act.preload_act_table_set("natural_log_exp_and_others")
            for u in range(2):
                split_hi(u, u, WORDS[u], None)
            act.wait_ge(consts, 1)
            for k in range(KD):
                norm_tile(0, k)
            norm_factor(0)
            for h in range(H0):
                act.wait_ge(strip_ps, h + 1)
                nc.scalar.activation(strips[:, h, :].rearrange("p (c n) -> p c n", c=2),
                                     P[:, 6:8, 0:NB // 2] if h % 2 == 0 else P[:, 2:4, 0:NB // 2], ACT.Copy
                                     ).then_inc(strip_ready, 1)
            act.wait_ge(lam_ps, 1)
            nc.scalar.activation(lame, P[:, 6, 0:2], ACT.Exp).then_inc(act_step, 1)

            for i in range(4):
                for j in range(2):
                    next_split("in0", i, j, 2)

            for c in range(4):
                act.wait_ge(vt_ps, c + 1)
                nc.scalar.activation(vtok[:, c, :], P[:, 4 + c, :], ACT.Copy).then_inc(vt_done, 1)

            for s in range(16):
                h, qt = divmod(s, 4)
                w = 128 * (qt + 1)
                act.wait_ge(nm_ready, s + 1)
                for m in range(2):
                    nc.scalar.activation(pr[:, m, 0:w], pr[:, m, 0:w], ACT.Exp, bias=nm[:, m:m + 1],
                                         accum_out=ls[:, m:m + 1]).then_inc(exp_done, 1)
                act.wait_ge(at_ps, s + 1)
                if s >= 1:
                    act.wait_ge(pv_done, s)
                nc.scalar.activation(aT[:, 0:w], P[:, 6, 0:w], ACT.Copy).then_inc(at_done, 1)
                if qt == 3:
                    act.wait_ge(pv_done, s + 1)
                    nc.scalar.activation(oT[:, h, 0:SEQ], P[:, 7, :], ACT.Copy).then_inc(o_evac, 1)
                if qt == 2:
                    g = h
                    act.wait_ge(pool_ps, g + 1)
                    nc.scalar.activation(paired(mh[:, g, :]), P[:, 2:4, 0:CH], ACT.Copy,
                                         scale=par[:, P_POOL + g:P_POOL + g + 1]).then_inc(m_hi, 1)
            act.wait_ge(dp_ready, 1)
            nc.scalar.activation(td[0:64, :], td[0:64, :], ACT.Exp, bias=tsm[0:64, 1:2],
                                 accum_out=tsm[0:64, 2:3]).then_inc(exp_done, 1)
            act.wait_ge(ad_ps, 1)
            nc.scalar.activation(aD, P[:, 1, 0:160], ACT.Copy).then_inc(ad_done, 1)
            act.wait_ge(dec_o, 1)
            for h in range(H0):
                if h >= 2:
                    act.wait_ge(ostat, h - 1)
                nc.scalar.activation(sq[:, h % 2, :], oT[:, h, :], ACT.Square).then_inc(osq, 1)
            for h in range(H0):
                act.wait_ge(ostat, h + 1)
                if h >= 2:
                    act.wait_ge(yn_ready, h - 1)
                nc.scalar.activation(paired(ors[h % 2]), P[:, 4 + 2 * (h % 2):6 + 2 * (h % 2), 0:CH], ACT.Ln,
                                     bias=epsc[:, 1:2]).then_inc(oln, 1)
                act.wait_ge(oln, h + 1)
                nc.scalar.activation(ors[h % 2], ors[h % 2], ACT.Exp, scale=-0.5).then_inc(ors_ready, 1)
            for h in range(H0):
                act.wait_ge(yn_ready, h + 1)
                nc.scalar.activation(mh[:, 4 + h, :], yn[h % 2], ACT.Copy).then_inc(m_hi, 1)

            def project_out(name, b):
                for i in range(2 if name[:3] == "out" else 4):
                    for j in range(2):
                        for k in ((4 * i + 2 * j, 4 * i + 2 * j + 1) if name[:3] == "out" else (2 * i + j,)):
                            norm_tile(b, k, name)
                        next_split(name, i, j, 2)
                norm_factor(b)

            def ffn_up(layer):
                name = f"gu{layer}"
                act.preload_act_table(ACT.Silu)

                def body(i):
                    t = FIRST_TILE[name] + 4 * i
                    f = 2 * (11 * layer + i)
                    for j in range(2):
                        act.wait_ge(pm_free, t + j + 1)
                        nc.scalar.activation(gt[:, j, :], gt[:, j, :], ACT.Silu).then_inc(silu_done, 1)
                    next_split(name, i, 0, 2)
                    for j in range(2):
                        act.wait_ge(prod_done, f + j + 1)
                        nc.scalar.activation(fh[:, bass.ds(2 * i + j, 1), :], gu[:, j:j + 1, :], ACT.Copy
                                             ).then_inc(f_hi, 1)
                    next_split(name, i, 1, 2)
                with act.Fori(0, 10) as i:
                    body(i)
                body(10)
                act.preload_act_table_set("natural_log_exp_and_others")

            project_out("out0", 1)
            ffn_up(0)
            project_out("dn0", 2)

            act.wait_ge(l1_in, 16 * 5)
            nc.scalar.activation(wabh.rearrange("p k n -> p (k n)"), wabf, ACT.Copy, scale=WS).then_inc(ab_split, 1)
            nc.scalar.activation(gate[0:8, 2:3], gate[0:8, 0:1], ACT.Exp).then_inc(ab_step, 1)
            act.wait_ge(ab_step, 2)
            nc.scalar.activation(rowt[32:40, 1, :], rowt[32:40, 0, :], ACT.Exp, scale=-1.0)
            nc.scalar.activation(rowt[0:8, 1, :], rowt[0:8, 1, :], ACT.Exp).then_inc(ab_step, 1)
            act.wait_ge(ab_step, 3)
            nc.scalar.activation(rowt[0:8, 1, :], rowt[0:8, 1, :], ACT.Ln, bias=ones[0:8, 0:1]).then_inc(ab_step, 1)

            def norm_l2(m):
                act.wait_ge(nstat, m + 1)
                if m >= 2:
                    act.wait_ge(nq, m - 1)
                nc.scalar.activation(paired(rs2[:, m % 2, :]), P[:, 4 + 2 * (m % 2):6 + 2 * (m % 2), 0:CH], ACT.Ln,
                                     scale=128.0 if m < 8 else 1.0,
                                     bias=epsc[:, 2:3] if m < 8 else epsc[:, 1:2]).then_inc(nln, 1)
                act.wait_ge(nln, m + 1)
                nc.scalar.activation(rs2[:, m % 2, :], rs2[:, m % 2, :], ACT.Exp, scale=-0.5).then_inc(nrs, 1)

            for grp in range(3):
                for u in range(4 * grp, 4 * grp + 4):
                    next_split("in1", u // 2, u % 2, 2)
                    if grp > 0:
                        norm_l2(2 * u - 8)
                        norm_l2(2 * u - 7)
                if grp == 1:
                    act.wait_ge(tok_ps, 1)
                    nc.scalar.activation(tokm, P[:, 6, 0:160].rearrange("p (c n) -> p c n", c=4), ACT.Copy
                                         ).then_inc(tok_done, 1)
                act.preload_act_table(ACT.Silu)
                act.wait_ge(convd_done, grp + 1)
                for t in range(8 * grp, 8 * grp + 8):
                    act.wait_ge(conv_done, t + 1)
                    nc.scalar.activation(qkvc[:, t, :], qkvc[:, t, :], ACT.Silu).then_inc(csilu, 1)
                act.preload_act_table_set("natural_log_exp_and_others")

            def evac(dst, bank, ready, name, h):
                act.wait_ge(*G(ready, h + 1))
                nc.scalar.activation(dst, P[:, bank, :], ACT.Copy).then_inc(S[name], 1)

            for h in range(HG):
                act.wait_ge(*G("gb_ps", h + 1))
                nc.scalar.activation(gamB, P[:, 2, :], ACT.Exp).then_inc(S["gam"], 1)
                nc.scalar.activation(gD[:, :, h], P[:, 7, 0:8], ACT.Exp).then_inc(S["gd"], 1)
                act.wait_ge(*G("ex", h + 1))
                nc.scalar.activation(et, et, ACT.Exp).then_inc(S["et"], 1)
                nc.scalar.activation(kd4, d4, ACT.Exp).then_inc(S["kd4"], 1)
                act.wait_ge(*G("d", h + 1))
                evac(ets_nf_u, 6, "n_ps", "nf", h)
                act.wait_ge(*G("tk_ps", h + 1))
                act.wait_ge(*G("kd4", h + 1))
                for c in range(4):
                    ins = nc.scalar.activation(Kd[:, c * 128:(c + 1) * 128], P[:, 7, c * 128:(c + 1) * 128], ACT.Copy,
                                               scale=kd4[:, c:c + 1])
                ins.then_inc(S["kd"], 1)
                evac(d2_8, 2, "d2_ps", "d2", h)
                evac(bV, 5, "tv_ps", "bv", h)
                evac(dd, 6, "d4_ps", "d4", h)
                act.wait_ge(*G("y1", h + 1))
                evac(ddt, 7, "dt4_ps", "dt4", h)
                evac(d2_8, 3, "d8_ps", "d8", h)
                for l in range(3):
                    act.wait_ge(*G("x_ps", 3 * h + l + 1))
                    nc.scalar.activation(dt2_x, P[:, 5, :], ACT.Copy).then_inc(S["x"], 1)
                evac(kbg_w, 4, "w_ps", "w", h)
                if h % 2:
                    next_split("in1", 6 + h // 4, h // 2 % 2, 2)
                act.wait_ge(*G("o_ps", h + 1))
                nc.scalar.activation(qkvc[:, h, 0:SEQ], P[:, 7, :], ACT.Copy).then_inc(S["o"], 1)

            act.wait_ge(krow_ps, 1)
            act.wait_ge(qk_dps, 1)
            nc.scalar.activation(qkD, P[:, 5, 0:64].rearrange("p (b h) -> p b h", b=NDEC), ACT.Copy)
            for b in range(NDEC):
                act.wait_ge(krow_ps, b + 1)
                nc.scalar.activation(krow[0:8, :], P[0:8, 3, 0:128], ACT.Copy).then_inc(krow_s, 1)
                act.wait_ge(du_ps, b + 1)
                nc.scalar.activation(urow[0:8, :], P[0:8, 4, 0:128], ACT.Copy).then_inc(urow_s, 1)
            act.preload_act_table(ACT.Silu)
            for h in range(HG):
                act.wait_ge(pm_free, FIRST_TILE["in1"] + 24 + h + 1)
                nc.scalar.activation(sz[:, h, :], sz[:, h, :], ACT.Silu).then_inc(zsilu, 1)
            act.preload_act_table_set("natural_log_exp_and_others")
            act.wait_ge(du, NDEC)
            for j in range(2):
                act.wait_ge(st_out[j], 16 * NDEC // 2)
            for h in range(2):
                nc.scalar.activation(sq[:, h % 2, :], qkvc[:, h, :], ACT.Square).then_inc(o1sq, 1)
            for h in range(HG):
                act.wait_ge(o1stat, h + 1)
                if h >= 2:
                    act.wait_ge(yo, h - 1)
                nc.scalar.activation(paired(ors1[h % 2]), P[:, 4 + 2 * (h % 2):6 + 2 * (h % 2), 0:CH], ACT.Ln,
                                     bias=epsc[:, 1:2]).then_inc(o1ln, 1)
                act.wait_ge(o1ln, h + 1)
                nc.scalar.activation(ors1[h % 2], ors1[h % 2], ACT.Exp, scale=-0.5).then_inc(o1rs, 1)
                if h + 2 < HG:
                    nc.scalar.activation(sq[:, h % 2, :], qkvc[:, h + 2, :], ACT.Square).then_inc(o1sq, 1)
                if h >= 1:
                    act.wait_ge(yz, h)
                    nc.scalar.activation(mh1[:, h - 1, :], yn1[(h - 1) % 2], ACT.Copy).then_inc(m1_hi, 1)
            act.wait_ge(yz, HG)
            nc.scalar.activation(mh1[:, HG - 1, :], yn1[(HG - 1) % 2], ACT.Copy).then_inc(m1_hi, 1)
            project_out("out1", 3)
            ffn_up(1)
            project_out("dn1", 4)

        @block.vector
        def _(dve):
            steps = [0]

            def link(ins):
                steps[0] += 1
                ins.then_inc(dve_step, 1)
                dve.wait_ge(dve_step, steps[0])

            def split_lo(u, j, words):
                dve.wait_ge(hi_ready, u + 1)
                nc.vector.scalar_tensor_tensor(out=wl[:, j, 0:words], in0=stage[:, j, 0:words], scalar=WS,
                                               in1=wh[:, j, 0:words], op0=MUL, op1=SUB).then_inc(lo_ready, 1)

            def next_split(name, i, j):
                base = FIRST_UNIT[name]
                if isinstance(i, int) and base + 2 * i + j + 2 >= UNITS:
                    return
                words = WORDS[base + 2 * i + j + 2] if isinstance(i, int) else WORDS[base + j + 2]
                split_lo(base + 2 * i + j + 2, j, words)

            def norm_lo(b, k):
                dve.wait_ge(z_hi, KD * b + k + 1)
                nc.vector.scalar_tensor_tensor(out=zl[:, k, :], in0=hT[:, k, :],
                                               scalar=par[:, NORM[b] + k:NORM[b] + k + 1], in1=zh[:, k, :],
                                               op0=MUL, op1=SUB).then_inc(z_lo, 1)

            for u in range(2):
                split_lo(u, u, WORDS[u])
            for k in range(KD):
                norm_lo(0, k)
            dve.wait_ge(c_in, 16 * 8)
            nc.vector.tensor_tensor(lpr[0:64, :], lamt[0:64, 0:2], lamt[0:64, 2:4], MUL).then_inc(lam_pr, 1)
            dve.wait_ge(act_step, 1)
            nc.vector.scalar_tensor_tensor(out=nlam, in0=lame[:, 1:2], scalar=-LAM0, in1=lame[:, 0:1],
                                           op0=ADD, op1=SUB).then_inc(lam_ready, 1)

            dve.wait_ge(rstd_ready, 1)
            for u in range(8):
                for j in range(2):
                    t = 2 * u + j
                    dve.wait_ge(mm_done, t + 1)
                    if t < 4:
                        nc.vector.tensor_tensor(paired(upad[:, t, 16:]), pm[j], paired(rstd[:, :]), MUL
                                                ).then_inc(pm_free, 1)
                    else:
                        nc.vector.scalar_tensor_tensor(out=paired(qkv[:, t - 4, :]), in0=pm[j],
                                                       scalar=HALF ** -0.5 if t < 8 else 1.0,
                                                       in1=paired(rstd[:, :]), op0=MUL, op1=MUL).then_inc(pm_free, 1)
                next_split("in0", u // 2, u % 2)
                if u == 1:
                    dve.wait_ge(pm_free, 4)
                    link(nc.vector.tensor_copy(ext[:, :, :, 15], upad[:, :, 16 + SEQ:]))
                    for g, w in enumerate(PW):
                        ins = nc.vector.tensor_reduce(out=extsum[:, g, :], in_=ext[:, g, :, 16 - w:], axis=AX.X, op=ADD)
                    link(ins)
                    dve.nop().then_inc(dext, 1)
            dve.wait_ge(x_in, 32)
            link(nc.vector.tensor_scalar(subw, par[:, P_SUB:P_SUB + 1], 1 - LAM0, None, MUL))
            dve.wait_ge(pm_free, 16)
            dve.wait_ge(consts, 1)
            for m in range(2):
                part = slice(64 * m, 64 * m + 64)
                dst = qpad[part, :].rearrange("p (b x) -> p b x", b=NDEC)[:, :, 0:264].rearrange(
                    "p b (h y) -> p b h y", y=66)[:, :, :, m]
                nc.vector.tensor_copy(dst, qkv[part, 0:4, SEQ:].rearrange("p h b -> p b h"))
                ins = nc.vector.tensor_tensor(qk2[part, :].rearrange("p (b h m) -> p b h m", b=NDEC, m=2)[:, :, :, m],
                                              qkv[part, 0:4, SEQ:].rearrange("p h b -> p b h"),
                                              qkv[part, 4:8, SEQ:].rearrange("p h b -> p b h"), MUL)
            link(ins)
            dve.nop().then_inc(qpad_ready, 1)

            dve.wait_ge(bias_in, 16)
            for s in range(16):
                h, qt = divmod(s, 4)
                w = 128 * (qt + 1)
                for m in range(2):
                    dve.wait_ge(s_ready, 2 * s + m + 1)
                    nc.vector.tensor_tensor_reduce(out=pr[:, m, 0:w], in0=P[:, 4 + m, 0:w], in1=biasT[:, h, 512 - w:],
                                                   scale=1.0, scalar=NEG, op0=ADD, op1=MAX,
                                                   accum_out=mx[:, m:m + 1]).then_inc(s_read, 1)
                dve.wait_ge(s_read, 2 * s + 2)
                nc.vector.tensor_scalar(nm, mx, -1.0, None, MUL).then_inc(nm_ready, 1)
                dve.wait_ge(exp_done, 2 * s + 2)
                link(nc.vector.reciprocal(rl, ls))
                link(nc.vector.tensor_scalar(pr[:, 1, 0:w], pr[:, 1, 0:w], rl[:, 1:2], nlam, MUL, MUL))
                if s >= 1:
                    dve.wait_ge(at_ps, s)
                nc.vector.scalar_tensor_tensor(out=am[:, 0:w], in0=pr[:, 0, 0:w], scalar=rl[:, 0:1],
                                               in1=pr[:, 1, 0:w], op0=MUL, op1=ADD).then_inc(a_ready, 1)
                if qt == 3:
                    g = h
                    dve.wait_ge(m_hi, g + 1)
                    nc.vector.scalar_tensor_tensor(out=paired(ml[:, g, :]), in0=P[:, 2:4, 0:CH],
                                                   scalar=par[:, P_POOL + g:P_POOL + g + 1], in1=paired(mh[:, g, :]),
                                                   op0=MUL, op1=SUB).then_inc(m_lo, 1)
            dve.wait_ge(kv_used, NDEC)
            nc.vector.tensor_copy(td[0:64, 0:PAST], P[0:64, 0, :])
            link(nc.vector.tensor_copy(td[0:64, PAST:PAST + 1], P[0:64, 1, 0:1]))
            link(nc.vector.tensor_reduce(out=tsm[0:64, 0:1], in_=td[0:64, :], axis=AX.X, op=MAX))
            nc.vector.tensor_scalar(tsm[0:64, 1:2], tsm[0:64, 0:1], -1.0, None, MUL).then_inc(dp_ready, 1)
            link(nc.vector.scalar_tensor_tensor(out=tsm[0:64, 3:4], in0=sel[0:64, 1:2], scalar=nlam[0:64, :],
                                                in1=sel[0:64, 0:1], op0=MUL, op1=ADD))
            dve.wait_ge(exp_done, 33)
            link(nc.vector.reciprocal(tsm[0:64, 4:5], tsm[0:64, 2:3]))
            link(nc.vector.tensor_tensor(tsm[0:64, 5:6], tsm[0:64, 4:5], tsm[0:64, 3:4], MUL))
            nc.vector.tensor_scalar(pnew[0:64, :], ones[0:64, :], td[0:64, PAST:PAST + 1], None, MUL)
            nc.vector.tensor_scalar(comb[0:64, :], sel[0:64, 2:34], tsm[0:64, 5:6], None, MUL).then_inc(comb_ready, 1)
            dve.wait_ge(ad_done, 1)
            link(nc.vector.tensor_tensor(vn.rearrange("p (b h) -> p b h", b=NDEC),
                                         aD[:, 128:160].rearrange("p (b h) -> p b h", b=NDEC),
                                         qkv[:, 8:12, SEQ:].rearrange("p h b -> p b h"), MUL))
            dve.wait_ge(kv_used, 2 * NDEC)
            dve.wait_ge(o_evac, 4)
            nc.vector.tensor_tensor(oT[:, :, SEQ:].rearrange("p h b -> p b h"),
                                    P[:, 2, 0:32].rearrange("p (b h) -> p b h", b=NDEC),
                                    vn.rearrange("p (b h) -> p b h", b=NDEC), ADD).then_inc(dec_o, 1)
            for h in range(H0):
                dve.wait_ge(ors_ready, h + 1)
                if h >= 2:
                    dve.wait_ge(m_lo, 4 + h - 1)
                nc.vector.scalar_tensor_tensor(out=yn[h % 2], in0=oT[:, h, :], scalar=subw,
                                               in1=ors[h % 2], op0=MUL, op1=MUL).then_inc(yn_ready, 1)

            def project_out(name, b):
                pairs = name[:3] == "out"
                for i in range(2 if pairs else 4):
                    for j in range(2):
                        ks = (4 * i + 2 * j, 4 * i + 2 * j + 1) if pairs else (2 * i + j,)
                        for n, k in enumerate(ks):
                            slot = n if pairs else j
                            dve.wait_ge(mm_done, FIRST_TILE[name] + k + 1)
                            nc.vector.scalar_tensor_tensor(out=paired(hT[:, k, :]), in0=pm[slot], scalar=1 / WS,
                                                           in1=paired(hT[:, k, :]), op0=MUL, op1=ADD
                                                           ).then_inc(pm_free, 1)
                        if b < 4:
                            for k in ks:
                                norm_lo(b, k)
                        next_split(name, i, j)

            def ffn_up(layer, b):
                name = f"gu{layer}"
                dve.wait_ge(rstd_ready, b + 1)

                def body(i):
                    t = FIRST_TILE[name] + 4 * i
                    f = 2 * (11 * layer + i)
                    for part, dst in enumerate((gt, ut)):
                        for j in range(2):
                            dve.wait_ge(mm_done, t + 2 * part + j + 1)
                            if not isinstance(i, int) or i > 0:
                                dve.wait_ge(prod_done, f + j - 1)
                            nc.vector.tensor_tensor(paired(dst[:, j, :]), pm[j], paired(rstd[:, :]), MUL
                                                    ).then_inc(pm_free, 1)
                        next_split(name, i, part)
                body(0)
                with dve.Fori(1, 10) as i:
                    body(i)
                body(10)

            project_out("out0", 1)
            ffn_up(0, 1)
            project_out("dn0", 2)

            dve.wait_ge(l1_free, 1)
            dve.wait_ge(ab_split, 1)
            nc.vector.scalar_tensor_tensor(out=wabl.rearrange("p k n -> p (k n)"), in0=wabf, scalar=WS,
                                           in1=wabh.rearrange("p k n -> p (k n)"), op0=MUL, op1=SUB
                                           ).then_inc(ab_split, 1)
            dve.wait_ge(ab_ps, 1)
            dve.wait_ge(rstd_ready, 3)
            link(nc.vector.tensor_tensor(paired(rowt[0:40, 0, :]), P[0:40, 4:6, 0:CH], paired(rstd[0:40, :]), MUL))
            link(nc.vector.tensor_scalar(rowt[0:8, 2, :], rowt[0:8, 0, :], gate[0:8, 1:2], 0.0, ADD, MAX))
            link(nc.vector.tensor_scalar(rowt[0:8, 3, :], rowt[0:8, 0, :], gate[0:8, 1:2], 0.0, ADD, MIN))
            nc.vector.tensor_tensor(rowt[0:8, 1, :], rowt[0:8, 3, :], rowt[0:8, 2, :], SUB).then_inc(ab_step, 1)
            dve.wait_ge(ab_step, 4)
            link(nc.vector.tensor_tensor(rowt[0:8, 2, :], rowt[0:8, 2, :], rowt[0:8, 1, :], ADD))
            link(nc.vector.tensor_scalar(rowt[0:8, 2, :], rowt[0:8, 2, :], gate[0:8, 2:3], -1.0, MUL, MUL))
            for c in range(4):
                nc.vector.tensor_tensor_scan(rows[0:8, c * 128:(c + 1) * 128], ones[0:8, :],
                                             rowt[0:8, 2, c * 128:(c + 1) * 128], 0.0, MUL, ADD)
            nc.vector.tensor_copy(rows[0:8, SEQ:], rowt[0:8, 2, SEQ:])
            link(nc.vector.tensor_scalar(rowt[32:40, 1, :], rowt[32:40, 1, :], 1.0, None, ADD))
            nc.vector.reciprocal(rows[32:40, :], rowt[32:40, 1, :]).then_inc(rows_ready, 1)

            for t in range(24):
                dve.wait_ge(mm_done, FIRST_TILE["in1"] + t + 1)
                if t >= 2:
                    dve.wait_ge(tail_done, t - 1)
                x, c = pre[:, t % 2, :], qkvc[:, t, 0:SEQ]
                nc.vector.tensor_tensor(paired(x[:, 3:3 + T]), pm[t % 2], paired(rstd[:, :]), MUL).then_inc(pm_free, 1)
                dve.wait_ge(pm_free, FIRST_TILE["in1"] + t + 1)
                link(nc.vector.tensor_scalar(c, x[:, 0:SEQ], cw[:, 0, t:t + 1], None, MUL))
                for i in range(1, 3):
                    link(nc.vector.scalar_tensor_tensor(out=c, in0=x[:, i:i + SEQ], scalar=cw[:, i, t:t + 1], in1=c,
                                                        op0=MUL, op1=ADD))
                nc.vector.scalar_tensor_tensor(out=c, in0=x[:, 3:3 + SEQ], scalar=cw[:, 3, t:t + 1], in1=c,
                                               op0=MUL, op1=ADD).then_inc(conv_done, 1)
                if t % 2:
                    next_split("in1", t // 4, t // 2 % 2)

            def four(ap):
                return ap.rearrange("p (c n) -> p c n", c=4)

            def mask(i):
                return msk[:, i, :].unsqueeze(1).to_broadcast([128, 4, 128])

            def add(dst, bank, src, ready, name, count, op=ADD):
                dve.wait_ge(*G(ready, count))
                if op == ADD:
                    nc.vector.tensor_tensor(dst, P[:, bank, :], src, ADD).then_inc(S[name], 1)
                else:
                    nc.vector.tensor_tensor(dst, src, P[:, bank, :], SUB).then_inc(S[name], 1)

            dve.wait_ge(nq, 16)
            dve.wait_ge(csilu, 24)
            dve.wait_ge(tok_done, 1)
            for h in range(HG):
                k, v = qkvc[:, 8 + h, 0:SEQ], qkvc[:, 16 + h, 0:SEQ]
                dve.wait_ge(*G("gb_ps", h + 1))
                nc.vector.tensor_tensor(kbg_w, P[:, 3, :], k, MUL).then_inc(S["kb"], 1)
                dve.wait_ge(*G("gd", h + 1))
                for c in range(4):
                    nc.vector.tensor_scalar(et[:, c * 128:(c + 1) * 128], P[:, 2, c * 128:(c + 1) * 128],
                                            tokm[:, c, h:h + 1], 0.0, SUB, MIN)
                nc.vector.tensor_tensor(d4, P[:, 2, :].rearrange("p (c n) -> p c n", c=4)[:, :, 127],
                                        tokm[:, :, h], SUB).then_inc(S["ex"], 1)
                nc.vector.tensor_copy(bD[:, :, h], P[:, 7, 8:16]).then_inc(S["bd"], 1)
                nc.vector.tensor_tensor(v, P[:, 3, :], v, MUL).then_inc(S["vb"], 1)
                dve.wait_ge(*G("ets", h + 1))
                dve.wait_ge(*G("kk_ps", h + 1))
                nc.vector.tensor_tensor(nt_z, P[:, 4, :], ets_nf_u, MUL).then_inc(S["nt"], 1)
                dve.wait_ge(*G("nt", h + 1))
                nc.vector.tensor_tensor(four(ddt), four(nt_z), mask(2), MUL).then_inc(S["dt"], 1)
                dve.wait_ge(*G("eti", h + 1))
                dve.wait_ge(*G("qk_ps", h + 1))
                nc.vector.tensor_tensor(At, P[:, 5, :], et, MUL).then_inc(S["at"], 1)
                dve.wait_ge(*G("n_ps", h + 1))
                nc.vector.tensor_tensor(four(dd), four(P[:, 6, :]), mask(2), MUL).then_inc(S["d"], 1)
                dve.wait_ge(*G("dt", h + 1))
                nc.vector.scalar_tensor_tensor(out=four(ya), in0=four(ddt), scalar=-1.0,
                                               in1=ident[:, :].unsqueeze(1).to_broadcast([128, 4, 128]),
                                               op0=MUL, op1=ADD).then_inc(S["y1"], 1)
                dve.wait_ge(*G("dt2_ps", h + 1))
                nc.vector.tensor_copy(dt2_x, P[:, 3, :]).then_inc(S["dt2"], 1)
                dve.wait_ge(*G("tkb_ps", h + 1))
                nc.vector.tensor_copy(Kp, P[:, 4, :]).then_inc(S["kp"], 1)
                dve.wait_ge(*G("y1", h + 1))
                add(yb, 2, ya, "y2_ps", "y2", h + 1)
                dve.wait_ge(*G("y2", h + 1))
                add(ya, 4, yb, "y3_ps", "y3", h + 1)
                dve.wait_ge(*G("y3", h + 1))
                add(yb, 6, ya, "y4_ps", "xt", h + 1)
                for l in range(3):
                    src, dst = (yb, ya) if l % 2 == 0 else (ya, yb)
                    dve.wait_ge(*G("z_ps", 3 * h + l + 1))
                    nc.vector.tensor_copy(nt_z, P[:, 7, :]).then_inc(S["z"], 1)
                    dve.wait_ge(*G("xt", 4 * h + l + 1))
                    add(dst, 6, src, "v_ps", "xt", 3 * h + l + 1, SUB)
                dve.wait_ge(*G("u_ps", h + 1))
                nc.vector.tensor_copy(ets_nf_u, P[:, 5, :]).then_inc(S["u"], 1)
                for c in range(4):
                    cc = slice(c * 128, (c + 1) * 128)
                    if c > 0:
                        dve.wait_ge(*G("ws_ps", 3 * h + c))
                        dve.wait_ge(*G("u", 4 * h + c))
                        nc.vector.tensor_tensor(ets_nf_u[:, cc], ets_nf_u[:, cc], P[:, 2, cc], SUB).then_inc(S["u"], 1)
                    dve.wait_ge(*G("ds_ps", 4 * h + c + 1))
                    dst = sall[:, h, :] if c == 3 else sping[:, c % 2, :]
                    if c == 0:
                        nc.vector.tensor_copy(dst, P[:, 3, cc]).then_inc(S["s"], 1)
                    else:
                        dve.wait_ge(*G("s", 4 * h + c))
                        nc.vector.scalar_tensor_tensor(out=dst, in0=sping[:, (c - 1) % 2, :],
                                                       scalar=gamB[:, c * 128 + 127:c * 128 + 128], in1=P[:, 3, cc],
                                                       op0=MUL, op1=ADD).then_inc(S["s"], 1)
                dve.wait_ge(mm_done, FIRST_TILE["in1"] + 24 + h + 1)
                nc.vector.tensor_tensor(paired(sz[:, h, :]), pm[0], paired(rstd[:, :]), MUL).then_inc(pm_free, 1)
                if h % 2:
                    next_split("in1", 6 + h // 4, h // 2 % 2)

            def dec(i):
                return qkvc[:, 8 * i:8 * i + 8, SEQ:].rearrange("p h b -> p b h")
            dve.wait_ge(*G("gd", HG))
            dve.wait_ge(*G("bd", HG))
            nc.vector.tensor_copy(kq[:, :, :, 0], dec(1))
            nc.vector.tensor_copy(kq[:, :, :, 1], dec(0))
            nc.vector.tensor_tensor(qkp.rearrange("p (b h) -> p b h", b=NDEC), dec(0), dec(1), MUL).then_inc(dprep, 1)
            dve.wait_ge(krow_s, 1)
            for b in range(NDEC):
                kqS = P[:, 2, 16 * b:16 * b + 16].rearrange("p (h m) -> p h m", m=2)
                dve.wait_ge(kqs_ps, b + 1)
                nc.vector.tensor_tensor(od[:, b, :], kqS[:, :, 1], gD[:, b, :], MUL)
                link(nc.vector.tensor_tensor(t8[:, b, :], kqS[:, :, 0], gD[:, b, :], MUL))
                link(nc.vector.tensor_tensor(t8[:, b, :], qkvc[:, 16:24, SEQ + b], t8[:, b, :], SUB))
                link(nc.vector.tensor_tensor(ud[:, b, :], t8[:, b, :], bD[:, b, :], MUL))
                link(nc.vector.tensor_tensor(t8[:, b, :], ud[:, b, :], qkD[:, b, :], MUL))
                nc.vector.tensor_tensor(qkvc[:, 0:8, SEQ + b], od[:, b, :], t8[:, b, :], ADD).then_inc(du, 1)
                dve.wait_ge(urow_s, b + 1)
                if b >= 1:
                    dve.wait_ge(outer_ps, b)
                nc.vector.tensor_tensor(um[0:8, :].rearrange("p (h n) -> p h n", h=HG),
                                        urow[0:8, :].unsqueeze(1).to_broadcast([8, HG, 128]),
                                        ident[0:8, 0:8].unsqueeze(2).to_broadcast([8, HG, 128]), MUL
                                        ).then_inc(um_s, 1)
                dve.wait_ge(outer_ps, b + 1)
                dve.wait_ge(sdec, b + 1)
                nc.vector.tensor_tensor(dS[:, b % 2, :].rearrange("p (c n) -> p c n", c=2), P[:, 6:8, :],
                                        dS[:, b % 2, :].rearrange("p (c n) -> p c n", c=2), ADD).then_inc(snew, 1)
            for h in range(HG):
                dve.wait_ge(o1rs, h + 1)
                if h >= 2:
                    dve.wait_ge(m1_lo, h - 1)
                nc.vector.scalar_tensor_tensor(out=yn1[h % 2], in0=qkvc[:, h, :], scalar=par[:, P_ONORM:P_ONORM + 1],
                                               in1=ors1[h % 2], op0=MUL, op1=MUL).then_inc(yo, 1)
            project_out("out1", 3)
            ffn_up(1, 3)
            project_out("dn1", 4)

            dve.wait_ge(rstd_ready, 5)
            for k in range(KD):
                if k >= 2:
                    dve.wait_ge(y_out[k % 2], 16 * (k // 2))
                nc.vector.scalar_tensor_tensor(out=yf[:, k % 2, :], in0=hT[:, k, :],
                                               scalar=par[:, P_FIN + k:P_FIN + k + 1], in1=rstd[:, :],
                                               op0=MUL, op1=MUL).then_inc(y_ready, 1)

        @block.tensor
        def _(pe):
            def product(j, wslot, woff, xh, xl, nk, stride, k0=0):
                for k in range(nk):
                    o = woff + k * stride
                    for w, x in ((wh, xh), (wh, xl), (wl, xh)):
                        for c in range(2):
                            mm = nc.tensor.matmul(pm[j][:, c, :], w[:, wslot, o:o + 128],
                                                  x[:, k, c * CH:(c + 1) * CH],
                                                  start=(k == 0 and w is wh and x is xh),
                                                  stop=(k == nk - 1 and w is wl))
                return mm

            def unit(name, u, i, j, xh, xl, ready=None):
                base, per, words = FIRST_UNIT[name], *[(p, w) for a, _, p, w in PHASES if a == name][0]
                pe.wait_ge(hi_ready, base + 2 * i + j + 1)
                pe.wait_ge(lo_ready, base + 2 * i + j + 1)
                nk = KF if per == 1 else KD
                for n in range(per):
                    slot = n if per == 2 else j
                    t = FIRST_TILE[name] + per * (2 * i + j) + n
                    if not isinstance(t, int) or t >= 2:
                        pe.wait_ge(pm_free, t - 1)
                    product(slot, j, 128 * n, xh, xl, nk, words // nk).then_inc(mm_done, 1)

            def phase(name, xh, xl):
                n = [c for a, c, _, _ in PHASES if a == name][0] // 2
                first = 1 if FIRST_UNIT[name] == 0 else 0
                for i in range(first):
                    for j in range(2):
                        unit(name, None, i, j, xh, xl)
                with pe.Fori(first, n) as i:
                    for j in range(2):
                        unit(name, None, i, j, xh, xl)

            def statistics(b):
                pe.wait_ge(ssq_ready, KD * (b + 1))
                if b > 0:
                    pe.wait_ge(rstd_ready, b)
                for c in range(2):
                    mm = nc.tensor.matmul(stat[:, c, :], onesD[:, :], ssq[:, c * CH:(c + 1) * CH], start=True, stop=True)
                mm.then_inc(stat_ready, 1)

            pe.wait_ge(consts, 1)
            statistics(0)
            pe.wait_ge(tabB_ready, 1)
            pe.wait_ge(c_in, 16 * 8)
            for h in range(H0):
                if h >= 2:
                    pe.wait_ge(strip_ready, h - 1)
                for c in range(2):
                    mm = nc.tensor.matmul(P[:, (6 if h % 2 == 0 else 2) + c, 0:NB // 2], tabB[0:33, h, :],
                                          oh[0:33, c * NB // 2:(c + 1) * NB // 2], start=True, stop=True)
                mm.then_inc(strip_ps, 1)
            pe.wait_ge(lam_pr, 1)
            pe.wait_ge(strip_ready, H0)
            nc.tensor.matmul(P[:, 6, 0:2], ones[0:64, :], lpr[0:64, :], start=True, stop=True).then_inc(lam_ps, 1)

            pe.wait_ge(z_hi, KD)
            pe.wait_ge(z_lo, KD)
            phase("in0", zh, zl)

            pe.wait_ge(pm_free, 16)
            pe.wait_ge(rstd_ready, 1)
            pe.wait_ge(lam_ready, 1)
            for c in range(4):
                for h in range(H0):
                    mm = nc.tensor.transpose(P[:, 4 + c, h * 128:(h + 1) * 128], qkv[:, 8 + h, c * 128:(c + 1) * 128],
                                             ident[:, :])
                mm.then_inc(vt_ps, 1)
            pe.wait_ge(qpad_ready, 1)
            nc.tensor.matmul(P[0:64, 0, :], tab64[0:33, :], oh[0:33, NB:NB + PAST], start=True, stop=False)
            nc.tensor.matmul(P[0:64, 1, 0:1], tab64[0:33, :], oh[0:33, NB + PAST:NB + PAST + 1], start=True, stop=False)
            nc.tensor.matmul(P[0:64, 1, 0:1], qk2, ones[:, 0:1], start=False, stop=True)

            def decode_scores(i):
                b, h = bh(i)
                if h == 0:
                    pe.wait_ge(kv_in[b % NKV], 16 * NPG * (b // NKV + 1))
                mm = nc.tensor.matmul(P[0:64, 0, :], qpad[:, i * 64 + 0:i * 64 + 64],
                                      kv[:, b % NKV, :, h * 128:(h + 1) * 128], start=False, stop=(i == 31))
                if h == 3:
                    mm.then_inc(kv_used, 1)

            def attend(s):
                h, qt = divmod(s, 4)
                pe.wait_ge(at_done, s + 1)
                if s >= 4 and qt == 0:
                    pe.wait_ge(o_evac, h)
                for c in range(qt + 1):
                    mm = nc.tensor.matmul(P[:, 7, qt * 128:(qt + 1) * 128], vtok[:, c, h * 128:(h + 1) * 128],
                                          aT[:, c * 128:(c + 1) * 128], start=(c == 0), stop=(c == qt))
                mm.then_inc(pv_done, 1)

            for s in range(16):
                h, qt = divmod(s, 4)
                w = 128 * (qt + 1)
                if s == 0:
                    pe.wait_ge(vt_done, 4)
                for m in range(2):
                    if s >= 1:
                        pe.wait_ge(s_read, 2 * s - 1 + m)
                    part = slice(64 * m, 64 * m + 64)
                    nc.tensor.matmul(P[:, 4 + m, 0:w], qkv[part, h, qt * 128:(qt + 1) * 128], qkv[part, 4 + h, 0:w],
                                     start=True, stop=True).then_inc(s_ready, 1)
                decode_scores(2 * s)
                if s >= 1:
                    attend(s - 1)
                if qt == 2:
                    pe.wait_ge(d_ready, h + 1)
                    if h >= 1:
                        pe.wait_ge(m_lo, h)
                    for c in range(2):
                        mm = nc.tensor.matmul(P[:, 2 + c, 0:CH], poolw[:, h, :], dT[:, c * CH:(c + 1) * CH],
                                              start=True, stop=True)
                    mm.then_inc(pool_ps, 1)
                decode_scores(2 * s + 1)
                pe.wait_ge(a_ready, s + 1)
                if s >= 1:
                    pe.wait_ge(at_done, s)
                for c in range(qt + 1):
                    mm = nc.tensor.transpose(P[:, 6, c * 128:(c + 1) * 128], am[:, c * 128:(c + 1) * 128], ident[:, :])
                mm.then_inc(at_ps, 1)
            attend(15)

            pe.wait_ge(comb_ready, 1)
            for g in range(NPG + 1):
                lhs = td[0:64, g * 128:(g + 1) * 128] if g < NPG else pnew[0:64, :]
                mm = nc.tensor.matmul(P[:, 1, g * 32:(g + 1) * 32], lhs, comb[0:64, :], start=True, stop=True)
            mm.then_inc(ad_ps, 1)
            pe.wait_ge(ad_done, 1)
            pe.wait_ge(m_lo, 4)
            for i in range(32):
                b, h = bh(i)
                n = NDEC + b
                if h == 0:
                    pe.wait_ge(kv_in[n % NKV], 16 * NPG * (n // NKV + 1))
                for g in range(NPG):
                    mm = nc.tensor.matmul(P[:, 2, i:i + 1], kv[:, n % NKV, g, h * 128:(h + 1) * 128],
                                          aD[:, g * 32 + i:g * 32 + i + 1], start=(g == 0), stop=(g == NPG - 1))
                if h == 3:
                    mm.then_inc(kv_used, 1)
            for h in range(H0):
                pe.wait_ge(osq, h + 1)
                if h >= 2:
                    pe.wait_ge(oln, h - 1)
                for c in range(2):
                    mm = nc.tensor.matmul(P[:, 4 + 2 * (h % 2) + c, 0:CH], onesH[:, :],
                                          sq[:, h % 2, c * CH:(c + 1) * CH], start=True, stop=True)
                mm.then_inc(ostat, 1)
            pe.wait_ge(m_hi, 8)
            pe.wait_ge(m_lo, 8)
            pe.wait_ge(oln, 4)
            phase("out0", mh, ml)
            statistics(1)
            pe.wait_ge(z_hi, 2 * KD)
            pe.wait_ge(z_lo, 2 * KD)
            phase("gu0", zh, zl)
            pe.wait_ge(f_lo, KF)
            phase("dn0", fh, fl)
            statistics(2)
            pe.wait_ge(z_hi, 3 * KD)
            pe.wait_ge(z_lo, 3 * KD)

            pe.wait_ge(ab_split, 2)
            pe.wait_ge(rstd_ready, 3)
            for k in range(KD):
                for w, x in ((wabh, zh), (wabh, zl), (wabl, zh)):
                    for c in range(2):
                        mm = nc.tensor.matmul(P[0:40, 4 + c, 0:CH], w[:, k, :], x[:, k, c * CH:(c + 1) * CH],
                                              start=(k == 0 and w is wabh and x is zh),
                                              stop=(k == KD - 1 and w is wabl))
            mm.then_inc(ab_ps, 1)

            def stat_l2(m, s):
                pe.wait_ge(nsq, m + 1)
                if not isinstance(m, int) or m >= 2:
                    pe.wait_ge(nln, m - 1)
                for c in range(2):
                    mm = nc.tensor.matmul(P[:, 4 + 2 * s + c, 0:CH], ones[:, :], sq[:, s, c * CH:(c + 1) * CH],
                                          start=True, stop=True)
                mm.then_inc(nstat, 1)

            with pe.Fori(0, 2) as i:
                for j in range(2):
                    unit("in1", None, i, j, zh, zl)
            pe.wait_ge(rows_ready, 1)
            for i in range(2, 4):
                for j in range(2):
                    unit("in1", None, i, j, zh, zl)
                    for s in range(2):
                        stat_l2(4 * (i - 2) + 2 * j + s, s)
            pe.wait_ge(nln, 8)
            for c in range(4):
                mm = nc.tensor.transpose(P[:, 6, 40 * c:40 * c + 40], rows[0:40, c * 128:(c + 1) * 128],
                                         ident[0:40, 0:40])
            mm.then_inc(tok_ps, 1)
            pe.wait_ge(tok_done, 1)
            with pe.Fori(4, 6) as i:
                for j in range(2):
                    unit("in1", None, i, j, zh, zl)
                    for s in range(2):
                        stat_l2(4 * i - 8 + 2 * j + s, s)

            def gate_part(h, k):
                u, n = 12 + h // 2, h % 2
                if k == 0:
                    pe.wait_ge(hi_ready, FIRST_UNIT["in1"] + u + 1)
                    pe.wait_ge(lo_ready, FIRST_UNIT["in1"] + u + 1)
                    pe.wait_ge(pm_free, FIRST_TILE["in1"] + 24 + h)
                o = 128 * n + 256 * k
                for w, x in ((wh, zh), (wh, zl), (wl, zh)):
                    for c in range(2):
                        mm = nc.tensor.matmul(pm[0][:, c, :], w[:, u % 2, o:o + 128], x[:, k, c * CH:(c + 1) * CH],
                                              start=(k == 0 and w is wh and x is zh), stop=(k == KD - 1 and w is wl))
                if k == KD - 1:
                    mm.then_inc(mm_done, 1)

            def chunks(bank, lhs, rhs, name):
                for c in range(4):
                    cc = slice(c * 128, (c + 1) * 128)
                    mm = nc.tensor.matmul(P[:, bank, cc], lhs[:, cc], rhs[:, cc], start=True, stop=True)
                mm.then_inc(S[name], 1)

            def turn(bank, src, name):
                for c in range(4):
                    cc = slice(c * 128, (c + 1) * 128)
                    mm = nc.tensor.transpose(P[:, bank, cc], src[:, cc], ident[:, :])
                mm.then_inc(S[name], 1)

            def ready(h, *names):
                for n in names:
                    pe.wait_ge(*G(n, h + 1))

            pe.wait_ge(nq, 16)
            pe.wait_ge(nln, 16)
            pe.wait_ge(pm_free, FIRST_TILE["in1"] + 24)
            for h in range(HG):
                q, k, v = (qkvc[:, 8 * i + h, 0:SEQ] for i in range(3))
                ready(h, "selb")
                if h >= 1:
                    pe.wait_ge(*G("s", 4 * h))
                    ready(h - 1, "o")
                nc.tensor.matmul(P[:, 2, :], selb[0:40, h % 2, 0, :], rows[0:40, 0:SEQ], start=True, stop=True)
                nc.tensor.matmul(P[:, 3, :], selb[0:40, h % 2, 1, :], rows[0:40, 0:SEQ], start=True, stop=True)
                nc.tensor.matmul(P[:, 7, 0:8], selb[0:40, h % 2, 0, :], rows[0:40, SEQ:], start=True, stop=True)
                nc.tensor.matmul(P[:, 7, 8:16], selb[0:40, h % 2, 1, :], rows[0:40, SEQ:], start=True, stop=True
                                 ).then_inc(S["gb_ps"], 1)
                chunks(5, k, q, "qk_ps")
                gate_part(h, 0)
                ready(h, "kb")
                chunks(4, k, kbg_w, "kk_ps")
                ready(h, "gd", "bd")
                turn(7, k, "tk_ps")
                gate_part(h, 1)
                ready(h, "nt")
                turn(6, nt_z, "n_ps")
                ready(h, "kbg")
                turn(4, kbg_w, "tkb_ps")
                ready(h, "vb", "at")
                turn(5, v, "tv_ps")
                ready(h, "d", "dt", "gam")
                chunks(2, ddt, dd, "d2_ps")
                chunks(3, dd, ddt, "dt2_ps")
                gate_part(h, 2)
                ready(h, "d2", "dt2", "nf", "kd")
                chunks(6, dt2_x, d2_8, "d4_ps")
                chunks(7, d2_8, dt2_x, "dt4_ps")
                ready(h, "y1")
                chunks(2, d2_8, ya, "y2_ps")
                gate_part(h, 3)
                ready(h, "d4", "dt4", "y2", "kp")
                chunks(3, ddt, dd, "d8_ps")
                chunks(4, dd, yb, "y3_ps")
                gate_part(h, 4)
                ready(h, "d8", "y3")
                chunks(6, d2_8, ya, "y4_ps")
                gate_part(h, 5)
                ready(h, "bv")
                for l in range(3):
                    src = yb if l % 2 == 0 else ya
                    pe.wait_ge(*G("xt", 4 * h + l + 1))
                    turn(5, src, "x_ps")
                    pe.wait_ge(*G("om", 3 * h + l + 1))
                    chunks(7, offs[l], src, "z_ps")
                    if l < 2:
                        gate_part(h, 6 + l)
                    pe.wait_ge(*G("x", 3 * h + l + 1))
                    pe.wait_ge(*G("z", 3 * h + l + 1))
                    chunks(6, dt2_x, nt_z, "v_ps")
                pe.wait_ge(*G("xt", 4 * h + 4))
                chunks(4, Kp, ya, "w_ps")
                chunks(5, ya, bV, "u_ps")
                ready(h, "w", "qd")
                for c in range(4):
                    cc = slice(c * 128, (c + 1) * 128)
                    s_prev = sping[:, (c - 1) % 2, :]
                    if c > 0:
                        pe.wait_ge(*G("s", 4 * h + c))
                        nc.tensor.matmul(P[:, 2, cc], kbg_w[:, cc], s_prev, start=True, stop=True
                                         ).then_inc(S["ws_ps"], 1)
                        nc.tensor.matmul(P[:, 7, cc], s_prev, q[:, cc], start=True, stop=False)
                    pe.wait_ge(*G("u", 4 * h + c + 1))
                    nc.tensor.matmul(P[:, 3, cc], Kd[:, cc], ets_nf_u[:, cc], start=True, stop=True
                                     ).then_inc(S["ds_ps"], 1)
                    mm = nc.tensor.matmul(P[:, 7, cc], ets_nf_u[:, cc], At[:, cc], start=(c == 0), stop=True)
                mm.then_inc(S["o_ps"], 1)

            pe.wait_ge(dprep, 1)
            pe.wait_ge(*G("s", 4 * HG))
            pe.wait_ge(*G("o", HG))
            nc.tensor.matmul(P[:, 5, 0:64], ones[:, :], qkp, start=True, stop=True).then_inc(qk_dps, 1)
            for b in range(NDEC):
                if b >= 1:
                    pe.wait_ge(urow_s, b)
                nc.tensor.transpose(P[0:8, 3, 0:128], kq[:, b, :, 0], ident[:, :]).then_inc(krow_ps, 1)
                pe.wait_ge(st_in[b % 2], 16 * (b // 2 + 1))
                for h in range(HG):
                    mm = nc.tensor.matmul(P[:, 2, 16 * b + 2 * h:16 * b + 2 * h + 2],
                                          dS[:, b % 2, h * 128:(h + 1) * 128], kq[:, b, h, :], start=True, stop=True)
                mm.then_inc(kqs_ps, 1)
                pe.wait_ge(du, b + 1)
                nc.tensor.transpose(P[0:8, 4, 0:128], ud[:, b, :], ident[:, :]).then_inc(du_ps, 1)
                pe.wait_ge(um_s, b + 1)
                pe.wait_ge(krow_s, b + 1)
                if b >= 1:
                    pe.wait_ge(snew, b)
                for c in range(2):
                    mm = nc.tensor.matmul(P[:, 6 + c, :], krow[0:8, :], um[0:8, c * 512:(c + 1) * 512],
                                          start=True, stop=True)
                mm.then_inc(outer_ps, 1)
            for h in range(HG):
                pe.wait_ge(o1sq, h + 1)
                if h >= 2:
                    pe.wait_ge(o1ln, h - 1)
                elif h == 0:
                    pe.wait_ge(snew, NDEC)
                for c in range(2):
                    mm = nc.tensor.matmul(P[:, 4 + 2 * (h % 2) + c, 0:CH], onesH[:, :],
                                          sq[:, h % 2, c * CH:(c + 1) * CH], start=True, stop=True)
                mm.then_inc(o1stat, 1)
            pe.wait_ge(m1_hi, HG)
            pe.wait_ge(m1_lo, HG)
            phase("out1", mh1, ml1)
            statistics(3)
            pe.wait_ge(z_hi, 4 * KD)
            pe.wait_ge(z_lo, 4 * KD)
            phase("gu1", zh, zl)
            pe.wait_ge(f_lo, 2 * KF)
            phase("dn1", fh, fl)
            statistics(4)


NORM = (P_MIX, P_FFN, P_MIX + 8, P_FFN + 8)


def kernel(**inputs):
    import numpy as np
    import concourse.bacc as bacc
    from concourse.bass_utils import run_bass_kernel_spmd
    a = {k: np.asarray(v) for k, v in inputs.items()}
    f = np.float32

    def units(w, width):
        k, n = w.shape
        return np.ascontiguousarray(w.reshape(k // 128, 128, n // width, width).transpose(2, 1, 0, 3)
                                    ).reshape(n // width, 128, -1)

    def rows(v):
        return v.reshape(-1, 128).T

    def gate_up(w):
        g, u = units(w[:, :DFF], 256), units(w[:, DFF:], 256)
        return np.stack([g, u], 1).reshape(22, 128, -1)

    x = np.concatenate([a["x_prompt"][0], a["x_sample"][:, 0]])
    pool_pages = a["cache_k"].shape[0]
    n = np.arange(0, PAST + 1)
    large = 16 + (np.log(np.maximum(n, 1).astype(f) / f(16)) / f(np.log(8.0)) * f(16)).astype(np.int32)
    bucket = np.where(n < 16, n, np.minimum(large, 31))
    onehot = np.zeros((33, NB + PAST + 1), f)
    for m in range(NB):
        d = SEQ - 1 - m
        onehot[bucket[d] if d >= 0 else 32, m] = 1
    for t in range(PAST + 1):
        onehot[bucket[PAST - t], NB + t] = 1
    sel64 = np.zeros((64, 34), f)
    for r in range(64):
        sel64[r, r % 2] = 1
        sel64[r, 2 + r // 2] = 1
    p, n = np.arange(128)[:, None], np.arange(128)[None]
    masks = np.stack([p <= n, p < n, p // 16 == n // 16] +
                     [(p // (2 * s) == n // (2 * s)) & (p // s > n // s) for s in (16, 32, 64)], 1).astype(f)
    wab = np.zeros((128, KD, 40), f)
    w2 = a["w_in_odd"][0][:, 4096:].reshape(KD, 128, 16).transpose(1, 0, 2)
    wab[:, :, 0:8], wab[:, :, 32:40] = w2[:, :, 0:8], w2[:, :, 8:16]
    arrays = {
        "xT": np.ascontiguousarray(x.T.reshape(KD, 128, T).transpose(1, 0, 2)),
        "w_in0": units(a["w_in_even"][0], 256), "w_out0": units(a["w_out_even"][0], 256),
        "w_gu": np.stack([gate_up(w) for w in a["w_gate_up"]]),
        "w_dn": np.stack([units(w, 128) for w in a["w_down"]]),
        "w_in1": units(a["w_in_odd"][0][:, :4096], 256), "w_out1": units(a["w_out_odd"][0], 256),
        "params": np.ascontiguousarray(np.concatenate(
            [rows(a[k]) for k in ("norm_mix", "norm_ffn", "norm_final", "pool_scale", "subln_w", "o_norm")], 1)),
        "convw": np.ascontiguousarray(rows(a["conv_w"][0])),
        "wab": wab,
        "gates": np.ascontiguousarray(np.concatenate([a["a_log"], a["dt_bias"]]).T),
        "cache_k": np.ascontiguousarray(a["cache_k"][:, 0].transpose(0, 3, 2, 1)).reshape(pool_pages, 128, 512),
        "cache_v": np.ascontiguousarray(a["cache_v"][:, 0]).reshape(pool_pages, 128, 512),
        "pages": a["page_table"].reshape(1, -1),
        "pool_w": np.ascontiguousarray(a["pool_w"][0].transpose(1, 0, 2)),
        "pool_state": np.ascontiguousarray(a["state_pool"][0].reshape(NDEC, 15, 4, 128).transpose(3, 2, 0, 1)),
        "conv_state": np.ascontiguousarray(a["state_conv"][0].reshape(NDEC, 3, 24, 128).transpose(3, 2, 0, 1)),
        "delta_state": np.ascontiguousarray(a["state_delta"][0].transpose(0, 2, 1, 3)).reshape(NDEC, 128, HG * 128),
        "rel_tab": np.concatenate([a["rel_bias"], np.full((1, 4), NEG, f)]),
        "onehot": onehot,
        "lam_vec": np.ascontiguousarray(np.stack([a[k][0] for k in ("lambda_q1", "lambda_q2", "lambda_k1",
                                                                   "lambda_k2")], 1)),
        "sel64": sel64,
        "invcnt": np.ascontiguousarray(np.broadcast_to((1 / np.arange(1, 16)).astype(f), (128, 15))),
        "masks": np.ascontiguousarray(masks),
    }
    outs = {"o_y": (128, KD, T), "o_k": (128, 4, T), "o_v": (128, 4, T), "o_pp": (128, 4, 15),
            "o_ps": (128, 4, NDEC, 16), "o_ct": (128, 24, 11), "o_cs": (128, 24, NDEC, 4),
            "o_dp": (128, HG, 128), "o_ds": (NDEC, 128, HG * 128)}
    nc = bacc.Bacc("TRN2", target_bir_lowering=False, num_devices=1)
    aps = [nc.dram_tensor(k, v.shape, mybir.dt.from_np(v.dtype), kind="ExternalInput").ap() for k, v in arrays.items()]
    aps += [nc.dram_tensor(k, s, mybir.dt.float32, kind="ExternalOutput").ap() for k, s in outs.items()]
    hybrid_trunk(nc, *aps)
    r = run_bass_kernel_spmd(nc, [arrays], core_ids=[0]).results[0]
    feat = {k: r[k].transpose(2, 1, 0).reshape(T, -1) for k in ("o_y", "o_k", "o_v")}
    k, v = (feat[n].reshape(T, 4, 128) for n in ("o_k", "o_v"))
    return (feat["o_y"][None, :SEQ], feat["o_y"][SEQ:, None], k[None, None, :SEQ], v[None, None, :SEQ],
            k[SEQ:, None, None], v[SEQ:, None, None],
            r["o_pp"].transpose(2, 1, 0).reshape(1, 1, 15, 512),
            r["o_ps"][:, :, :, 1:].transpose(2, 3, 1, 0).reshape(1, NDEC, 15, 512),
            r["o_ct"][:, :, :3].transpose(2, 1, 0).reshape(1, 1, 3, 3072),
            r["o_cs"][:, :, :, 1:].transpose(2, 3, 1, 0).reshape(1, NDEC, 3, 3072),
            r["o_dp"].transpose(1, 0, 2)[None, None],
            r["o_ds"].reshape(NDEC, 128, HG, 128).transpose(0, 2, 1, 3)[None])
```

```python
import concourse.bass as bass
from concourse import mybir
from contextlib import ExitStack

D, SEQ, NDEC, PAST, PAGE = 1024, 512, 8, 512, 128
T = SEQ + NDEC
CH = T // 2
KD = D // 128
H0, HALF = 4, 64
PW = (2, 4, 8, 16)
DFF = 2816
KF = DFF // 128
HG = 8
NPG = PAST // PAGE
WS = 64.0
EPS = 1e-6
LAM0 = 0.2
NEG = -1e30
NB = 640
SKEW = NB + 1

UNIT = KF * 128
PHASES = (("in0", 8, 2, KD * 256), ("out0", 4, 2, KD * 256), ("gu0", 22, 2, KD * 256), ("dn0", 8, 1, UNIT),
          ("in1", 16, 2, KD * 256), ("out1", 4, 2, KD * 256), ("gu1", 22, 2, KD * 256), ("dn1", 8, 1, UNIT))
FIRST_UNIT, FIRST_TILE, WORDS = {}, {}, []
_u = _t = 0
for _n, _c, _j, _w in PHASES:
    FIRST_UNIT[_n], FIRST_TILE[_n] = _u, _t
    _u, _t = _u + _c, _t + _c * _j
    WORDS += [_w] * _c
UNITS = _u
HEAD_TILES = {
    "pe": ["gb_ps", "qk_ps", "kk_ps", "tk_ps", "n_ps", "tkb_ps", "tv_ps", "d2_ps", "dt2_ps", "d4_ps", "dt4_ps", "y2_ps",
           "d8_ps", "y3_ps", "y4_ps"] + ["x_ps", "z_ps", "v_ps"] * 3 + ["w_ps", "u_ps", "ds_ps"] +
          ["ws_ps", "ds_ps"] * 3 + ["o_ps"],
    "act": ["gam", "gd", "et", "kd4", "nf", "kd", "d2", "bv", "d4", "dt4", "d8", "x", "x", "x", "w", "o"],
    "dve": ["ex", "bd", "kb", "vb", "nt", "dt", "at", "d", "y1", "dt2", "kp", "y2", "y3", "xt"] + ["z", "xt"] * 3 +
           ["u", "s"] * 4,
    "pool": ["selb", "ets", "eti", "kbg", "om", "om", "om", "qd"],
}
P_MIX, P_FFN, P_FIN, P_POOL, P_SUB, P_ONORM, P_N = 0, 16, 32, 40, 44, 45, 46


def hybrid_trunk(nc, xT, w_in0, w_out0, w_gu, w_dn, w_in1, w_out1, params, convw, wab, gates, cache_k, cache_v, pages,
                 pool_w, pool_state, conv_state, delta_state, rel_tab, onehot, lam_vec, sel64, invcnt, masks,
                 o_y, o_k, o_v, o_pp, o_ps, o_ct, o_cs, o_dp, o_ds):
    f32, f16, i32 = mybir.dt.float32, mybir.dt.float16, mybir.dt.int32
    ALU, ACT, AX = mybir.AluOpType, mybir.ActivationFunctionType, mybir.AxisListType
    MUL, ADD, SUB, MAX, MIN = ALU.mult, ALU.add, ALU.subtract, ALU.max, ALU.min

    ctx = ExitStack()
    with ctx:
        def sb(name, shape, dt=f32):
            return ctx.enter_context(nc.sbuf_tensor(name, shape, dt))

        def sem(name):
            return ctx.enter_context(nc.semaphore(name))

        hT = sb("hT", [128, KD, T])
        zh = sb("zh", [128, KD, T], f16)
        zl = sb("zl", [128, KD, T], f16)
        stage = sb("stage", [128, 2, UNIT])
        wh = sb("wh", [128, 2, UNIT], f16)
        wl = sb("wl", [128, 2, UNIT], f16)
        rstd = sb("rstd", [128, T])
        sq = sb("sq", [128, 2, T])
        ssq = sb("ssq", [128, T])
        par = sb("par", [128, P_N])
        ident = sb("ident", [128, 128])
        ones = sb("ones", [128, 128])
        onesD = sb("onesD", [128, 128])
        onesH = sb("onesH", [128, 128])
        epsc = sb("epsc", [128, 3])
        pt = sb("pt", [1, NDEC * NPG], i32)
        ARENA = 30936
        arena = sb("arena", [128, ARENA])
        P = ctx.enter_context(nc.psum_tensor("P", [128, 8, 512], f32))
        pm = [P[:, 2 * j:2 * j + 2, 0:CH] for j in range(2)]
        stat = P[:, 4:6, 0:CH]

        def carver():
            at = [0]

            def take(n, dt=f32):
                n32 = n if dt == f32 else n // 2
                at[0] += n32
                assert at[0] <= ARENA, at[0]
                v = arena[:, at[0] - n32:at[0]]
                return v if dt == f32 else v.bitcast(dt)
            return take

        a0 = carver()
        qkv = a0(12 * T).rearrange("p (a t) -> p a t", t=T)
        mix = a0(KD * T)
        mh = mix[:, 0:KD * T // 2].bitcast(f16).rearrange("p (a t) -> p a t", t=T)
        ml = mix[:, KD * T // 2:].bitcast(f16).rearrange("p (a t) -> p a t", t=T)
        UP = 16 + T
        upad = a0(4 * UP).rearrange("p (g t) -> p g t", t=UP)
        win = a0(2 * (16 + SEQ)).rearrange("p (a t) -> p a t", a=2)
        dT = a0(T)
        ext = a0(4 * NDEC * 16).rearrange("p (g b t) -> p g b t", g=4, b=NDEC)
        extsum = a0(4 * NDEC).rearrange("p (g b) -> p g b", g=4)
        inv = a0(15)
        vtok = a0(4 * 512).rearrange("p (c n) -> p c n", c=4)
        biasT = a0(4 * 512).rearrange("p (h n) -> p h n", h=4)
        pr = a0(2 * 512).rearrange("p (m n) -> p m n", m=2)
        am = a0(512)
        aT = a0(512)
        mx, nm, ls, rl = a0(2), a0(2), a0(2), a0(2)
        oT = a0(4 * T).rearrange("p (h t) -> p h t", t=T)
        NKV = 3
        kv = a0(NKV * NPG * 512).rearrange("p (s g n) -> p s g n", s=NKV, g=NPG)
        poolw = a0(4 * 128).rearrange("p (g n) -> p g n", g=4)
        qk2 = a0(64)
        td = a0(PAST + 1)
        tsm = a0(8)
        comb = a0(32)
        pnew = a0(128)
        aD = a0(32)
        vn = a0(32)
        lamt = a0(4)
        lpr = a0(2)
        lame = a0(2)
        nlam = a0(1)
        subw = a0(1)
        sel = a0(34)
        tab = a0(4)
        tab64 = a0(64)
        qpad = [mix[:, KD * T // 4:][:, 0:1024], mix[:, 3 * KD * T // 4:][:, 0:1024]]
        apad = qpad[0]
        oh = oT.rearrange("p h t -> p (h t)")[:, 0:NB + PAST + 1]
        tabB = am.rearrange("p (h n) -> p h n", h=4)
        strips = mix[:, 0:H0 * NB].rearrange("p (h n) -> p h n", h=H0)
        oy = pr.rearrange("p m n -> p (m n)")
        ors = [oy[:, 0:T], vtok.rearrange("p c n -> p (c n)")[:, 0:T]]
        yn = [biasT.rearrange("p h n -> p (h n)")[:, i * T:(i + 1) * T] for i in range(2)]

        a2 = carver()
        qkvc = a2(6 * T).rearrange("p (s a t) -> p s a t", s=2, a=3)
        sz = a2(2 * T).rearrange("p (s t) -> p s t", s=2)
        oh1 = a2(2 * T).rearrange("p (s t) -> p s t", s=2)
        tail = a2(24 * 11).rearrange("p (a t) -> p a t", t=11)
        cext = a2(24 * NDEC * 4).rearrange("p (a b t) -> p a b t", a=24, b=NDEC)
        cw = a2(96).rearrange("p (i a) -> p i a", i=4)
        msk = a2(6 * 128).rearrange("p (m n) -> p m n", m=6)
        rows = a2(T)
        tokm = a2(4 * 40).rearrange("p (c n) -> p c n", c=4)
        selb = a2(2 * 2 * 128).rearrange("p (s m n) -> p s m n", s=2, m=2)
        gD, bD = (a2(64).rearrange("p (h b) -> p h b", h=HG) for _ in range(2))
        gate = a2(8)
        sall = a2(HG * 128).rearrange("p (h n) -> p h n", h=HG)
        sping = a2(2 * 128).rearrange("p (s n) -> p s n", s=2)
        d4, kd4 = a2(4), a2(4)
        mix1 = a2(KD * T)
        mh1 = mix1[:, 0:KD * T // 2].bitcast(f16).rearrange("p (a t) -> p a t", t=T)
        ml1 = mix1[:, KD * T // 2:].bitcast(f16).rearrange("p (a t) -> p a t", t=T)
        pre = a2(2 * 524).rearrange("p (s t) -> p s t", s=2)
        rs2 = a2(T)
        ors1 = a2(T)
        yn1 = a2(T)
        dS = a2(2 * 1024).rearrange("p (s n) -> p s n", s=2)
        um = a2(1024)
        krow, urow = a2(128), a2(128)
        ud, od, t8, qkp = a2(8), a2(8), a2(8), a2(8)
        ctmp = a2(24).rearrange("p (a b) -> p a b", a=3)
        rest = a2(18 * 512)
        (et, ets_nf_u, gamB, kbg_w, nt_z, At, dd, ddt, off1, off2, off3, d2_8, dt2_x, ya, yb, Kd, Kp, bV) = (
            rest[:, i * 512:(i + 1) * 512] for i in range(18))
        offs = (off1, off2, off3)
        rowt = rest[:, 0:4 * T].rearrange("p (s t) -> p s t", s=4)
        wabf = rest[:, 4 * T:4 * T + 320]
        wabh, wabl = (rest[:, 4 * T + 320 + 160 * i:4 * T + 480 + 160 * i].bitcast(f16).rearrange(
            "p (k n) -> p k n", k=KD) for i in range(2))

        a1 = carver()
        fh = a1(KF * T, f16).rearrange("p (a t) -> p a t", t=T)
        fl = a1(KF * T, f16).rearrange("p (a t) -> p a t", t=T)
        gt = a1(2 * T).rearrange("p (a t) -> p a t", t=T)
        ut = a1(2 * T).rearrange("p (a t) -> p a t", t=T)
        gu = a1(2 * T).rearrange("p (a t) -> p a t", t=T)
        yf = a1(2 * T).rearrange("p (a t) -> p a t", t=T)

        scratch = nc.dram_tensor("bias_scratch", (4, 128 * SKEW), f32).ap()

        x_in, c_in, aux_in = sem("x_in"), sem("c_in"), sem("aux_in")
        kv_in = [sem(f"kv_in{i}") for i in range(NKV)]
        w_in = [sem(f"w_in{i}") for i in range(2)]
        consts = sem("consts")
        hi_ready, lo_ready = sem("hi_ready"), sem("lo_ready")
        mm_done, pm_free = sem("mm_done"), sem("pm_free")
        z_hi, z_lo, sq_ready, ssq_ready, stat_ready = (sem("z_hi"), sem("z_lo"),
                                                                sem("sq_ready"), sem("ssq_ready"), sem("stat_ready"))
        ln_done, rstd_ready = sem("ln_done"), sem("rstd_ready")
        silu_done, prod_done, f_hi, f_lo = sem("silu_done"), sem("prod_done"), sem("f_hi"), sem("f_lo")
        outs, dve_step, pool_step, act_step = sem("outs"), sem("dve_step"), sem("pool_step"), sem("act_step")
        y_ready = sem("y_ready")
        y_out = [sem(f"y_out{i}") for i in range(2)]
        tabB_ready, strip_ps, strip_ready, strip_out, bias_in = (sem("tabB_ready"), sem("strip_ps"),
                                                                 sem("strip_ready"), sem("strip_out"), sem("bias_in"))
        lam_pr, lam_ps, lam_ready = sem("lam_pr"), sem("lam_ps"), sem("lam_ready")
        vt_ps, vt_done = sem("vt_ps"), sem("vt_done")
        dq_ready, s_ready, s_read, nm_ready, exp_done, a_ready = (sem("dq_ready"), sem("s_ready"), sem("s_read"),
                                                                    sem("nm_ready"), sem("exp_done"), sem("a_ready"))
        at_ps, at_done, pv_done, o_evac = sem("at_ps"), sem("at_done"), sem("pv_done"), sem("o_evac")
        kv_used, dp_ready, comb_ready, ad_ps, ad_done = (sem("kv_used"), sem("dp_ready"),
                                                         sem("comb_ready"), sem("ad_ps"), sem("ad_done"))
        dec_o = sem("dec_o")
        d_ready, pool_ps, m_hi, m_lo = sem("d_ready"), sem("pool_ps"), sem("m_hi"), sem("m_lo")
        osq, ostat, oln, ors_ready, yn_ready = (sem("osq"), sem("ostat"), sem("oln"), sem("ors_ready"),
                                                sem("yn_ready"))
        dext = sem("dext")
        l1_in, l1_free, ab_split, ab_ps, ab_step, rows_ready, tok_ps, tok_done = (
            sem("l1_in"), sem("l1_free"), sem("ab_split"), sem("ab_ps"), sem("ab_step"), sem("rows_ready"),
            sem("tok_ps"), sem("tok_done"))
        conv_done, tail_done, convd_done, csilu = (sem("conv_done"), sem("tail_done"), sem("convd_done"),
                                                   sem("csilu"))
        nsq, nstat, nln, nrs, nq = sem("nsq"), sem("nstat"), sem("nln"), sem("nrs"), sem("nq")
        head_done = {e: sem(f"head_{e}") for e in HEAD_TILES}
        S = {n: head_done[e] for e, tiles in HEAD_TILES.items() for n in tiles}

        def G(name, n):
            e = next(e for e, tiles in HEAD_TILES.items() if name in tiles)
            at = [i for i, t in enumerate(HEAD_TILES[e]) if t == name]
            h, i = divmod(n - 1, len(at))
            return head_done[e], len(HEAD_TILES[e]) * h + at[i] + 1
        st_in = [sem(f"st_in{i}") for i in range(2)]
        st_out = [sem(f"st_out{i}") for i in range(2)]
        dprep, kqs_ps, du, du_ps, krow_s, urow_s, um_s, outer_ps, sdec, snew, zsilu = (
            sem("dprep"), sem("kqs_ps"), sem("du"), sem("du_ps"), sem("krow_s"),
            sem("urow_s"), sem("um_s"), sem("outer_ps"), sem("sdec"), sem("snew"), sem("zsilu"))
        o1sq, o1stat, o1ln, o1rs, yo, yz, m1_hi, m1_lo = (sem("o1sq"), sem("o1stat"), sem("o1ln"), sem("o1rs"),
                                                          sem("yo"), sem("yz"), sem("m1_hi"), sem("m1_lo"))

        block = ctx.enter_context(nc.Block())

        def bh(i):
            return divmod(i, H0)

        def paired(ap):
            return ap.rearrange("p (c n) -> p c n", c=2)

        @block.sync
        def _(sp):
            def weights(src, u, j, index, words):
                if not isinstance(u, int) or u >= 2:
                    sp.wait_ge(hi_ready, u - 1)
                    sp.wait_ge(lo_ready, u - 1)
                sp.dma_start(stage[:, j, 0:words], src[index].rearrange("a p n -> (a p) n")
                             if not isinstance(index, int) else src[index]).then_inc(w_in[j], 16)

            def stream(src, name, skip=0):
                base = FIRST_UNIT[name]
                n, words = [(c, w) for a, c, _, w in PHASES if a == name][0]
                with sp.Fori(skip // 2, n // 2) as i:
                    for j in range(2):
                        weights(src, base + 2 * i + j, j, bass.ds(2 * i + j, 1), words)

            sp.dma_start(hT[:, :, :], xT).then_inc(x_in, 16)
            sp.dma_start(par[:, :], params).then_inc(x_in, 16)
            for u in range(2):
                weights(w_in0, u, u, u, WORDS[u])
            sp.dma_start(pt[:, :], pages).then_inc(c_in, 16)
            sp.dma_start(oh[0:33, :], onehot).then_inc(c_in, 16)
            sp.dma_start(tab[0:33, :], rel_tab).then_inc(c_in, 16)
            sp.dma_start(lamt[0:64, :], lam_vec).then_inc(c_in, 16)
            sp.dma_start(sel[0:64, :], sel64).then_inc(c_in, 16)
            sp.dma_start(inv, invcnt).then_inc(c_in, 16)
            sp.dma_start(poolw, pool_w).then_inc(c_in, 16)
            sp.dma_start(ext[:, :, :, 0:15], pool_state).then_inc(c_in, 16)

            sp.wait_ge(c_in, 16 * 8)
            with ExitStack() as es:
                def load_kv(n):
                    src, b, s = (cache_k, n, n % NKV) if n < NDEC else (cache_v, n - NDEC, n % NKV)
                    if n >= NKV:
                        sp.wait_ge(kv_used, n - NKV + 1)
                    for g in range(NPG):
                        i = b * NPG + g
                        page = sp.value_load(pt[0:1, i:i + 1], min_val=0, max_val=cache_k.shape[0] - 1)
                        sp.dma_start(kv[:, s, g, :], src[bass.ds(page, 1)].rearrange("a p n -> (a p) n")
                                     ).then_inc(kv_in[s], 16)

                for n in range(NKV):
                    load_kv(n)
                for u in range(2, 4):
                    weights(w_in0, u, u % 2, u, WORDS[u])
                sp.wait_ge(strip_ready, H0)
                sp.dma_start(scratch.rearrange("h (p m) -> p h m", m=SKEW)[:, :, 0:NB], strips).then_inc(strip_out, 16)
                sp.wait_ge(strip_out, 16)
                sp.dma_start(biasT, scratch[:, 127:127 + 128 * NB].rearrange("h (p c) -> p h c", c=NB)[:, :, 0:512]
                             ).then_inc(bias_in, 16)
                stream(w_in0, "in0", skip=4)
                for u in range(FIRST_UNIT["out0"], FIRST_UNIT["out0"] + 2):
                    weights(w_out0, u, u % 2, u - FIRST_UNIT["out0"], WORDS[u])
                sp.wait_ge(pm_free, FIRST_TILE["out0"])
                sp.dma_start(o_k, qkv[:, 4:8, :]).then_inc(outs, 16)
                sp.dma_start(o_v, qkv[:, 8:12, :]).then_inc(outs, 16)
                sp.dma_start(o_pp, upad[:, :, 16 + SEQ - 15:16 + SEQ]).then_inc(outs, 16)
                sp.wait_ge(dext, 1)
                sp.dma_start(o_ps, ext).then_inc(outs, 16)
                for n in range(NKV, 2 * NDEC):
                    load_kv(n)
            stream(w_out0, "out0", skip=2)
            stream(w_gu[0], "gu0")
            stream(w_dn[0], "dn0")
            for u in range(FIRST_UNIT["in1"], FIRST_UNIT["in1"] + 2):
                weights(w_in1, u, u % 2, u - FIRST_UNIT["in1"], WORDS[u])
            sp.wait_ge(pm_free, FIRST_TILE["in1"])
            sp.dma_start(wabf, wab.rearrange("p k n -> p (k n)")).then_inc(l1_in, 16)
            sp.dma_start(gate[0:8, 0:2], gates).then_inc(l1_in, 16)
            sp.dma_start(cw, convw).then_inc(l1_in, 16)
            sp.dma_start(msk, masks).then_inc(l1_in, 16)
            sp.dma_start(cext[:, :, :, 0:3], conv_state).then_inc(l1_in, 16)
            for h in range(2):
                sp.dma_start(dS[:, h, :], delta_state[h]).then_inc(st_in[h], 16)
            for u in range(2, 6):
                weights(w_in1, FIRST_UNIT["in1"] + u, u % 2, u, WORDS[FIRST_UNIT["in1"] + u])
            for h in range(HG):
                for u in range(2 * h + 6, 2 * h + 8):
                    if u < 16:
                        weights(w_in1, FIRST_UNIT["in1"] + u, u % 2, u, WORDS[FIRST_UNIT["in1"] + u])
                    elif u < 18:
                        weights(w_out1, FIRST_UNIT["in1"] + u, u % 2, u - 16, WORDS[FIRST_UNIT["in1"] + u])
                sp.wait_ge(snew, h + 1)
                sp.dma_start(o_ds[h], dS[:, h % 2, :]).then_inc(st_out[h % 2], 16)
                if h + 2 < HG:
                    sp.wait_ge(st_out[h % 2], 16 * (h // 2 + 1))
                    sp.dma_start(dS[:, h % 2, :], delta_state[h + 2]).then_inc(st_in[h % 2], 16)
            sp.wait_ge(convd_done, HG)
            sp.dma_start(o_ct, tail).then_inc(outs, 16)
            sp.dma_start(o_cs, cext).then_inc(outs, 16)
            sp.wait_ge(*G("s", 4 * HG))
            sp.dma_start(o_dp, sall).then_inc(outs, 16)
            stream(w_out1, "out1", skip=2)
            stream(w_gu[1], "gu1")
            stream(w_dn[1], "dn1")
            for k in range(KD):
                sp.wait_ge(y_ready, k + 1)
                sp.dma_start(o_y[:, k, :], yf[:, k % 2, :]).then_inc(y_out[k % 2], 16)
            sp.wait_ge(outs, 16 * 7)
            for j in range(2):
                sp.wait_ge(st_out[j], 16 * NDEC // 2)
            for j in range(2):
                sp.wait_ge(y_out[j], 16 * KD // 2)

        @block.gpsimd
        def _(pool):
            steps = [0]

            def link(ins):
                steps[0] += 1
                ins.then_inc(pool_step, 1)
                pool.wait_ge(pool_step, steps[0])

            link(nc.gpsimd.memset(ident[:, :], 0.0))
            link(nc.gpsimd.affine_select(out=ident[:, :], in_=ident[:, :], compare_op=ALU.not_equal, fill=1.0, base=0,
                                         pattern=[[-1, 128]], channel_multiplier=1))
            nc.gpsimd.memset(ones[:, :], 1.0)
            nc.gpsimd.memset(onesD[:, :], 1.0 / D)
            nc.gpsimd.memset(onesH[:, :], 1.0 / 128)
            nc.gpsimd.memset(epsc[:, 0:1], EPS * WS * WS)
            nc.gpsimd.memset(epsc[:, 1:2], EPS)
            nc.gpsimd.memset(epsc[:, 2:3], EPS * 128)
            nc.gpsimd.memset(upad[:, :, 0:16], 0.0)
            nc.gpsimd.memset(qk2, 0.0)
            pool.nop().then_inc(consts, 1)
            pool.wait_ge(c_in, 16 * 8)
            for h in range(H0):
                link(nc.gpsimd.tensor_copy(tabB[0:33, h, :], tab[0:33, h:h + 1].to_broadcast([33, 128])))
            for m in range(2):
                link(nc.gpsimd.tensor_copy(tab64[0:33, :].rearrange("p (b h m) -> p b h m", b=NDEC, m=2)[:, :, :, m],
                                           tab[0:33, :].unsqueeze(1).to_broadcast([33, NDEC, H0])))
            pool.nop().then_inc(tabB_ready, 1)

            def sum_squares(b):
                for k in range(KD):
                    pool.wait_ge(sq_ready, KD * b + k + 1)
                    if k == 0:
                        if b > 0:
                            pool.wait_ge(stat_ready, b)
                        ins = nc.gpsimd.tensor_copy(ssq[:, :], sq[:, 0, :])
                    else:
                        ins = nc.gpsimd.tensor_tensor(ssq[:, :], ssq[:, :], sq[:, k % 2, :], ADD)
                    ins.then_inc(ssq_ready, 1)
                    pool.wait_ge(ssq_ready, KD * b + k + 1)

            sum_squares(0)

            pool.wait_ge(strip_out, 16)
            link(nc.gpsimd.memset(qpad[0], 0.0))
            link(nc.gpsimd.memset(qpad[1], 0.0))
            pool.nop().then_inc(consts, 1)
            pool.wait_ge(pm_free, 4)
            for g, w in enumerate(PW):
                src = upad[:, g, 0:16 + SEQ]
                for l in range(g + 1):
                    s, lo = 1 << l, (2 << l) - 1
                    dst = win[:, l % 2, :]
                    link(nc.gpsimd.tensor_tensor(dst[:, lo:], src[:, lo:], src[:, lo - s:16 + SEQ - s], ADD))
                    src = dst
                if g >= 1:
                    pool.wait_ge(pool_ps, g)
                link(nc.gpsimd.tensor_scalar(dT[:, 0:SEQ], src[:, 16:], 1.0 / w, None, MUL))
                link(nc.gpsimd.tensor_tensor(dT[:, 0:w - 1], src[:, 16:15 + w], inv[:, 0:w - 1], MUL))
                link(nc.gpsimd.tensor_tensor(dT[:, 0:SEQ], dT[:, 0:SEQ], upad[:, g, 16:16 + SEQ], SUB))
                if g == 0:
                    pool.wait_ge(dext, 1)
                link(nc.gpsimd.tensor_scalar(dT[:, SEQ:T], extsum[:, g, :], 1.0 / w, None, MUL))
                nc.gpsimd.tensor_tensor(dT[:, SEQ:T], dT[:, SEQ:T], ext[:, g, :, 15], SUB).then_inc(d_ready, 1)
                if g == 1:
                    pool.wait_ge(kv_used, NDEC)
                    nc.gpsimd.memset(apad, 0.0).then_inc(consts, 1)

            for h in range(H0):
                pool.wait_ge(m_hi, 4 + h + 1)
                nc.gpsimd.tensor_tensor(ml[:, 4 + h, :], yn[h % 2], mh[:, 4 + h, :], SUB).then_inc(m_lo, 1)
            sum_squares(1)

            def ffn_up(layer):
                name = f"gu{layer}"

                def body(i):
                    t = FIRST_TILE[name] + 4 * i
                    f = 2 * (11 * layer + i)
                    for j in range(2):
                        pool.wait_ge(silu_done, f + j + 1)
                        pool.wait_ge(pm_free, t + 2 + j + 1)
                        nc.gpsimd.tensor_tensor(gu[:, j, :], gt[:, j, :], ut[:, j, :], MUL).then_inc(prod_done, 1)
                    for j in range(2):
                        pool.wait_ge(f_hi, f + j + 1)
                        nc.gpsimd.tensor_tensor(fl[:, bass.ds(2 * i + j, 1), :], gu[:, j:j + 1, :],
                                                fh[:, bass.ds(2 * i + j, 1), :], SUB).then_inc(f_lo, 1)
                    pool.wait_ge(f_lo, f + 2)
                with pool.Fori(0, 11) as i:
                    body(i)

            ffn_up(0)
            sum_squares(2)

            pool.wait_ge(pm_free, FIRST_TILE["in1"])
            nc.gpsimd.memset(rows[0:40, :], 0.0)
            nc.gpsimd.memset(pre[:, :, 0:3], 0.0).then_inc(l1_free, 1)
            pool.wait_ge(l1_in, 16 * 5)

            def tail_of(h, kind):
                pool.wait_ge(pm_free, FIRST_TILE["in1"] + 4 * h + kind + 1)
                nc.gpsimd.tensor_copy(tail[:, 8 * kind + h, :], pre[:, (3 * h + kind) % 2, SEQ:SEQ + 11]
                                      ).then_inc(tail_done, 1)

            def decode_conv(h):
                pool.wait_ge(tail_done, 3 * h + 3)
                link(nc.gpsimd.tensor_copy(cext[:, h:24:8, :, 3], tail[:, h:24:8, 3:11]))
                dst = qkvc[:, h % 2, :, SEQ:]
                for i in range(4):
                    wt = cw[:, i, h:24:8].unsqueeze(2).to_broadcast([128, 3, NDEC])
                    link(nc.gpsimd.tensor_tensor(dst if i == 0 else ctmp, cext[:, h:24:8, :, i], wt, MUL))
                    if i > 0:
                        link(nc.gpsimd.tensor_tensor(dst, dst, ctmp, ADD))
                pool.nop().then_inc(convd_done, 1)

            def square(h, kind):
                pool.wait_ge(csilu, 3 * h + kind + 1)
                if h >= 1:
                    pool.wait_ge(nstat, 2 * h)
                x = qkvc[:, h % 2, kind, :]
                nc.gpsimd.tensor_tensor(sq[:, kind, :], x, x, MUL).then_inc(nsq, 1)

            def normalize(h, kind):
                pool.wait_ge(nrs, 2 * h + kind + 1)
                x = qkvc[:, h % 2, kind, :]
                nc.gpsimd.tensor_tensor(x, x, rs2, MUL).then_inc(nq, 1)

            def select_head(h):
                if h >= 2:
                    pool.wait_ge(*G("gb_ps", h - 1))
                nc.gpsimd.tensor_copy(selb[0:40, h % 2, 0, :], ident[0:40, h:h + 1].to_broadcast([40, 128]))
                nc.gpsimd.tensor_copy(selb[0:40, h % 2, 1, :], ident[0:40, 32 + h:33 + h].to_broadcast([40, 128])
                                      ).then_inc(S["selb"], 1)

            def gate_out(h):
                pool.wait_ge(yo, h + 1)
                pool.wait_ge(zsilu, h + 1)
                nc.gpsimd.tensor_tensor(yn1, yn1, sz[:, h % 2, :], MUL).then_inc(yz, 1)

            def gate_lo(h):
                pool.wait_ge(m1_hi, h + 1)
                nc.gpsimd.tensor_tensor(ml1[:, h, :], yn1, mh1[:, h, :], SUB).then_inc(m1_lo, 1)

            for kind in range(3):
                tail_of(0, kind)
            decode_conv(0)
            square(0, 0)
            square(0, 1)
            select_head(0)

            def four(ap):
                return ap.rearrange("p (c n) -> p c n", c=4)

            def mask(i):
                return msk[:, i, :].unsqueeze(1).to_broadcast([128, 4, 128])

            for h in range(HG):
                p, n = h + 1, h - 1
                q, k = qkvc[:, h % 2, 0, :], qkvc[:, h % 2, 1, :]
                normalize(h, 0)
                normalize(h, 1)
                pool.wait_ge(nq, 2 * h + 2)
                nc.gpsimd.tensor_tensor(qkp, q[:, SEQ:], k[:, SEQ:], MUL).then_inc(dprep, 1)
                pool.wait_ge(*G("et", h + 1))
                nc.gpsimd.tensor_tensor(four(ets_nf_u), four(et), mask(1), MUL).then_inc(S["ets"], 1)
                pool.wait_ge(*G("ets", h + 1))
                nc.gpsimd.tensor_tensor(four(et), four(et), mask(0), MUL).then_inc(S["eti"], 1)
                pool.wait_ge(*G("gam", h + 1))
                pool.wait_ge(*G("kk_ps", h + 1))
                nc.gpsimd.tensor_tensor(kbg_w, kbg_w, gamB, MUL).then_inc(S["kbg"], 1)
                pool.wait_ge(*G("nf", h + 1))
                for l in range(3):
                    nc.gpsimd.tensor_tensor(four(offs[l]), four(ets_nf_u), mask(3 + l), MUL).then_inc(S["om"], 1)
                pool.wait_ge(*G("qk_ps", h + 1))
                nc.gpsimd.tensor_tensor(q[:, 0:SEQ], q[:, 0:SEQ], gamB, MUL).then_inc(S["qd"], 1)
                if p < HG:
                    for kind in range(3):
                        tail_of(p, kind)
                pool.wait_ge(kqs_ps, h + 1)
                pool.wait_ge(*G("gd", h + 1))
                v = dS[:, h % 2, :].rearrange("p (b n) -> p b n", b=NDEC)
                nc.gpsimd.tensor_tensor(v, v, gD[:, h, :].unsqueeze(2).to_broadcast([128, NDEC, 128]), MUL
                                        ).then_inc(sdec, 1)
                if p < HG:
                    decode_conv(p)
                    select_head(p)
                    square(p, 0)
                    square(p, 1)
                if n >= 0:
                    gate_out(n)
                    gate_lo(n)
            gate_out(HG - 1)
            gate_lo(HG - 1)
            sum_squares(3)
            ffn_up(1)
            sum_squares(4)

        @block.scalar
        def _(act):
            def split_hi(u, j, words, used):
                act.wait_ge(w_in[j], 16 * (u // 2 + 1) if isinstance(u, int) else u)
                if used is not None:
                    act.wait_ge(mm_done, used)
                nc.scalar.activation(wh[:, j, 0:words], stage[:, j, 0:words], ACT.Copy, scale=WS).then_inc(hi_ready, 1)

            def next_split(name, i, j, n):
                base, per = FIRST_UNIT[name], [p for a, _, p, _ in PHASES if a == name][0]
                if isinstance(i, int) and base + 2 * i + j + 2 >= UNITS:
                    return
                words = WORDS[base + 2 * i + j + 2] if isinstance(i, int) else WORDS[base + j + 2]
                act.wait_ge(w_in[j], 16 * (base // 2 + i + 2))
                act.wait_ge(mm_done, FIRST_TILE[name] + per * (2 * i + j + 1))
                nc.scalar.activation(wh[:, j, 0:words], stage[:, j, 0:words], ACT.Copy, scale=WS).then_inc(hi_ready, 1)

            def norm_tile(b, k, name=None):
                if name is None:
                    act.wait_ge(x_in, 32)
                else:
                    act.wait_ge(pm_free, FIRST_TILE[name] + k + 1)
                if b < 4:
                    nc.scalar.activation(zh[:, k, :], hT[:, k, :], ACT.Copy,
                                         scale=par[:, NORM[b] + k:NORM[b] + k + 1]).then_inc(z_hi, 1)
                if KD * b + k >= 2:
                    act.wait_ge(ssq_ready, KD * b + k - 1)
                nc.scalar.activation(sq[:, k % 2, :], hT[:, k, :], ACT.Square).then_inc(sq_ready, 1)

            def norm_factor(b):
                act.wait_ge(stat_ready, b + 1)
                c = epsc[:, 0:1] if b < 4 else epsc[:, 1:2]
                nc.scalar.activation(paired(rstd[:, :]), stat, ACT.Ln, scale=WS * WS if b < 4 else 1.0, bias=c
                                     ).then_inc(ln_done, 1)
                act.wait_ge(ln_done, b + 1)
                nc.scalar.activation(rstd[:, :], rstd[:, :], ACT.Exp, scale=-0.5).then_inc(rstd_ready, 1)

            act.preload_act_table_set("natural_log_exp_and_others")
            for u in range(2):
                split_hi(u, u, WORDS[u], None)
            act.wait_ge(consts, 1)
            for k in range(KD):
                norm_tile(0, k)
            norm_factor(0)
            for h in range(H0):
                act.wait_ge(strip_ps, h + 1)
                nc.scalar.activation(strips[:, h, :].rearrange("p (c n) -> p c n", c=2),
                                     P[:, 6:8, 0:NB // 2] if h % 2 == 0 else P[:, 2:4, 0:NB // 2], ACT.Copy
                                     ).then_inc(strip_ready, 1)
            act.wait_ge(lam_ps, 1)
            nc.scalar.activation(lame, P[:, 6, 0:2], ACT.Exp).then_inc(act_step, 1)

            for i in range(4):
                for j in range(2):
                    next_split("in0", i, j, 2)

            for c in range(4):
                act.wait_ge(vt_ps, c + 1)
                nc.scalar.activation(vtok[:, c, :], P[:, 4 + c, :], ACT.Copy).then_inc(vt_done, 1)

            for s in range(16):
                h, qt = divmod(s, 4)
                w = 128 * (qt + 1)
                act.wait_ge(nm_ready, s + 1)
                for m in range(2):
                    nc.scalar.activation(pr[:, m, 0:w], pr[:, m, 0:w], ACT.Exp, bias=nm[:, m:m + 1],
                                         accum_out=ls[:, m:m + 1]).then_inc(exp_done, 1)
                act.wait_ge(at_ps, s + 1)
                if s >= 1:
                    act.wait_ge(pv_done, s)
                nc.scalar.activation(aT[:, 0:w], P[:, 6, 0:w], ACT.Copy).then_inc(at_done, 1)
                if qt == 3:
                    act.wait_ge(pv_done, s + 1)
                    nc.scalar.activation(oT[:, h, 0:SEQ], P[:, 7, :], ACT.Copy).then_inc(o_evac, 1)
                if s == 8:
                    act.wait_ge(dp_ready, 1)
                    nc.scalar.activation(td[0:64, :], td[0:64, :], ACT.Exp, bias=tsm[0:64, 1:2],
                                         accum_out=tsm[0:64, 2:3]).then_inc(act_step, 1)
                if s == 10:
                    act.wait_ge(ad_ps, 1)
                    act.wait_ge(consts, 3)
                    nc.scalar.activation(aD, P[:, 0, 128:160], ACT.Copy)
                    for g in range(NPG):
                        v = apad[:, g * 256:(g + 1) * 256]
                        for h1 in range(H0):
                            ins = nc.scalar.activation(v[:, h1:h1 + 36 * 7 + 1:36], P[:, 0, g * 32 + h1:g * 32 + 32:4],
                                                       ACT.Copy)
                    ins.then_inc(ad_done, 1)
                if qt == 2:
                    g = h
                    act.wait_ge(pool_ps, g + 1)
                    nc.scalar.activation(paired(mh[:, g, :]), P[:, 2:4, 0:CH], ACT.Copy,
                                         scale=par[:, P_POOL + g:P_POOL + g + 1]).then_inc(m_hi, 1)
            act.wait_ge(kv_used, 2 * NDEC)
            nc.scalar.activation(td[0:32, 0:512], P[0:32, 1, :], ACT.Copy).then_inc(ad_done, 1)
            act.wait_ge(dec_o, 1)
            for h in range(H0):
                if h >= 2:
                    act.wait_ge(ostat, h - 1)
                nc.scalar.activation(sq[:, h % 2, :], oT[:, h, :], ACT.Square).then_inc(osq, 1)
            for h in range(H0):
                act.wait_ge(ostat, h + 1)
                if h >= 2:
                    act.wait_ge(yn_ready, h - 1)
                nc.scalar.activation(paired(ors[h % 2]), P[:, 4 + 2 * (h % 2):6 + 2 * (h % 2), 0:CH], ACT.Ln,
                                     bias=epsc[:, 1:2]).then_inc(oln, 1)
                act.wait_ge(oln, h + 1)
                nc.scalar.activation(ors[h % 2], ors[h % 2], ACT.Exp, scale=-0.5).then_inc(ors_ready, 1)
            for h in range(H0):
                act.wait_ge(yn_ready, h + 1)
                nc.scalar.activation(mh[:, 4 + h, :], yn[h % 2], ACT.Copy).then_inc(m_hi, 1)

            def project_out(name, b):
                for i in range(2 if name[:3] == "out" else 4):
                    for j in range(2):
                        for k in ((4 * i + 2 * j, 4 * i + 2 * j + 1) if name[:3] == "out" else (2 * i + j,)):
                            norm_tile(b, k, name)
                        next_split(name, i, j, 2)
                norm_factor(b)

            def ffn_up(layer):
                name = f"gu{layer}"
                act.preload_act_table(ACT.Silu)

                def body(i):
                    t = FIRST_TILE[name] + 4 * i
                    f = 2 * (11 * layer + i)
                    for j in range(2):
                        act.wait_ge(pm_free, t + j + 1)
                        nc.scalar.activation(gt[:, j, :], gt[:, j, :], ACT.Silu).then_inc(silu_done, 1)
                    next_split(name, i, 0, 2)
                    for j in range(2):
                        act.wait_ge(prod_done, f + j + 1)
                        nc.scalar.activation(fh[:, bass.ds(2 * i + j, 1), :], gu[:, j:j + 1, :], ACT.Copy
                                             ).then_inc(f_hi, 1)
                    next_split(name, i, 1, 2)
                with act.Fori(0, 10) as i:
                    body(i)
                body(10)
                act.preload_act_table_set("natural_log_exp_and_others")

            project_out("out0", 1)
            ffn_up(0)
            project_out("dn0", 2)

            act.wait_ge(l1_in, 16 * 5)
            nc.scalar.activation(wabh.rearrange("p k n -> p (k n)"), wabf, ACT.Copy, scale=WS).then_inc(ab_split, 1)
            nc.scalar.activation(gate[0:8, 2:3], gate[0:8, 0:1], ACT.Exp).then_inc(ab_step, 1)
            act.wait_ge(ab_step, 2)
            nc.scalar.activation(rowt[32:40, 1, :], rowt[32:40, 0, :], ACT.Exp, scale=-1.0)
            nc.scalar.activation(rowt[0:8, 1, :], rowt[0:8, 1, :], ACT.Exp).then_inc(ab_step, 1)
            act.wait_ge(ab_step, 3)
            nc.scalar.activation(rowt[0:8, 1, :], rowt[0:8, 1, :], ACT.Ln, bias=ones[0:8, 0:1]).then_inc(ab_step, 1)

            def norm_l2(h, kind):
                m = 2 * h + kind
                act.wait_ge(nstat, m + 1)
                if m >= 1:
                    act.wait_ge(nq, m)
                nc.scalar.activation(paired(rs2), stat, ACT.Ln, scale=128.0 if kind == 0 else 1.0,
                                     bias=epsc[:, 2:3] if kind == 0 else epsc[:, 1:2]).then_inc(nln, 1)
                act.wait_ge(nln, m + 1)
                nc.scalar.activation(rs2, rs2, ACT.Exp, scale=-0.5).then_inc(nrs, 1)

            def silu(h):
                act.preload_act_table(ACT.Silu)
                if h < HG:
                    act.wait_ge(convd_done, h + 1)
                    for kind in range(3):
                        act.wait_ge(conv_done, 12 * h + 4 * kind + 4)
                        x = qkvc[:, h % 2, kind, :]
                        nc.scalar.activation(x, x, ACT.Silu).then_inc(csilu, 1)
                if h >= 1:
                    act.wait_ge(pm_free, FIRST_TILE["in1"] + 4 * h)
                    z = sz[:, (h - 1) % 2, :]
                    nc.scalar.activation(z, z, ACT.Silu).then_inc(zsilu, 1)
                act.preload_act_table_set("natural_log_exp_and_others")

            def head_square(h):
                act.wait_ge(*G("o", h + 1))
                act.wait_ge(du, h + 1)
                if h >= 1:
                    act.wait_ge(o1stat, h)
                nc.scalar.activation(ssq[:, :], oh1[:, h % 2, :], ACT.Square).then_inc(o1sq, 1)

            def head_factor(h):
                act.wait_ge(o1stat, h + 1)
                if h >= 1:
                    act.wait_ge(yo, h)
                nc.scalar.activation(paired(ors1), P[:, 2:4, 0:CH], ACT.Ln, bias=epsc[:, 1:2]).then_inc(o1ln, 1)
                act.wait_ge(o1ln, h + 1)
                nc.scalar.activation(ors1, ors1, ACT.Exp, scale=-0.5).then_inc(o1rs, 1)

            def head_hi(h):
                act.wait_ge(yz, h + 1)
                nc.scalar.activation(mh1[:, h, :], yn1, ACT.Copy).then_inc(m1_hi, 1)

            next_split("in1", 0, 0, 2)
            act.wait_ge(tok_ps, 1)
            nc.scalar.activation(tokm, P[:, 6, 0:160].rearrange("p (c n) -> p c n", c=4), ACT.Copy
                                 ).then_inc(tok_done, 1)
            silu(0)

            def evac(dst, bank, ready, name, h):
                act.wait_ge(*G(ready, h + 1))
                nc.scalar.activation(dst, P[:, bank, :], ACT.Copy).then_inc(S[name], 1)

            for h in range(HG):
                p, n = h + 1, h - 1
                act.wait_ge(*G("gb_ps", h + 1))
                nc.scalar.activation(gamB, P[:, 2, :], ACT.Exp).then_inc(S["gam"], 1)
                nc.scalar.activation(gD[:, h, :], P[:, 7, 0:8], ACT.Exp).then_inc(S["gd"], 1)
                norm_l2(h, 0)
                act.wait_ge(*G("ex", h + 1))
                nc.scalar.activation(et, et, ACT.Exp).then_inc(S["et"], 1)
                nc.scalar.activation(kd4, d4, ACT.Exp).then_inc(S["kd4"], 1)
                norm_l2(h, 1)
                next_split("in1", h, 1, 2)
                act.wait_ge(*G("d", h + 1))
                evac(ets_nf_u, 6, "n_ps", "nf", h)
                act.wait_ge(*G("tk_ps", h + 1))
                act.wait_ge(*G("kd4", h + 1))
                for c in range(4):
                    ins = nc.scalar.activation(Kd[:, c * 128:(c + 1) * 128], P[:, 7, c * 128:(c + 1) * 128], ACT.Copy,
                                               scale=kd4[:, c:c + 1])
                ins.then_inc(S["kd"], 1)
                evac(d2_8, 2, "d2_ps", "d2", h)
                evac(bV, 5, "tv_ps", "bv", h)
                evac(dd, 6, "d4_ps", "d4", h)
                act.wait_ge(*G("y1", h + 1))
                evac(ddt, 7, "dt4_ps", "dt4", h)
                evac(d2_8, 3, "d8_ps", "d8", h)
                for l in range(3):
                    act.wait_ge(*G("x_ps", 3 * h + l + 1))
                    nc.scalar.activation(dt2_x, P[:, 5, :], ACT.Copy).then_inc(S["x"], 1)
                    if l == 0:
                        act.wait_ge(kqs_ps, h + 1)
                        if h >= 1:
                            act.wait_ge(outer_ps, h)
                        nc.scalar.activation(krow[0:8, :], P[0:8, 4, 32:160], ACT.Copy).then_inc(krow_s, 1)
                        if n >= 0:
                            head_factor(n)
                    if l == 1:
                        act.wait_ge(du_ps, h + 1)
                        nc.scalar.activation(urow[0:8, :], P[0:8, 4, 160:288], ACT.Copy).then_inc(urow_s, 1)
                evac(kbg_w, 4, "w_ps", "w", h)
                if p < HG:
                    next_split("in1", p, 0, 2)
                silu(p)
                if n >= 0:
                    head_hi(n)
                act.wait_ge(*G("o_ps", h + 1))
                if h >= 2:
                    act.wait_ge(yo, h - 1)
                nc.scalar.activation(oh1[:, h % 2, 0:SEQ], P[:, 7, :], ACT.Copy).then_inc(S["o"], 1)
                head_square(h)
            head_factor(HG - 1)
            head_hi(HG - 1)
            project_out("out1", 3)
            ffn_up(1)
            project_out("dn1", 4)

        @block.vector
        def _(dve):
            steps = [0]

            def link(ins):
                steps[0] += 1
                ins.then_inc(dve_step, 1)
                dve.wait_ge(dve_step, steps[0])

            def split_lo(u, j, words):
                dve.wait_ge(hi_ready, u + 1)
                nc.vector.scalar_tensor_tensor(out=wl[:, j, 0:words], in0=stage[:, j, 0:words], scalar=WS,
                                               in1=wh[:, j, 0:words], op0=MUL, op1=SUB).then_inc(lo_ready, 1)

            def next_split(name, i, j):
                base = FIRST_UNIT[name]
                if isinstance(i, int) and base + 2 * i + j + 2 >= UNITS:
                    return
                words = WORDS[base + 2 * i + j + 2] if isinstance(i, int) else WORDS[base + j + 2]
                split_lo(base + 2 * i + j + 2, j, words)

            def norm_lo(b, k):
                dve.wait_ge(z_hi, KD * b + k + 1)
                nc.vector.scalar_tensor_tensor(out=zl[:, k, :], in0=hT[:, k, :],
                                               scalar=par[:, NORM[b] + k:NORM[b] + k + 1], in1=zh[:, k, :],
                                               op0=MUL, op1=SUB).then_inc(z_lo, 1)

            for u in range(2):
                split_lo(u, u, WORDS[u])
            for k in range(KD):
                norm_lo(0, k)
            dve.wait_ge(c_in, 16 * 8)
            nc.vector.tensor_tensor(lpr[0:64, :], lamt[0:64, 0:2], lamt[0:64, 2:4], MUL).then_inc(lam_pr, 1)
            dve.wait_ge(act_step, 1)
            nc.vector.scalar_tensor_tensor(out=nlam, in0=lame[:, 1:2], scalar=-LAM0, in1=lame[:, 0:1],
                                           op0=ADD, op1=SUB).then_inc(lam_ready, 1)

            dve.wait_ge(rstd_ready, 1)
            for u in range(8):
                for j in range(2):
                    t = 2 * u + j
                    dve.wait_ge(mm_done, t + 1)
                    if t < 4:
                        nc.vector.tensor_tensor(paired(upad[:, t, 16:]), pm[j], paired(rstd[:, :]), MUL
                                                ).then_inc(pm_free, 1)
                    else:
                        nc.vector.scalar_tensor_tensor(out=paired(qkv[:, t - 4, :]), in0=pm[j],
                                                       scalar=HALF ** -0.5 if t < 8 else 1.0,
                                                       in1=paired(rstd[:, :]), op0=MUL, op1=MUL).then_inc(pm_free, 1)
                next_split("in0", u // 2, u % 2)
                if u == 1:
                    dve.wait_ge(pm_free, 4)
                    link(nc.vector.tensor_copy(ext[:, :, :, 15], upad[:, :, 16 + SEQ:]))
                    for g, w in enumerate(PW):
                        ins = nc.vector.tensor_reduce(out=extsum[:, g, :], in_=ext[:, g, :, 16 - w:], axis=AX.X, op=ADD)
                    link(ins)
                    dve.nop().then_inc(dext, 1)
            dve.wait_ge(x_in, 32)
            link(nc.vector.tensor_scalar(subw, par[:, P_SUB:P_SUB + 1], 1 - LAM0, None, MUL))
            dve.wait_ge(pm_free, 16)
            dve.wait_ge(consts, 2)
            for m in range(2):
                part = slice(64 * m, 64 * m + 64)
                for half in range(2):
                    for b in range(4):
                        at = 264 * b + 32 * half + m
                        dst = qpad[half][part, at:at + 66 * 3 + 1:66]
                        nc.vector.tensor_copy(dst, qkv[part, 0:4, SEQ + 4 * half + b])
                ins = nc.vector.tensor_tensor(qk2[part, :].rearrange("p (b h m) -> p b h m", b=NDEC, m=2)[:, :, :, m],
                                              qkv[part, 0:4, SEQ:].rearrange("p h b -> p b h"),
                                              qkv[part, 4:8, SEQ:].rearrange("p h b -> p b h"), MUL)
            link(ins)
            dve.nop().then_inc(dq_ready, 1)

            def decode_softmax(s):
                if s == 7:
                    dve.wait_ge(kv_used, NDEC)
                    nc.vector.tensor_copy(td[0:64, 0:PAST], P[0:64, 0, :])
                    link(nc.vector.tensor_copy(td[0:64, PAST:PAST + 1], P[0:64, 1, 0:1]))
                    link(nc.vector.tensor_reduce(out=tsm[0:64, 0:1], in_=td[0:64, :], axis=AX.X, op=MAX))
                    nc.vector.tensor_scalar(tsm[0:64, 1:2], tsm[0:64, 0:1], -1.0, None, MUL).then_inc(dp_ready, 1)
                elif s == 9:
                    link(nc.vector.scalar_tensor_tensor(out=tsm[0:64, 3:4], in0=sel[0:64, 1:2], scalar=nlam[0:64, :],
                                                        in1=sel[0:64, 0:1], op0=MUL, op1=ADD))
                    dve.wait_ge(act_step, 2)
                    link(nc.vector.reciprocal(tsm[0:64, 4:5], tsm[0:64, 2:3]))
                    link(nc.vector.tensor_tensor(tsm[0:64, 5:6], tsm[0:64, 4:5], tsm[0:64, 3:4], MUL))
                    nc.vector.tensor_scalar(pnew[0:64, :], ones[0:64, :], td[0:64, PAST:PAST + 1], None, MUL)
                    nc.vector.tensor_scalar(comb[0:64, :], sel[0:64, 2:34], tsm[0:64, 5:6], None, MUL
                                            ).then_inc(comb_ready, 1)

            dve.wait_ge(bias_in, 16)
            for s in range(16):
                h, qt = divmod(s, 4)
                w = 128 * (qt + 1)
                for m in range(2):
                    dve.wait_ge(s_ready, 2 * s + m + 1)
                    nc.vector.tensor_tensor_reduce(out=pr[:, m, 0:w], in0=P[:, 4 + m, 0:w], in1=biasT[:, h, 512 - w:],
                                                   scale=1.0, scalar=NEG, op0=ADD, op1=MAX,
                                                   accum_out=mx[:, m:m + 1]).then_inc(s_read, 1)
                dve.wait_ge(s_read, 2 * s + 2)
                nc.vector.tensor_scalar(nm, mx, -1.0, None, MUL).then_inc(nm_ready, 1)
                dve.wait_ge(exp_done, 2 * s + 2)
                link(nc.vector.reciprocal(rl, ls))
                link(nc.vector.tensor_scalar(pr[:, 1, 0:w], pr[:, 1, 0:w], rl[:, 1:2], nlam, MUL, MUL))
                if s >= 1:
                    dve.wait_ge(at_ps, s)
                nc.vector.scalar_tensor_tensor(out=am[:, 0:w], in0=pr[:, 0, 0:w], scalar=rl[:, 0:1],
                                               in1=pr[:, 1, 0:w], op0=MUL, op1=ADD).then_inc(a_ready, 1)
                decode_softmax(s)
                if qt == 3:
                    g = h
                    dve.wait_ge(m_hi, g + 1)
                    nc.vector.scalar_tensor_tensor(out=paired(ml[:, g, :]), in0=P[:, 2:4, 0:CH],
                                                   scalar=par[:, P_POOL + g:P_POOL + g + 1], in1=paired(mh[:, g, :]),
                                                   op0=MUL, op1=SUB).then_inc(m_lo, 1)
            dve.wait_ge(ad_done, 1)
            link(nc.vector.tensor_tensor(vn.rearrange("p (b h) -> p b h", b=NDEC),
                                         aD.rearrange("p (b h) -> p b h", b=NDEC),
                                         qkv[:, 8:12, SEQ:].rearrange("p h b -> p b h"), MUL))
            dve.wait_ge(ad_ps, 2)
            dve.wait_ge(o_evac, 4)
            for h in range(H0):
                ins = nc.vector.tensor_tensor(oT[:, h, SEQ:], P[:, 0, 33 * h:32 * h + 32:4], vn[:, h:32:4], ADD)
            ins.then_inc(dec_o, 1)
            for h in range(H0):
                dve.wait_ge(ors_ready, h + 1)
                if h >= 2:
                    dve.wait_ge(m_lo, 4 + h - 1)
                nc.vector.scalar_tensor_tensor(out=yn[h % 2], in0=oT[:, h, :], scalar=subw,
                                               in1=ors[h % 2], op0=MUL, op1=MUL).then_inc(yn_ready, 1)

            def project_out(name, b):
                pairs = name[:3] == "out"
                for i in range(2 if pairs else 4):
                    for j in range(2):
                        ks = (4 * i + 2 * j, 4 * i + 2 * j + 1) if pairs else (2 * i + j,)
                        for n, k in enumerate(ks):
                            slot = n if pairs else j
                            dve.wait_ge(mm_done, FIRST_TILE[name] + k + 1)
                            nc.vector.scalar_tensor_tensor(out=paired(hT[:, k, :]), in0=pm[slot], scalar=1 / WS,
                                                           in1=paired(hT[:, k, :]), op0=MUL, op1=ADD
                                                           ).then_inc(pm_free, 1)
                        if b < 4:
                            for k in ks:
                                norm_lo(b, k)
                        next_split(name, i, j)

            def ffn_up(layer, b):
                name = f"gu{layer}"
                dve.wait_ge(rstd_ready, b + 1)

                def body(i):
                    t = FIRST_TILE[name] + 4 * i
                    f = 2 * (11 * layer + i)
                    for part, dst in enumerate((gt, ut)):
                        for j in range(2):
                            dve.wait_ge(mm_done, t + 2 * part + j + 1)
                            if not isinstance(i, int) or i > 0:
                                dve.wait_ge(prod_done, f + j - 1)
                            nc.vector.tensor_tensor(paired(dst[:, j, :]), pm[j], paired(rstd[:, :]), MUL
                                                    ).then_inc(pm_free, 1)
                        next_split(name, i, part)
                body(0)
                with dve.Fori(1, 10) as i:
                    body(i)
                body(10)

            project_out("out0", 1)
            ffn_up(0, 1)
            project_out("dn0", 2)

            dve.wait_ge(l1_free, 1)
            dve.wait_ge(ab_split, 1)
            nc.vector.scalar_tensor_tensor(out=wabl.rearrange("p k n -> p (k n)"), in0=wabf, scalar=WS,
                                           in1=wabh.rearrange("p k n -> p (k n)"), op0=MUL, op1=SUB
                                           ).then_inc(ab_split, 1)
            dve.wait_ge(ab_ps, 1)
            dve.wait_ge(rstd_ready, 3)
            link(nc.vector.tensor_tensor(paired(rowt[0:40, 0, :]), P[0:40, 4:6, 0:CH], paired(rstd[0:40, :]), MUL))
            link(nc.vector.tensor_scalar(rowt[0:8, 2, :], rowt[0:8, 0, :], gate[0:8, 1:2], 0.0, ADD, MAX))
            link(nc.vector.tensor_scalar(rowt[0:8, 3, :], rowt[0:8, 0, :], gate[0:8, 1:2], 0.0, ADD, MIN))
            nc.vector.tensor_tensor(rowt[0:8, 1, :], rowt[0:8, 3, :], rowt[0:8, 2, :], SUB).then_inc(ab_step, 1)
            dve.wait_ge(ab_step, 4)
            link(nc.vector.tensor_tensor(rowt[0:8, 2, :], rowt[0:8, 2, :], rowt[0:8, 1, :], ADD))
            link(nc.vector.tensor_scalar(rowt[0:8, 2, :], rowt[0:8, 2, :], gate[0:8, 2:3], -1.0, MUL, MUL))
            for c in range(4):
                nc.vector.tensor_tensor_scan(rows[0:8, c * 128:(c + 1) * 128], ones[0:8, :],
                                             rowt[0:8, 2, c * 128:(c + 1) * 128], 0.0, MUL, ADD)
            nc.vector.tensor_copy(rows[0:8, SEQ:], rowt[0:8, 2, SEQ:])
            link(nc.vector.tensor_scalar(rowt[32:40, 1, :], rowt[32:40, 1, :], 1.0, None, ADD))
            nc.vector.reciprocal(rows[32:40, :], rowt[32:40, 1, :]).then_inc(rows_ready, 1)

            def leave(h, kind):
                t = FIRST_TILE["in1"] + 4 * h + kind
                acc = pm[kind % 2] if h == 0 else pm[0]
                dve.wait_ge(mm_done, t + 1)
                if kind == 3:
                    if h >= 2:
                        dve.wait_ge(yz, h - 1)
                    dst = sz[:, h % 2, :]
                else:
                    e = 3 * h + kind
                    if e >= 2:
                        dve.wait_ge(tail_done, e - 1)
                    dst = pre[:, e % 2, 3:3 + T]
                nc.vector.tensor_tensor(paired(dst), acc, paired(rstd[:, :]), MUL).then_inc(pm_free, 1)

            def convolve(h, kind, i):
                a, e = 8 * kind + h, 3 * h + kind
                x, c = pre[:, e % 2, :], qkvc[:, h % 2, kind, 0:SEQ]
                if i == 0:
                    dve.wait_ge(pm_free, FIRST_TILE["in1"] + 4 * h + kind + 1)
                    ins = nc.vector.tensor_scalar(c, x[:, 0:SEQ], cw[:, 0, a:a + 1], None, MUL)
                else:
                    dve.wait_ge(conv_done, 4 * e + i)
                    ins = nc.vector.scalar_tensor_tensor(out=c, in0=x[:, i:i + SEQ], scalar=cw[:, i, a:a + 1], in1=c,
                                                         op0=MUL, op1=ADD)
                ins.then_inc(conv_done, 1)

            leave(0, 0)
            leave(0, 1)
            next_split("in1", 0, 0)
            for i in range(4):
                convolve(0, 0, i)
            for i in range(4):
                convolve(0, 1, i)
            leave(0, 2)
            leave(0, 3)
            for i in range(4):
                convolve(0, 2, i)

            def four(ap):
                return ap.rearrange("p (c n) -> p c n", c=4)

            def mask(i):
                return msk[:, i, :].unsqueeze(1).to_broadcast([128, 4, 128])

            def add(dst, bank, src, ready, name, count, op=ADD):
                dve.wait_ge(*G(ready, count))
                if op == ADD:
                    nc.vector.tensor_tensor(dst, P[:, bank, :], src, ADD).then_inc(S[name], 1)
                else:
                    nc.vector.tensor_tensor(dst, src, P[:, bank, :], SUB).then_inc(S[name], 1)

            def head_scale(h):
                dve.wait_ge(o1rs, h + 1)
                if h >= 1:
                    dve.wait_ge(m1_lo, h)
                nc.vector.scalar_tensor_tensor(out=yn1, in0=oh1[:, h % 2, :], scalar=par[:, P_ONORM:P_ONORM + 1],
                                               in1=ors1, op0=MUL, op1=MUL).then_inc(yo, 1)

            def decode_update(h):
                dve.wait_ge(kqs_ps, h + 1)
                dve.wait_ge(krow_s, h + 1)
                kqS = P[:, 4, 0:16].rearrange("p (b m) -> p b m", m=2)
                g = gD[:, h, :]
                nc.vector.tensor_tensor(od, kqS[:, :, 0], g, MUL)
                link(nc.vector.tensor_tensor(t8, kqS[:, :, 1], g, MUL))
                link(nc.vector.tensor_tensor(t8, qkvc[:, h % 2, 2, SEQ:], t8, SUB))
                link(nc.vector.tensor_tensor(ud, t8, bD[:, h, :], MUL))
                link(nc.vector.tensor_tensor(t8, ud, P[:, 4, 16:24], MUL))
                nc.vector.tensor_tensor(oh1[:, h % 2, SEQ:], od, t8, ADD).then_inc(du, 1)

            def decode_rows(h):
                dve.wait_ge(urow_s, h + 1)
                nc.vector.tensor_tensor(um[0:8, :].rearrange("p (b n) -> p b n", b=NDEC),
                                        urow[0:8, :].unsqueeze(1).to_broadcast([8, NDEC, 128]),
                                        ident[0:8, 0:8].unsqueeze(2).to_broadcast([8, NDEC, 128]), MUL
                                        ).then_inc(um_s, 1)

            def decode_state(h):
                dve.wait_ge(outer_ps, h + 1)
                dve.wait_ge(sdec, h + 1)
                v = dS[:, h % 2, :].rearrange("p (c n) -> p c n", c=2)
                nc.vector.tensor_tensor(v, P[:, 2:4, :], v, ADD).then_inc(snew, 1)

            dve.wait_ge(tok_done, 1)
            for h in range(HG):
                p, n = h + 1, h - 1
                k, v = qkvc[:, h % 2, 1, 0:SEQ], qkvc[:, h % 2, 2, 0:SEQ]
                dve.wait_ge(*G("gd", h + 1))
                for c in range(4):
                    nc.vector.tensor_scalar(et[:, c * 128:(c + 1) * 128], P[:, 2, c * 128:(c + 1) * 128],
                                            tokm[:, c, h:h + 1], 0.0, SUB, MIN)
                nc.vector.tensor_tensor(d4, P[:, 2, :].rearrange("p (c n) -> p c n", c=4)[:, :, 127],
                                        tokm[:, :, h], SUB).then_inc(S["ex"], 1)
                nc.vector.tensor_copy(bD[:, h, :], P[:, 7, 8:16]).then_inc(S["bd"], 1)
                dve.wait_ge(nq, 2 * h + 2)
                nc.vector.tensor_tensor(kbg_w, P[:, 3, :], k, MUL).then_inc(S["kb"], 1)
                dve.wait_ge(csilu, 3 * h + 3)
                nc.vector.tensor_tensor(v, P[:, 3, :], v, MUL).then_inc(S["vb"], 1)
                next_split("in1", h, 1)
                dve.wait_ge(*G("ets", h + 1))
                dve.wait_ge(*G("kk_ps", h + 1))
                nc.vector.tensor_tensor(nt_z, P[:, 4, :], ets_nf_u, MUL).then_inc(S["nt"], 1)
                dve.wait_ge(*G("nt", h + 1))
                nc.vector.tensor_tensor(four(ddt), four(nt_z), mask(2), MUL).then_inc(S["dt"], 1)
                dve.wait_ge(*G("eti", h + 1))
                dve.wait_ge(*G("qk_ps", h + 1))
                nc.vector.tensor_tensor(At, P[:, 5, :], et, MUL).then_inc(S["at"], 1)
                if p < HG:
                    leave(p, 0)
                dve.wait_ge(*G("n_ps", h + 1))
                nc.vector.tensor_tensor(four(dd), four(P[:, 6, :]), mask(2), MUL).then_inc(S["d"], 1)
                dve.wait_ge(*G("dt", h + 1))
                nc.vector.scalar_tensor_tensor(out=four(ya), in0=four(ddt), scalar=-1.0,
                                               in1=ident[:, :].unsqueeze(1).to_broadcast([128, 4, 128]),
                                               op0=MUL, op1=ADD).then_inc(S["y1"], 1)
                if p < HG:
                    convolve(p, 0, 0)
                dve.wait_ge(*G("dt2_ps", h + 1))
                nc.vector.tensor_copy(dt2_x, P[:, 3, :]).then_inc(S["dt2"], 1)
                dve.wait_ge(*G("tkb_ps", h + 1))
                nc.vector.tensor_copy(Kp, P[:, 4, :]).then_inc(S["kp"], 1)
                if p < HG:
                    convolve(p, 0, 1)
                    convolve(p, 0, 2)
                dve.wait_ge(*G("y1", h + 1))
                add(yb, 2, ya, "y2_ps", "y2", h + 1)
                if p < HG:
                    convolve(p, 0, 3)
                    leave(p, 1)
                dve.wait_ge(*G("y2", h + 1))
                add(ya, 4, yb, "y3_ps", "y3", h + 1)
                dve.wait_ge(*G("y3", h + 1))
                if p < HG:
                    convolve(p, 1, 0)
                    convolve(p, 1, 1)
                add(yb, 6, ya, "y4_ps", "xt", h + 1)
                if p < HG:
                    convolve(p, 1, 2)
                for l in range(3):
                    src, dst = (yb, ya) if l % 2 == 0 else (ya, yb)
                    dve.wait_ge(*G("z_ps", 3 * h + l + 1))
                    nc.vector.tensor_copy(nt_z, P[:, 7, :]).then_inc(S["z"], 1)
                    if p < HG and l == 0:
                        convolve(p, 1, 3)
                    dve.wait_ge(*G("xt", 4 * h + l + 1))
                    add(dst, 6, src, "v_ps", "xt", 3 * h + l + 1, SUB)
                    if l == 0:
                        decode_update(h)
                        if p < HG:
                            leave(p, 2)
                    elif l == 1:
                        decode_rows(h)
                    else:
                        decode_state(h)
                        if n >= 0:
                            head_scale(n)
                dve.wait_ge(*G("u_ps", h + 1))
                nc.vector.tensor_copy(ets_nf_u, P[:, 5, :]).then_inc(S["u"], 1)
                if p < HG:
                    next_split("in1", p, 0)
                for c in range(4):
                    cc = slice(c * 128, (c + 1) * 128)
                    if c > 0:
                        dve.wait_ge(*G("ws_ps", 3 * h + c))
                        dve.wait_ge(*G("u", 4 * h + c))
                        nc.vector.tensor_tensor(ets_nf_u[:, cc], ets_nf_u[:, cc], P[:, 2, cc], SUB).then_inc(S["u"], 1)
                    dve.wait_ge(*G("ds_ps", 4 * h + c + 1))
                    dst = sall[:, h, :] if c == 3 else sping[:, c % 2, :]
                    if c == 0:
                        nc.vector.tensor_copy(dst, P[:, 3, cc]).then_inc(S["s"], 1)
                    else:
                        dve.wait_ge(*G("s", 4 * h + c))
                        nc.vector.scalar_tensor_tensor(out=dst, in0=sping[:, (c - 1) % 2, :],
                                                       scalar=gamB[:, c * 128 + 127:c * 128 + 128], in1=P[:, 3, cc],
                                                       op0=MUL, op1=ADD).then_inc(S["s"], 1)
                    if p < HG:
                        convolve(p, 2, c)
                if p < HG:
                    leave(p, 3)
            head_scale(HG - 1)
            project_out("out1", 3)
            ffn_up(1, 3)
            project_out("dn1", 4)

            dve.wait_ge(rstd_ready, 5)
            for k in range(KD):
                if k >= 2:
                    dve.wait_ge(y_out[k % 2], 16 * (k // 2))
                nc.vector.scalar_tensor_tensor(out=yf[:, k % 2, :], in0=hT[:, k, :],
                                               scalar=par[:, P_FIN + k:P_FIN + k + 1], in1=rstd[:, :],
                                               op0=MUL, op1=MUL).then_inc(y_ready, 1)

        @block.tensor
        def _(pe):
            def product(j, wslot, woff, xh, xl, nk, stride, k0=0):
                for k in range(nk):
                    o = woff + k * stride
                    for w, x in ((wh, xh), (wh, xl), (wl, xh)):
                        for c in range(2):
                            mm = nc.tensor.matmul(pm[j][:, c, :], w[:, wslot, o:o + 128],
                                                  x[:, k, c * CH:(c + 1) * CH],
                                                  start=(k == 0 and w is wh and x is xh),
                                                  stop=(k == nk - 1 and w is wl))
                return mm

            def unit(name, u, i, j, xh, xl, ready=None):
                base, per, words = FIRST_UNIT[name], *[(p, w) for a, _, p, w in PHASES if a == name][0]
                pe.wait_ge(hi_ready, base + 2 * i + j + 1)
                pe.wait_ge(lo_ready, base + 2 * i + j + 1)
                nk = KF if per == 1 else KD
                for n in range(per):
                    slot = n if per == 2 else j
                    t = FIRST_TILE[name] + per * (2 * i + j) + n
                    if not isinstance(t, int) or t >= 2:
                        pe.wait_ge(pm_free, t - 1)
                    product(slot, j, 128 * n, xh, xl, nk, words // nk).then_inc(mm_done, 1)

            def phase(name, xh, xl):
                n = [c for a, c, _, _ in PHASES if a == name][0] // 2
                first = 1 if FIRST_UNIT[name] == 0 else 0
                for i in range(first):
                    for j in range(2):
                        unit(name, None, i, j, xh, xl)
                with pe.Fori(first, n) as i:
                    for j in range(2):
                        unit(name, None, i, j, xh, xl)

            def statistics(b):
                pe.wait_ge(ssq_ready, KD * (b + 1))
                if b > 0:
                    pe.wait_ge(rstd_ready, b)
                for c in range(2):
                    mm = nc.tensor.matmul(stat[:, c, :], onesD[:, :], ssq[:, c * CH:(c + 1) * CH], start=True, stop=True)
                mm.then_inc(stat_ready, 1)

            pe.wait_ge(consts, 1)
            statistics(0)
            pe.wait_ge(tabB_ready, 1)
            pe.wait_ge(c_in, 16 * 8)
            for h in range(H0):
                if h >= 2:
                    pe.wait_ge(strip_ready, h - 1)
                for c in range(2):
                    mm = nc.tensor.matmul(P[:, (6 if h % 2 == 0 else 2) + c, 0:NB // 2], tabB[0:33, h, :],
                                          oh[0:33, c * NB // 2:(c + 1) * NB // 2], start=True, stop=True)
                mm.then_inc(strip_ps, 1)
            pe.wait_ge(lam_pr, 1)
            pe.wait_ge(strip_ready, H0)
            nc.tensor.matmul(P[:, 6, 0:2], ones[0:64, :], lpr[0:64, :], start=True, stop=True).then_inc(lam_ps, 1)

            pe.wait_ge(z_hi, KD)
            pe.wait_ge(z_lo, KD)
            phase("in0", zh, zl)

            pe.wait_ge(pm_free, 16)
            pe.wait_ge(rstd_ready, 1)
            pe.wait_ge(lam_ready, 1)
            for c in range(4):
                for h in range(H0):
                    mm = nc.tensor.transpose(P[:, 4 + c, h * 128:(h + 1) * 128], qkv[:, 8 + h, c * 128:(c + 1) * 128],
                                             ident[:, :])
                mm.then_inc(vt_ps, 1)
            pe.wait_ge(dq_ready, 1)
            nc.tensor.matmul(P[0:64, 0, :], tab64[0:33, :], oh[0:33, NB:NB + PAST], start=True, stop=False)
            nc.tensor.matmul(P[0:64, 1, 0:1], tab64[0:33, :], oh[0:33, NB + PAST:NB + PAST + 1], start=True, stop=False)
            nc.tensor.matmul(P[0:64, 1, 0:1], qk2, ones[:, 0:1], start=False, stop=True)

            def decode_scores(i):
                b, h = bh(i)
                if h == 0:
                    pe.wait_ge(kv_in[b % NKV], 16 * NPG * (b // NKV + 1))
                mm = nc.tensor.matmul(P[0:64, 0, :], qpad[i // 16][:, i % 16 * 64:i % 16 * 64 + 64],
                                      kv[:, b % NKV, :, h * 128:(h + 1) * 128], start=False, stop=(i == 31))
                if h == 3:
                    mm.then_inc(kv_used, 1)

            def decode_probs():
                pe.wait_ge(comb_ready, 1)
                for g in range(NPG + 1):
                    lhs = td[0:64, g * 128:(g + 1) * 128] if g < NPG else pnew[0:64, :]
                    mm = nc.tensor.matmul(P[:, 0, g * 32:(g + 1) * 32], lhs, comb[0:64, :], start=True, stop=True)
                mm.then_inc(ad_ps, 1)

            def decode_values(b):
                n = NDEC + b
                if b == 0:
                    pe.wait_ge(ad_done, 1)
                pe.wait_ge(kv_in[n % NKV], 16 * NPG * (n // NKV + 1))
                for g in range(NPG):
                    mm = nc.tensor.matmul(P[0:32, 1, :], apad[:, g * 256 + b * 32:g * 256 + b * 32 + 32],
                                          kv[:, n % NKV, g, :], start=(b == 0 and g == 0),
                                          stop=(b == NDEC - 1 and g == NPG - 1))
                mm.then_inc(kv_used, 1)

            def attend(s):
                h, qt = divmod(s, 4)
                pe.wait_ge(at_done, s + 1)
                if s >= 4 and qt == 0:
                    pe.wait_ge(o_evac, h)
                for c in range(qt + 1):
                    mm = nc.tensor.matmul(P[:, 7, qt * 128:(qt + 1) * 128], vtok[:, c, h * 128:(h + 1) * 128],
                                          aT[:, c * 128:(c + 1) * 128], start=(c == 0), stop=(c == qt))
                mm.then_inc(pv_done, 1)

            for s in range(16):
                h, qt = divmod(s, 4)
                w = 128 * (qt + 1)
                if s == 0:
                    pe.wait_ge(vt_done, 4)
                for m in range(2):
                    if s >= 1:
                        pe.wait_ge(s_read, 2 * s - 1 + m)
                    part = slice(64 * m, 64 * m + 64)
                    nc.tensor.matmul(P[:, 4 + m, 0:w], qkv[part, h, qt * 128:(qt + 1) * 128], qkv[part, 4 + h, 0:w],
                                     start=True, stop=True).then_inc(s_ready, 1)
                if s < NDEC:
                    decode_scores(4 * s)
                    decode_scores(4 * s + 1)
                elif s == 10:
                    decode_probs()
                elif s > 10:
                    decode_values((0, 1, 2, 4, 6)[s - 11])
                if s >= 1:
                    attend(s - 1)
                if qt == 2:
                    pe.wait_ge(d_ready, h + 1)
                    if h >= 1:
                        pe.wait_ge(m_lo, h)
                    for c in range(2):
                        mm = nc.tensor.matmul(P[:, 2 + c, 0:CH], poolw[:, h, :], dT[:, c * CH:(c + 1) * CH],
                                              start=True, stop=True)
                    mm.then_inc(pool_ps, 1)
                if s < NDEC:
                    decode_scores(4 * s + 2)
                    decode_scores(4 * s + 3)
                elif s > 12:
                    decode_values((3, 5, 7)[s - 13])
                pe.wait_ge(a_ready, s + 1)
                if s >= 1:
                    pe.wait_ge(at_done, s)
                for c in range(qt + 1):
                    mm = nc.tensor.transpose(P[:, 6, c * 128:(c + 1) * 128], am[:, c * 128:(c + 1) * 128], ident[:, :])
                mm.then_inc(at_ps, 1)
            attend(15)

            pe.wait_ge(ad_done, 2)
            for h in range(H0):
                mm = nc.tensor.transpose(P[:, 0, h * 32:(h + 1) * 32], td[0:32, h * 128:(h + 1) * 128],
                                         ident[0:32, 0:32])
            mm.then_inc(ad_ps, 1)
            pe.wait_ge(m_lo, 4)
            for h in range(H0):
                pe.wait_ge(osq, h + 1)
                if h >= 2:
                    pe.wait_ge(oln, h - 1)
                for c in range(2):
                    mm = nc.tensor.matmul(P[:, 4 + 2 * (h % 2) + c, 0:CH], onesH[:, :],
                                          sq[:, h % 2, c * CH:(c + 1) * CH], start=True, stop=True)
                mm.then_inc(ostat, 1)
            pe.wait_ge(m_hi, 8)
            pe.wait_ge(m_lo, 8)
            pe.wait_ge(oln, 4)
            phase("out0", mh, ml)
            statistics(1)
            pe.wait_ge(z_hi, 2 * KD)
            pe.wait_ge(z_lo, 2 * KD)
            phase("gu0", zh, zl)
            pe.wait_ge(f_lo, KF)
            phase("dn0", fh, fl)
            statistics(2)
            pe.wait_ge(z_hi, 3 * KD)
            pe.wait_ge(z_lo, 3 * KD)

            pe.wait_ge(ab_split, 2)
            pe.wait_ge(rstd_ready, 3)
            for k in range(KD):
                for w, x in ((wabh, zh), (wabh, zl), (wabl, zh)):
                    for c in range(2):
                        mm = nc.tensor.matmul(P[0:40, 4 + c, 0:CH], w[:, k, :], x[:, k, c * CH:(c + 1) * CH],
                                              start=(k == 0 and w is wabh and x is zh),
                                              stop=(k == KD - 1 and w is wabl))
            mm.then_inc(ab_ps, 1)

            for j in range(2):
                unit("in1", None, 0, j, zh, zl)
            pe.wait_ge(rows_ready, 1)
            for c in range(4):
                mm = nc.tensor.transpose(P[:, 6, 40 * c:40 * c + 40], rows[0:40, c * 128:(c + 1) * 128],
                                         ident[0:40, 0:40])
            mm.then_inc(tok_ps, 1)

            def stat_l2(h, kind):
                pe.wait_ge(nsq, 2 * h + kind + 1)
                if kind == 1:
                    pe.wait_ge(nln, 2 * h + 1)
                for c in range(2):
                    mm = nc.tensor.matmul(stat[:, c, :], ones[:, :], sq[:, kind, c * CH:(c + 1) * CH],
                                          start=True, stop=True)
                mm.then_inc(nstat, 1)

            def stat_head(h):
                pe.wait_ge(o1sq, h + 1)
                for c in range(2):
                    mm = nc.tensor.matmul(P[:, 2 + c, 0:CH], onesH[:, :], ssq[:, c * CH:(c + 1) * CH],
                                          start=True, stop=True)
                mm.then_inc(o1stat, 1)

            def project_part(h, part):
                kind, k = divmod(part, KD)
                u, n = 2 * h + kind // 2, kind % 2
                if k == 0:
                    pe.wait_ge(hi_ready, FIRST_UNIT["in1"] + u + 1)
                    pe.wait_ge(lo_ready, FIRST_UNIT["in1"] + u + 1)
                    pe.wait_ge(pm_free, FIRST_TILE["in1"] + 4 * h + kind)
                o = 128 * n + 256 * k
                for w, x in ((wh, zh), (wh, zl), (wl, zh)):
                    for c in range(2):
                        mm = nc.tensor.matmul(pm[0][:, c, :], w[:, u % 2, o:o + 128], x[:, k, c * CH:(c + 1) * CH],
                                              start=(k == 0 and w is wh and x is zh), stop=(k == KD - 1 and w is wl))
                if k == KD - 1:
                    mm.then_inc(mm_done, 1)

            def chunks(bank, lhs, rhs, name):
                for c in range(4):
                    cc = slice(c * 128, (c + 1) * 128)
                    mm = nc.tensor.matmul(P[:, bank, cc], lhs[:, cc], rhs[:, cc], start=True, stop=True)
                mm.then_inc(S[name], 1)

            def turn(bank, src, name):
                for c in range(4):
                    cc = slice(c * 128, (c + 1) * 128)
                    mm = nc.tensor.transpose(P[:, bank, cc], src[:, cc], ident[:, :])
                mm.then_inc(S[name], 1)

            def ready(h, *names):
                for n in names:
                    pe.wait_ge(*G(n, h + 1))

            pe.wait_ge(pm_free, FIRST_TILE["in1"] + 4)
            pe.wait_ge(tok_done, 1)
            for h in range(HG):
                q, k, v = (qkvc[:, h % 2, i, 0:SEQ] for i in range(3))
                done = [0]

                def fill(n):
                    if h + 1 < HG:
                        for part in range(done[0], done[0] + n):
                            project_part(h + 1, part)
                        done[0] += n

                ready(h, "selb")
                if h >= 1:
                    pe.wait_ge(*G("s", 4 * h))
                    ready(h - 1, "o")
                nc.tensor.matmul(P[:, 2, :], selb[0:40, h % 2, 0, :], rows[0:40, 0:SEQ], start=True, stop=True)
                nc.tensor.matmul(P[:, 3, :], selb[0:40, h % 2, 1, :], rows[0:40, 0:SEQ], start=True, stop=True)
                nc.tensor.matmul(P[:, 7, 0:8], selb[0:40, h % 2, 0, :], rows[0:40, SEQ:], start=True, stop=True)
                nc.tensor.matmul(P[:, 7, 8:16], selb[0:40, h % 2, 1, :], rows[0:40, SEQ:], start=True, stop=True
                                 ).then_inc(S["gb_ps"], 1)
                fill(2)
                stat_l2(h, 0)
                fill(1)
                stat_l2(h, 1)
                fill(2)
                pe.wait_ge(nq, 2 * h + 2)
                chunks(5, k, q, "qk_ps")
                ready(h, "kb")
                chunks(4, k, kbg_w, "kk_ps")
                ready(h, "gd", "bd")
                turn(7, k, "tk_ps")
                fill(3)
                ready(h, "nt")
                turn(6, nt_z, "n_ps")
                fill(2)
                ready(h, "kbg")
                turn(4, kbg_w, "tkb_ps")
                fill(1)
                ready(h, "vb", "at")
                turn(5, v, "tv_ps")
                fill(2)
                ready(h, "d", "dt", "gam")
                chunks(2, ddt, dd, "d2_ps")
                chunks(3, dd, ddt, "dt2_ps")
                fill(3)
                ready(h, "d2", "dt2", "nf", "kd")
                chunks(6, dt2_x, d2_8, "d4_ps")
                chunks(7, d2_8, dt2_x, "dt4_ps")
                ready(h, "y1")
                chunks(2, d2_8, ya, "y2_ps")
                fill(3)
                ready(h, "d4", "dt4", "y2", "kp")
                chunks(3, ddt, dd, "d8_ps")
                chunks(4, dd, yb, "y3_ps")
                fill(2)
                ready(h, "d8", "y3")
                chunks(6, d2_8, ya, "y4_ps")
                pe.wait_ge(st_in[h % 2], 16 * (h // 2 + 1))
                pe.wait_ge(dprep, h + 1)
                for b in range(NDEC):
                    nc.tensor.matmul(P[:, 4, 2 * b:2 * b + 2], dS[:, h % 2, b * 128:(b + 1) * 128],
                                     qkvc[:, h % 2, 0:2, SEQ + b], start=True, stop=True)
                nc.tensor.matmul(P[:, 4, 16:24], ones[:, :], qkp, start=True, stop=True)
                nc.tensor.transpose(P[0:8, 4, 32:160], qkvc[:, h % 2, 1, SEQ:], ident[:, :]).then_inc(kqs_ps, 1)
                ready(h, "bv")
                for l in range(3):
                    src = yb if l % 2 == 0 else ya
                    pe.wait_ge(*G("xt", 4 * h + l + 1))
                    turn(5, src, "x_ps")
                    pe.wait_ge(*G("om", 3 * h + l + 1))
                    chunks(7, offs[l], src, "z_ps")
                    fill(1)
                    if l == 0 and h >= 1:
                        stat_head(h - 1)
                    if l == 2:
                        if h >= 1:
                            pe.wait_ge(o1ln, h)
                        pe.wait_ge(um_s, h + 1)
                        for c in range(2):
                            mm = nc.tensor.matmul(P[:, 2 + c, :], krow[0:8, :], um[0:8, c * 512:(c + 1) * 512],
                                                  start=True, stop=True)
                        mm.then_inc(outer_ps, 1)
                    pe.wait_ge(*G("x", 3 * h + l + 1))
                    pe.wait_ge(*G("z", 3 * h + l + 1))
                    chunks(6, dt2_x, nt_z, "v_ps")
                    fill(2 if l == 0 else 1)
                    if l == 1:
                        pe.wait_ge(du, h + 1)
                        pe.wait_ge(krow_s, h + 1)
                        nc.tensor.transpose(P[0:8, 4, 160:288], ud, ident[:, :]).then_inc(du_ps, 1)
                pe.wait_ge(*G("xt", 4 * h + 4))
                pe.wait_ge(urow_s, h + 1)
                chunks(4, Kp, ya, "w_ps")
                chunks(5, ya, bV, "u_ps")
                fill(1)
                ready(h, "w", "qd")
                pe.wait_ge(snew, h + 1)
                for c in range(4):
                    cc = slice(c * 128, (c + 1) * 128)
                    s_prev = sping[:, (c - 1) % 2, :]
                    if c > 0:
                        pe.wait_ge(*G("s", 4 * h + c))
                        nc.tensor.matmul(P[:, 2, cc], kbg_w[:, cc], s_prev, start=True, stop=True
                                         ).then_inc(S["ws_ps"], 1)
                        nc.tensor.matmul(P[:, 7, cc], s_prev, q[:, cc], start=True, stop=False)
                    pe.wait_ge(*G("u", 4 * h + c + 1))
                    nc.tensor.matmul(P[:, 3, cc], Kd[:, cc], ets_nf_u[:, cc], start=True, stop=True
                                     ).then_inc(S["ds_ps"], 1)
                    mm = nc.tensor.matmul(P[:, 7, cc], ets_nf_u[:, cc], At[:, cc], start=(c == 0), stop=True)
                mm.then_inc(S["o_ps"], 1)
                fill(3)

            pe.wait_ge(*G("s", 4 * HG))
            stat_head(HG - 1)
            pe.wait_ge(m1_hi, HG)
            pe.wait_ge(m1_lo, HG)
            phase("out1", mh1, ml1)
            statistics(3)
            pe.wait_ge(z_hi, 4 * KD)
            pe.wait_ge(z_lo, 4 * KD)
            phase("gu1", zh, zl)
            pe.wait_ge(f_lo, 2 * KF)
            phase("dn1", fh, fl)
            statistics(4)


NORM = (P_MIX, P_FFN, P_MIX + 8, P_FFN + 8)


def kernel(**inputs):
    import numpy as np
    import concourse.bacc as bacc
    from concourse.bass_utils import run_bass_kernel_spmd
    a = {k: np.asarray(v) for k, v in inputs.items()}
    f = np.float32

    def units(w, width):
        k, n = w.shape
        return np.ascontiguousarray(w.reshape(k // 128, 128, n // width, width).transpose(2, 1, 0, 3)
                                    ).reshape(n // width, 128, -1)

    def rows(v):
        return v.reshape(-1, 128).T

    def gate_up(w):
        g, u = units(w[:, :DFF], 256), units(w[:, DFF:], 256)
        return np.stack([g, u], 1).reshape(22, 128, -1)

    x = np.concatenate([a["x_prompt"][0], a["x_sample"][:, 0]])
    pool_pages = a["cache_k"].shape[0]
    n = np.arange(0, PAST + 1)
    large = 16 + (np.log(np.maximum(n, 1).astype(f) / f(16)) / f(np.log(8.0)) * f(16)).astype(np.int32)
    bucket = np.where(n < 16, n, np.minimum(large, 31))
    onehot = np.zeros((33, NB + PAST + 1), f)
    for m in range(NB):
        d = SEQ - 1 - m
        onehot[bucket[d] if d >= 0 else 32, m] = 1
    for t in range(PAST + 1):
        onehot[bucket[PAST - t], NB + t] = 1
    sel64 = np.zeros((64, 34), f)
    for r in range(64):
        sel64[r, r % 2] = 1
        sel64[r, 2 + r // 2] = 1
    p, n = np.arange(128)[:, None], np.arange(128)[None]
    masks = np.stack([p <= n, p < n, p // 16 == n // 16] +
                     [(p // (2 * s) == n // (2 * s)) & (p // s > n // s) for s in (16, 32, 64)], 1).astype(f)
    wab = np.zeros((128, KD, 40), f)
    w2 = a["w_in_odd"][0][:, 4096:].reshape(KD, 128, 16).transpose(1, 0, 2)
    wab[:, :, 0:8], wab[:, :, 32:40] = w2[:, :, 0:8], w2[:, :, 8:16]
    arrays = {
        "xT": np.ascontiguousarray(x.T.reshape(KD, 128, T).transpose(1, 0, 2)),
        "w_in0": units(a["w_in_even"][0], 256), "w_out0": units(a["w_out_even"][0], 256),
        "w_gu": np.stack([gate_up(w) for w in a["w_gate_up"]]),
        "w_dn": np.stack([units(w, 128) for w in a["w_down"]]),
        "w_in1": units(a["w_in_odd"][0][:, :4096].reshape(D, 4, HG, 128).transpose(0, 2, 1, 3).reshape(D, 4096), 256), "w_out1": units(a["w_out_odd"][0], 256),
        "params": np.ascontiguousarray(np.concatenate(
            [rows(a[k]) for k in ("norm_mix", "norm_ffn", "norm_final", "pool_scale", "subln_w", "o_norm")], 1)),
        "convw": np.ascontiguousarray(rows(a["conv_w"][0])),
        "wab": wab,
        "gates": np.ascontiguousarray(np.concatenate([a["a_log"], a["dt_bias"]]).T),
        "cache_k": np.ascontiguousarray(a["cache_k"][:, 0].transpose(0, 3, 2, 1)).reshape(pool_pages, 128, 512),
        "cache_v": np.ascontiguousarray(a["cache_v"][:, 0]).reshape(pool_pages, 128, 512),
        "pages": a["page_table"].reshape(1, -1),
        "pool_w": np.ascontiguousarray(a["pool_w"][0].transpose(1, 0, 2)),
        "pool_state": np.ascontiguousarray(a["state_pool"][0].reshape(NDEC, 15, 4, 128).transpose(3, 2, 0, 1)),
        "conv_state": np.ascontiguousarray(a["state_conv"][0].reshape(NDEC, 3, 24, 128).transpose(3, 2, 0, 1)),
        "delta_state": np.ascontiguousarray(a["state_delta"][0].transpose(1, 2, 0, 3)).reshape(HG, 128, NDEC * 128),
        "rel_tab": np.concatenate([a["rel_bias"], np.full((1, 4), NEG, f)]),
        "onehot": onehot,
        "lam_vec": np.ascontiguousarray(np.stack([a[k][0] for k in ("lambda_q1", "lambda_q2", "lambda_k1",
                                                                   "lambda_k2")], 1)),
        "sel64": sel64,
        "invcnt": np.ascontiguousarray(np.broadcast_to((1 / np.arange(1, 16)).astype(f), (128, 15))),
        "masks": np.ascontiguousarray(masks),
    }
    outs = {"o_y": (128, KD, T), "o_k": (128, 4, T), "o_v": (128, 4, T), "o_pp": (128, 4, 15),
            "o_ps": (128, 4, NDEC, 16), "o_ct": (128, 24, 11), "o_cs": (128, 24, NDEC, 4),
            "o_dp": (128, HG, 128), "o_ds": (HG, 128, NDEC * 128)}
    nc = bacc.Bacc("TRN2", target_bir_lowering=False, num_devices=1)
    aps = [nc.dram_tensor(k, v.shape, mybir.dt.from_np(v.dtype), kind="ExternalInput").ap() for k, v in arrays.items()]
    aps += [nc.dram_tensor(k, s, mybir.dt.float32, kind="ExternalOutput").ap() for k, s in outs.items()]
    hybrid_trunk(nc, *aps)
    r = run_bass_kernel_spmd(nc, [arrays], core_ids=[0]).results[0]
    feat = {k: r[k].transpose(2, 1, 0).reshape(T, -1) for k in ("o_y", "o_k", "o_v")}
    k, v = (feat[n].reshape(T, 4, 128) for n in ("o_k", "o_v"))
    return (feat["o_y"][None, :SEQ], feat["o_y"][SEQ:, None], k[None, None, :SEQ], v[None, None, :SEQ],
            k[SEQ:, None, None], v[SEQ:, None, None],
            r["o_pp"].transpose(2, 1, 0).reshape(1, 1, 15, 512),
            r["o_ps"][:, :, :, 1:].transpose(2, 3, 1, 0).reshape(1, NDEC, 15, 512),
            r["o_ct"][:, :, :3].transpose(2, 1, 0).reshape(1, 1, 3, 3072),
            r["o_cs"][:, :, :, 1:].transpose(2, 3, 1, 0).reshape(1, NDEC, 3, 3072),
            r["o_dp"].transpose(1, 0, 2)[None, None],
            r["o_ds"].reshape(HG, 128, NDEC, 128).transpose(2, 0, 1, 3)[None])
```

```python
import concourse.bass as bass
from concourse import mybir
from contextlib import ExitStack

D, SEQ, NDEC, PAST, PAGE = 1024, 512, 8, 512, 128
T = SEQ + NDEC
CH = T // 2
KD = D // 128
H0, HALF = 4, 64
PW = (2, 4, 8, 16)
DFF = 2816
KF = DFF // 128
HG = 8
OUT1_CALLS = (4, 5, 8, 10, 12, 15, 16)
NPG = PAST // PAGE
WS = 64.0
EPS = 1e-6
LAM0 = 0.2
NEG = -1e30
NB = 640
SKEW = NB + 1

UQ = KD * 256 // 4
UNIT = KF * 128
PHASES = (("in0", 8, 2, KD * 256), ("out0", 4, 2, KD * 256), ("gu0", 22, 2, KD * 256), ("dn0", 8, 1, UNIT),
          ("in1", 16, 2, KD * 256), ("out1", 4, 2, KD * 256), ("gu1", 22, 2, KD * 256), ("dn1", 8, 1, UNIT))
FIRST_UNIT, FIRST_TILE, WORDS = {}, {}, []
_u = _t = 0
for _n, _c, _j, _w in PHASES:
    FIRST_UNIT[_n], FIRST_TILE[_n] = _u, _t
    _u, _t = _u + _c, _t + _c * _j
    WORDS += [_w] * _c
UNITS = _u
HEAD_TILES = {
    "pe": ["gb_ps", "qk_ps", "kk_ps", "tk_ps", "n_ps", "tkb_ps", "d2_ps", "dt2_ps", "d4_ps", "dt4_ps", "y2_ps", "tv_ps",
           "d8_ps", "y3_ps", "y4_ps"] + ["x_ps", "z_ps", "v_ps"] * 3 + ["w_ps", "u_ps", "ds_ps"] +
          ["ws_ps", "ds_ps"] * 3 + ["o_ps"],
    "act": ["gam", "gd", "et", "kd4", "nf", "kd", "d2", "d4", "dt4", "bv", "d8", "x", "x", "x", "w", "o"],
    "dve": ["ex", "bd", "kb", "nt", "dt", "at", "d", "y1", "dt2", "kp", "y2", "y3", "xt"] + ["z", "xt"] * 3 +
           ["u", "s"] * 4,
    "pool": ["selb", "ets", "eti", "kbg", "om", "om", "om", "qd"],
}
P_MIX, P_FFN, P_FIN, P_POOL, P_SUB, P_ONORM, P_N = 0, 16, 32, 40, 44, 45, 46


def hybrid_trunk(nc, xT, w_in0, w_out0, w_gu, w_dn, w_in1, w_out1, params, convw, wab, gates, cache_k, cache_v, pages,
                 pool_w, pool_state, conv_state, delta_state, rel_tab, onehot, lam_vec, sel64, invcnt, masks,
                 o_y, o_k, o_v, o_pp, o_ps, o_ct, o_cs, o_dp, o_ds):
    f32, f16, i32 = mybir.dt.float32, mybir.dt.float16, mybir.dt.int32
    ALU, ACT, AX = mybir.AluOpType, mybir.ActivationFunctionType, mybir.AxisListType
    MUL, ADD, SUB, MAX, MIN = ALU.mult, ALU.add, ALU.subtract, ALU.max, ALU.min

    ctx = ExitStack()
    with ctx:
        def sb(name, shape, dt=f32):
            return ctx.enter_context(nc.sbuf_tensor(name, shape, dt))

        def sem(name):
            return ctx.enter_context(nc.semaphore(name))

        hT = sb("hT", [128, KD, T])
        zh = sb("zh", [128, KD, T], f16)
        zl = sb("zl", [128, KD, T], f16)
        stage = sb("stage", [128, 2, UNIT])
        wh = sb("wh", [128, 2, UNIT], f16)
        wl = sb("wl", [128, 2, UNIT], f16)
        rstd = sb("rstd", [128, T])
        sq = sb("sq", [128, 2, T])
        ssq = sb("ssq", [128, T])
        par = sb("par", [128, P_N])
        ident = sb("ident", [128, 128])
        ones = sb("ones", [128, 128])
        onesD = sb("onesD", [128, 128])
        onesH = sb("onesH", [128, 128])
        epsc = sb("epsc", [128, 3])
        pt = sb("pt", [1, NDEC * NPG], i32)
        ARENA = 30936
        arena = sb("arena", [128, ARENA])
        P = ctx.enter_context(nc.psum_tensor("P", [128, 8, 512], f32))
        pm = [P[:, 2 * j:2 * j + 2, 0:CH] for j in range(2)]
        stat = P[:, 4:6, 0:CH]

        def carver():
            at = [0]

            def take(n, dt=f32):
                n32 = n if dt == f32 else n // 2
                at[0] += n32
                assert at[0] <= ARENA, at[0]
                v = arena[:, at[0] - n32:at[0]]
                return v if dt == f32 else v.bitcast(dt)
            return take

        a0 = carver()
        qkv = a0(12 * T).rearrange("p (a t) -> p a t", t=T)
        mix = a0(KD * T)
        mh = mix[:, 0:KD * T // 2].bitcast(f16).rearrange("p (a t) -> p a t", t=T)
        ml = mix[:, KD * T // 2:].bitcast(f16).rearrange("p (a t) -> p a t", t=T)
        UP = 16 + T
        upad = a0(4 * UP).rearrange("p (g t) -> p g t", t=UP)
        win = a0(2 * (16 + SEQ)).rearrange("p (a t) -> p a t", a=2)
        dT = a0(T)
        ext = a0(4 * NDEC * 16).rearrange("p (g b t) -> p g b t", g=4, b=NDEC)
        extsum = a0(4 * NDEC).rearrange("p (g b) -> p g b", g=4)
        inv = a0(15)
        vtok = a0(4 * 512).rearrange("p (c n) -> p c n", c=4)
        biasT = a0(4 * 512).rearrange("p (h n) -> p h n", h=4)
        pr = a0(2 * 512).rearrange("p (m n) -> p m n", m=2)
        am = a0(512)
        aT = a0(512)
        mx, nm, ls, rl = a0(2), a0(2), a0(2), a0(2)
        oT = a0(4 * T).rearrange("p (h t) -> p h t", t=T)
        NKV = 3
        kv = a0(NKV * NPG * 512).rearrange("p (s g n) -> p s g n", s=NKV, g=NPG)
        poolw = a0(4 * 128).rearrange("p (g n) -> p g n", g=4)
        qk2 = a0(64)
        td = a0(PAST + 1)
        tsm = a0(8)
        comb = a0(32)
        pnew = a0(128)
        aD = a0(32)
        vn = a0(32)
        lamt = a0(4)
        lpr = a0(2)
        lame = a0(2)
        nlam = a0(1)
        subw = a0(1)
        sel = a0(34)
        tab = a0(4)
        tab64 = a0(64)
        qpad = [mix[:, KD * T // 4:][:, 0:1024], mix[:, 3 * KD * T // 4:][:, 0:1024]]
        apad = qpad[0]
        oh = oT.rearrange("p h t -> p (h t)")[:, 0:NB + PAST + 1]
        tabB = am.rearrange("p (h n) -> p h n", h=4)
        strips = mix[:, 0:H0 * NB].rearrange("p (h n) -> p h n", h=H0)
        oy = pr.rearrange("p m n -> p (m n)")
        ors = [oy[:, 0:T], vtok.rearrange("p c n -> p (c n)")[:, 0:T]]
        yn = [biasT.rearrange("p h n -> p (h n)")[:, i * T:(i + 1) * T] for i in range(2)]

        a2 = carver()
        qkvc = a2(6 * T).rearrange("p (s a t) -> p s a t", s=2, a=3)
        sz = a2(2 * T).rearrange("p (s t) -> p s t", s=2)
        oh1 = a2(2 * T).rearrange("p (s t) -> p s t", s=2)
        mix1 = a2(KD * T)
        mh1 = mix1[:, 0:KD * T // 2].bitcast(f16).rearrange("p (a t) -> p a t", t=T)
        ml1 = mix1[:, KD * T // 2:].bitcast(f16).rearrange("p (a t) -> p a t", t=T)
        pre = a2(2 * 524).rearrange("p (s t) -> p s t", s=2)
        rs2 = a2(2 * T).rearrange("p (s t) -> p s t", s=2)
        ors1 = a2(T)
        yn1 = a2(T)
        sall = a2(HG * 128).rearrange("p (h n) -> p h n", h=HG)
        sping = a2(2 * 128).rearrange("p (s n) -> p s n", s=2)
        rest = a2(18 * 512)
        tail = a2(24 * 11).rearrange("p (a t) -> p a t", t=11)
        cext = a2(24 * NDEC * 4).rearrange("p (a b t) -> p a b t", a=24, b=NDEC)
        cw = a2(96).rearrange("p (i a) -> p i a", i=4)
        msk = a2(6 * 128).rearrange("p (m n) -> p m n", m=6)
        rows = a2(T)
        tokm = a2(4 * 40).rearrange("p (c n) -> p c n", c=4)
        selb = a2(2 * 2 * 128).rearrange("p (s m n) -> p s m n", s=2, m=2)
        gD, bD = (a2(64).rearrange("p (h b) -> p h b", h=HG) for _ in range(2))
        gate = a2(8)
        d4, kd4 = a2(4), a2(4)
        dS = a2(2 * 1024).rearrange("p (s n) -> p s n", s=2)
        um = a2(1024)
        krow, urow = a2(128), a2(128)
        ud, od, t8, qkp = a2(8), a2(8), a2(8), a2(8)
        ctmp = a2(24).rearrange("p (a b) -> p a b", a=3)
        (et, ets_nf_u, gamB, kbg_w, nt_z, At, dd, ddt, off1, off2, off3, d2_8, dt2_x, ya, yb, Kd, Kp, bV) = (
            rest[:, i * 512:(i + 1) * 512] for i in range(18))
        offs = (off1, off2, off3)
        rowt = rest[:, 0:4 * T].rearrange("p (s t) -> p s t", s=4)
        wabf = rest[:, 4 * T:4 * T + 320]
        wabh, wabl = (rest[:, 4 * T + 320 + 160 * i:4 * T + 480 + 160 * i].bitcast(f16).rearrange(
            "p (k n) -> p k n", k=KD) for i in range(2))

        a1 = carver()
        fh = a1(KF * T, f16).rearrange("p (a t) -> p a t", t=T)
        fl = a1(KF * T, f16).rearrange("p (a t) -> p a t", t=T)
        gt = a1(2 * T).rearrange("p (a t) -> p a t", t=T)
        ut = a1(2 * T).rearrange("p (a t) -> p a t", t=T)
        gu = a1(2 * T).rearrange("p (a t) -> p a t", t=T)
        yf = arena[:, 2 * KF * T // 2:2 * KF * T // 2 + KD * T].rearrange("p (a t) -> p a t", t=T)

        scratch = nc.dram_tensor("bias_scratch", (4, 128 * SKEW), f32).ap()

        x_in, x2_in, c_in = sem("x_in"), sem("x2_in"), sem("c_in")
        kv_in = [sem(f"kv_in{i}") for i in range(NKV)]
        w_in = [sem(f"w_in{i}") for i in range(2)]
        consts = sem("consts")
        hi_ready, lo_ready = sem("hi_ready"), sem("lo_ready")
        mm_done, pm_free = sem("mm_done"), sem("pm_free")
        z_hi, z_lo, sq_ready, ssq_ready, stat_ready = (sem("z_hi"), sem("z_lo"),
                                                                sem("sq_ready"), sem("ssq_ready"), sem("stat_ready"))
        ln_done, rstd_ready = sem("ln_done"), sem("rstd_ready")
        silu_done, prod_done, f_hi, f_lo = sem("silu_done"), sem("prod_done"), sem("f_hi"), sem("f_lo")
        outs, dve_step, pool_step, act_step = sem("outs"), sem("dve_step"), sem("pool_step"), sem("act_step")
        y_dve, y_pool = sem("y_dve"), sem("y_pool")
        tabB_ready, strip_ps, strip_ready, strip_out, bias_in = (sem("tabB_ready"), sem("strip_ps"),
                                                                 sem("strip_ready"), sem("strip_out"), sem("bias_in"))
        lam_pr, lam_ps, lam_ready = sem("lam_pr"), sem("lam_ps"), sem("lam_ready")
        vt_ps, vt_done = sem("vt_ps"), sem("vt_done")
        dq_ready, s_ready, s_read, nm_ready, exp_done, a_ready = (sem("dq_ready"), sem("s_ready"), sem("s_read"),
                                                                    sem("nm_ready"), sem("exp_done"), sem("a_ready"))
        at_ps, at_done, pv_done, o_evac = sem("at_ps"), sem("at_done"), sem("pv_done"), sem("o_evac")
        kv_used, dp_ready, comb_ready, ad_ps, ad_done = (sem("kv_used"), sem("dp_ready"),
                                                         sem("comb_ready"), sem("ad_ps"), sem("ad_done"))
        dec_o = sem("dec_o")
        d_ready, pool_ps, m_hi, m_lo = sem("d_ready"), sem("pool_ps"), sem("m_hi"), sem("m_lo")
        osq, ostat, oln, ors_ready, yn_ready = (sem("osq"), sem("ostat"), sem("oln"), sem("ors_ready"),
                                                sem("yn_ready"))
        dext = sem("dext")
        l1_in, l1_free, ab_split, ab_ps, ab_step, rows_ready, tok_ps, tok_done = (
            sem("l1_in"), sem("l1_free"), sem("ab_split"), sem("ab_ps"), sem("ab_step"), sem("rows_ready"),
            sem("tok_ps"), sem("tok_done"))
        conv_done, tail_done, convd_done, csilu = (sem("conv_done"), sem("tail_done"), sem("convd_done"),
                                                   sem("csilu"))
        nsq, nstat, nln, nrs, nq = sem("nsq"), sem("nstat"), sem("nln"), sem("nrs"), sem("nq")
        head_done = {e: sem(f"head_{e}") for e in HEAD_TILES}
        S = {n: head_done[e] for e, tiles in HEAD_TILES.items() for n in tiles}

        def G(name, n):
            e = next(e for e, tiles in HEAD_TILES.items() if name in tiles)
            at = [i for i, t in enumerate(HEAD_TILES[e]) if t == name]
            h, i = divmod(n - 1, len(at))
            return head_done[e], len(HEAD_TILES[e]) * h + at[i] + 1
        st_in = [sem(f"st_in{i}") for i in range(2)]
        st_out = [sem(f"st_out{i}") for i in range(2)]
        dprep, kqs_ps, du, du_ps, krow_s, urow_s, um_s, outer_ps, sdec, snew, zsilu = (
            sem("dprep"), sem("kqs_ps"), sem("du"), sem("du_ps"), sem("krow_s"),
            sem("urow_s"), sem("um_s"), sem("outer_ps"), sem("sdec"), sem("snew"), sem("zsilu"))
        o1sq, o1stat, o1ln, o1rs, yo, yz, m1_hi, m1_lo = (sem("o1sq"), sem("o1stat"), sem("o1ln"), sem("o1rs"),
                                                          sem("yo"), sem("yz"), sem("m1_hi"), sem("m1_lo"))

        block = ctx.enter_context(nc.Block())

        def bh(i):
            return divmod(i, H0)

        def paired(ap):
            return ap.rearrange("p (c n) -> p c n", c=2)

        @block.sync
        def _(sp):
            def weights(src, u, j, index, words):
                if not isinstance(u, int) or u >= 2:
                    sp.wait_ge(hi_ready, u - 1)
                    sp.wait_ge(lo_ready, u - 1)
                sp.dma_start(stage[:, j, 0:words], src[index].rearrange("a p n -> (a p) n")
                             if not isinstance(index, int) else src[index]).then_inc(w_in[j], 16)

            def stream(src, name, skip=0, until=None):
                base = FIRST_UNIT[name]
                n, words = [(c, w) for a, c, _, w in PHASES if a == name][0]
                with sp.Fori(skip // 2, (until or n) // 2) as i:
                    for j in range(2):
                        weights(src, base + 2 * i + j, j, bass.ds(2 * i + j, 1), words)

            sp.dma_start(par[:, :], params).then_inc(x_in, 16)
            sp.dma_start(hT[:, 0:4, :], xT[:, 0:4, :]).then_inc(x_in, 16)
            weights(w_in0, 0, 0, 0, WORDS[0])
            sp.dma_start(hT[:, 4:8, :], xT[:, 4:8, :]).then_inc(x2_in, 16)
            sp.dma_start(pt[:, :], pages).then_inc(c_in, 16)
            sp.dma_start(oh[0:33, :], onehot).then_inc(c_in, 16)
            sp.dma_start(tab[0:33, :], rel_tab).then_inc(c_in, 16)
            sp.dma_start(lamt[0:64, :], lam_vec).then_inc(c_in, 16)
            sp.dma_start(sel[0:64, :], sel64).then_inc(c_in, 16)
            sp.dma_start(inv, invcnt).then_inc(c_in, 16)
            sp.dma_start(poolw, pool_w).then_inc(c_in, 16)
            sp.dma_start(ext, pool_state).then_inc(c_in, 16)

            weights(w_in0, 1, 1, 1, WORDS[1])
            sp.wait_ge(c_in, 16 * 8)

            def load_kv(n):
                src, b, s = (cache_k, n, n % NKV) if n < NDEC else (cache_v, n - NDEC, n % NKV)
                if n >= NKV:
                    sp.wait_ge(kv_used, n - NKV + 1)
                for g in range(NPG):
                    i = b * NPG + g
                    page = sp.value_load(pt[0:1, i:i + 1], min_val=0, max_val=cache_k.shape[0] - 1)
                    sp.dma_start(kv[:, s, g, :], src[bass.ds(page, 1)].rearrange("a p n -> (a p) n")
                                 ).then_inc(kv_in[s], 16)

            for u in range(2, 4):
                weights(w_in0, u, u % 2, u, WORDS[u])
            for n in range(NKV):
                load_kv(n)
            sp.wait_ge(strip_ready, H0)
            sp.dma_start(scratch.rearrange("h (p m) -> p h m", m=SKEW)[:, :, 0:NB], strips).then_inc(strip_out, 16)
            sp.wait_ge(strip_out, 16)
            sp.dma_start(biasT, scratch[:, 127:127 + 128 * NB].rearrange("h (p c) -> p h c", c=NB)[:, :, 0:512]
                         ).then_inc(bias_in, 16)
            stream(w_in0, "in0", skip=4)
            for u in range(FIRST_UNIT["out0"], FIRST_UNIT["out0"] + 2):
                weights(w_out0, u, u % 2, u - FIRST_UNIT["out0"], WORDS[u])
            sp.wait_ge(pm_free, FIRST_TILE["out0"])
            sp.dma_start(o_k, qkv[:, 4:8, :]).then_inc(outs, 16)
            sp.dma_start(o_v, qkv[:, 8:12, :]).then_inc(outs, 16)
            sp.dma_start(o_pp, upad[:, :, 16 + SEQ - 15:16 + SEQ]).then_inc(outs, 16)
            sp.wait_ge(dext, 1)
            sp.dma_start(o_ps, ext).then_inc(outs, 16)
            for n in range(NKV, 2 * NDEC):
                load_kv(n)
            stream(w_out0, "out0", skip=2)
            stream(w_gu[0], "gu0", until=8)
            sp.wait_ge(pm_free, FIRST_TILE["gu0"])
            sp.wait_ge(outs, 16 * 4)
            sp.dma_start(wabf, wab.rearrange("p k n -> p (k n)")).then_inc(l1_in, 16)
            sp.dma_start(gate[0:8, 0:2], gates).then_inc(l1_in, 16)
            sp.dma_start(cw, convw).then_inc(l1_in, 16)
            sp.dma_start(msk, masks).then_inc(l1_in, 16)
            sp.dma_start(cext, conv_state).then_inc(l1_in, 16)
            for h in range(2):
                sp.dma_start(dS[:, h, :], delta_state[h]).then_inc(st_in[h], 16)
            stream(w_gu[0], "gu0", skip=8)
            stream(w_dn[0], "dn0")
            for u in range(FIRST_UNIT["in1"], FIRST_UNIT["in1"] + 2):
                weights(w_in1, u, u % 2, u - FIRST_UNIT["in1"], WORDS[u])
            for u in range(2, 6):
                weights(w_in1, FIRST_UNIT["in1"] + u, u % 2, u, WORDS[FIRST_UNIT["in1"] + u])
            for h in range(HG):
                for u in range(2 * h + 6, 2 * h + 8):
                    if u < 16:
                        weights(w_in1, FIRST_UNIT["in1"] + u, u % 2, u, WORDS[FIRST_UNIT["in1"] + u])
                    elif u < 18:
                        weights(w_out1, FIRST_UNIT["in1"] + u, u % 2, u - 16, WORDS[FIRST_UNIT["in1"] + u])
                sp.wait_ge(snew, h + 1)
                sp.dma_start(o_ds[h], dS[:, h % 2, :]).then_inc(st_out[h % 2], 16)
                if h + 2 < HG:
                    sp.wait_ge(st_out[h % 2], 16 * (h // 2 + 1))
                    sp.dma_start(dS[:, h % 2, :], delta_state[h + 2]).then_inc(st_in[h % 2], 16)
            sp.wait_ge(convd_done, 2 * HG)
            sp.dma_start(o_ct, tail).then_inc(outs, 16)
            sp.dma_start(o_cs, cext).then_inc(outs, 16)
            sp.wait_ge(*G("s", 4 * HG))
            sp.dma_start(o_dp, sall).then_inc(outs, 16)
            stream(w_out1, "out1", skip=2)
            stream(w_gu[1], "gu1")
            stream(w_dn[1], "dn1")
            for k in (0, 1, 3, 2, 4, 6, 5, 7):
                if k % 3 == 2:
                    sp.wait_ge(y_pool, k // 3 + 1)
                else:
                    sp.wait_ge(y_dve, 2 * (k // 3) + k % 3 + 1)
                sp.dma_start(o_y[:, k, :], yf[:, k, :]).then_inc(outs, 16)
            sp.wait_ge(outs, 16 * (7 + KD))
            for j in range(2):
                sp.wait_ge(st_out[j], 16 * NDEC // 2)

        @block.gpsimd
        def _(pool):
            steps = [0]

            def link(ins):
                steps[0] += 1
                ins.then_inc(pool_step, 1)
                pool.wait_ge(pool_step, steps[0])

            link(nc.gpsimd.memset(ident[:, :], 0.0))
            link(nc.gpsimd.affine_select(out=ident[:, :], in_=ident[:, :], compare_op=ALU.not_equal, fill=1.0, base=0,
                                         pattern=[[-1, 128]], channel_multiplier=1))
            nc.gpsimd.memset(ones[:, :], 1.0)
            nc.gpsimd.memset(onesD[:, :], 1.0 / D)
            nc.gpsimd.memset(onesH[:, :], 1.0 / 128)
            nc.gpsimd.memset(epsc[:, 0:1], EPS * WS * WS)
            nc.gpsimd.memset(epsc[:, 1:2], EPS)
            nc.gpsimd.memset(epsc[:, 2:3], EPS * 128)
            nc.gpsimd.memset(upad[:, :, 0:16], 0.0)
            nc.gpsimd.memset(qk2, 0.0)
            pool.nop().then_inc(consts, 1)
            pool.wait_ge(c_in, 16 * 8)
            for h in range(H0):
                link(nc.gpsimd.tensor_copy(tabB[0:33, h, :], tab[0:33, h:h + 1].to_broadcast([33, 128])))
            for m in range(2):
                link(nc.gpsimd.tensor_copy(tab64[0:33, :].rearrange("p (b h m) -> p b h m", b=NDEC, m=2)[:, :, :, m],
                                           tab[0:33, :].unsqueeze(1).to_broadcast([33, NDEC, H0])))
            pool.nop().then_inc(tabB_ready, 1)

            def sum_squares(b):
                for k in range(KD):
                    pool.wait_ge(sq_ready, KD * b + k + 1)
                    if k == 0:
                        if b > 0:
                            pool.wait_ge(stat_ready, b)
                        ins = nc.gpsimd.tensor_copy(ssq[:, :], sq[:, 0, :])
                    else:
                        ins = nc.gpsimd.tensor_tensor(ssq[:, :], ssq[:, :], sq[:, k % 2, :], ADD)
                    ins.then_inc(ssq_ready, 1)
                    pool.wait_ge(ssq_ready, KD * b + k + 1)

            sum_squares(0)

            pool.wait_ge(strip_out, 16)
            link(nc.gpsimd.memset(qpad[0], 0.0))
            link(nc.gpsimd.memset(qpad[1], 0.0))
            pool.nop().then_inc(consts, 1)
            pool.wait_ge(pm_free, 4)
            for g, w in enumerate(PW):
                src = upad[:, g, 0:16 + SEQ]
                for l in range(g + 1):
                    s, lo = 1 << l, (2 << l) - 1
                    dst = win[:, l % 2, :]
                    link(nc.gpsimd.tensor_tensor(dst[:, lo:], src[:, lo:], src[:, lo - s:16 + SEQ - s], ADD))
                    src = dst
                if g >= 1:
                    pool.wait_ge(pool_ps, g)
                link(nc.gpsimd.tensor_scalar(dT[:, 0:SEQ], src[:, 16:], 1.0 / w, None, MUL))
                link(nc.gpsimd.tensor_tensor(dT[:, 0:w - 1], src[:, 16:15 + w], inv[:, 0:w - 1], MUL))
                link(nc.gpsimd.tensor_tensor(dT[:, 0:SEQ], dT[:, 0:SEQ], upad[:, g, 16:16 + SEQ], SUB))
                if g == 0:
                    pool.wait_ge(dext, 1)
                link(nc.gpsimd.tensor_scalar(dT[:, SEQ:T], extsum[:, g, :], 1.0 / w, None, MUL))
                nc.gpsimd.tensor_tensor(dT[:, SEQ:T], dT[:, SEQ:T], ext[:, g, :, 15], SUB).then_inc(d_ready, 1)
                if g == 1:
                    pool.wait_ge(kv_used, NDEC)
                    nc.gpsimd.memset(apad, 0.0).then_inc(consts, 1)

            sum_squares(1)

            def ffn_up(layer):
                name = f"gu{layer}"

                def body(i):
                    t = FIRST_TILE[name] + 4 * i
                    f = 2 * (11 * layer + i)
                    for j in range(2):
                        pool.wait_ge(silu_done, f + j + 1)
                        pool.wait_ge(pm_free, t + 2 + j + 1)
                        nc.gpsimd.tensor_tensor(gu[:, j, :], gt[:, j, :], ut[:, j, :], MUL).then_inc(prod_done, 1)
                    for j in range(2):
                        pool.wait_ge(f_hi, f + j + 1)
                        nc.gpsimd.tensor_tensor(fl[:, bass.ds(2 * i + j, 1), :], gu[:, j:j + 1, :],
                                                fh[:, bass.ds(2 * i + j, 1), :], SUB).then_inc(f_lo, 1)
                    pool.wait_ge(f_lo, f + 2)
                with pool.Fori(0, 11) as i:
                    body(i)

            ffn_up(0)
            sum_squares(2)

            pool.wait_ge(pm_free, FIRST_TILE["in1"])
            nc.gpsimd.memset(rows[0:40, :], 0.0)
            nc.gpsimd.memset(pre[:, :, 0:3], 0.0).then_inc(l1_free, 1)
            pool.wait_ge(l1_in, 16 * 5)

            def tail_of(h, kind):
                pool.wait_ge(pm_free, FIRST_TILE["in1"] + 4 * h + kind + 1)
                nc.gpsimd.tensor_copy(tail[:, 8 * kind + h, :], pre[:, (3 * h + kind) % 2, SEQ:SEQ + 11]
                                      ).then_inc(tail_done, 1)

            def decode_conv(h, kinds):
                n = len(kinds)
                pool.wait_ge(tail_done, 3 * h + kinds[-1] + 1)
                a = slice(8 * kinds[0] + h, 8 * kinds[-1] + h + 1, 8)
                link(nc.gpsimd.tensor_copy(cext[:, a, :, 3], tail[:, a, 3:11]))
                dst = qkvc[:, h % 2, kinds[0]:kinds[-1] + 1, SEQ:]
                for i in range(4):
                    wt = cw[:, i, a].unsqueeze(2).to_broadcast([128, n, NDEC])
                    link(nc.gpsimd.tensor_tensor(dst if i == 0 else ctmp[:, 0:n, :], cext[:, a, :, i], wt, MUL))
                    if i > 0:
                        link(nc.gpsimd.tensor_tensor(dst, dst, ctmp[:, 0:n, :], ADD))
                pool.nop().then_inc(convd_done, 1)

            def square(h, kind):
                pool.wait_ge(csilu, 3 * h + kind + 1)
                if h >= 1:
                    pool.wait_ge(nstat, 2 * h)
                x = qkvc[:, h % 2, kind, :]
                nc.gpsimd.tensor_tensor(sq[:, kind, :], x, x, MUL).then_inc(nsq, 1)

            def normalize(h, kind):
                pool.wait_ge(nrs, 2 * h + kind + 1)
                x = qkvc[:, h % 2, kind, :]
                nc.gpsimd.tensor_tensor(x, x, rs2[:, kind, :], MUL).then_inc(nq, 1)

            def select_head(h):
                if h >= 2:
                    pool.wait_ge(*G("gb_ps", h - 1))
                nc.gpsimd.tensor_copy(selb[0:40, h % 2, 0, :], ident[0:40, h:h + 1].to_broadcast([40, 128]))
                nc.gpsimd.tensor_copy(selb[0:40, h % 2, 1, :], ident[0:40, 32 + h:33 + h].to_broadcast([40, 128])
                                      ).then_inc(S["selb"], 1)

            def gate_out(h):
                pool.wait_ge(yo, h + 1)
                pool.wait_ge(zsilu, h + 1)
                nc.gpsimd.tensor_tensor(yn1, yn1, sz[:, h % 2, :], MUL).then_inc(yz, 1)

            def gate_lo(h):
                pool.wait_ge(m1_hi, h + 1)
                nc.gpsimd.tensor_tensor(ml1[:, h, :], yn1, mh1[:, h, :], SUB).then_inc(m1_lo, 1)

            tail_of(0, 0)
            tail_of(0, 1)
            decode_conv(0, (0, 1))
            square(0, 0)
            square(0, 1)
            tail_of(0, 2)
            decode_conv(0, (2,))
            select_head(0)
            normalize(0, 0)
            normalize(0, 1)

            def four(ap):
                return ap.rearrange("p (c n) -> p c n", c=4)

            def mask(i):
                return msk[:, i, :].unsqueeze(1).to_broadcast([128, 4, 128])

            for h in range(HG):
                p, n = h + 1, h - 1
                q, k = qkvc[:, h % 2, 0, :], qkvc[:, h % 2, 1, :]
                pool.wait_ge(nq, 2 * h + 2)
                nc.gpsimd.tensor_tensor(qkp, q[:, SEQ:], k[:, SEQ:], MUL).then_inc(dprep, 1)
                pool.wait_ge(*G("et", h + 1))
                nc.gpsimd.tensor_tensor(four(ets_nf_u), four(et), mask(1), MUL).then_inc(S["ets"], 1)
                pool.wait_ge(*G("ets", h + 1))
                nc.gpsimd.tensor_tensor(four(et), four(et), mask(0), MUL).then_inc(S["eti"], 1)
                pool.wait_ge(*G("gam", h + 1))
                pool.wait_ge(*G("kk_ps", h + 1))
                nc.gpsimd.tensor_tensor(kbg_w, kbg_w, gamB, MUL).then_inc(S["kbg"], 1)
                pool.wait_ge(*G("nf", h + 1))
                for l in range(3):
                    nc.gpsimd.tensor_tensor(four(offs[l]), four(ets_nf_u), mask(3 + l), MUL).then_inc(S["om"], 1)
                if n >= 0:
                    gate_out(n)
                pool.wait_ge(*G("qk_ps", h + 1))
                nc.gpsimd.tensor_tensor(q[:, 0:SEQ], q[:, 0:SEQ], gamB, MUL).then_inc(S["qd"], 1)
                if n >= 0:
                    gate_lo(n)
                if p < HG:
                    tail_of(p, 0)
                    tail_of(p, 1)
                pool.wait_ge(kqs_ps, h + 1)
                pool.wait_ge(*G("gd", h + 1))
                v = dS[:, h % 2, :].rearrange("p (b n) -> p b n", b=NDEC)
                nc.gpsimd.tensor_tensor(v, v, gD[:, h, :].unsqueeze(2).to_broadcast([128, NDEC, 128]), MUL
                                        ).then_inc(sdec, 1)
                if p < HG:
                    decode_conv(p, (0, 1))
                    select_head(p)
                    tail_of(p, 2)
                    square(p, 0)
                    square(p, 1)
                    decode_conv(p, (2,))
                    normalize(p, 0)
                    normalize(p, 1)
            gate_out(HG - 1)
            gate_lo(HG - 1)
            sum_squares(3)
            ffn_up(1)
            sum_squares(4)
            pool.wait_ge(rstd_ready, 5)
            pool.wait_ge(z_hi, 5 * KD)
            for k in range(2, KD, 3):
                nc.gpsimd.tensor_tensor(yf[:, k, :], yf[:, k, :], rstd[:, :], MUL).then_inc(y_pool, 1)

        @block.scalar
        def _(act):
            def split_hi(u, j, words):
                act.wait_ge(w_in[j], 16)
                nc.scalar.activation(wh[:, j, 0:words], stage[:, j, 0:words], ACT.Copy, scale=WS).then_inc(hi_ready, 1)

            def next_split(name, i, j):
                base, per = FIRST_UNIT[name], [p for a, _, p, _ in PHASES if a == name][0]
                if isinstance(i, int) and base + 2 * i + j + 2 >= UNITS:
                    return
                words = WORDS[base + 2 * i + j + 2] if isinstance(i, int) else WORDS[base + j + 2]
                act.wait_ge(w_in[j], 16 * (base // 2 + i + 2))
                act.wait_ge(mm_done, FIRST_TILE[name] + per * (2 * i + j + 1))
                nc.scalar.activation(wh[:, j, 0:words], stage[:, j, 0:words], ACT.Copy, scale=WS).then_inc(hi_ready, 1)

            def square_tile(b, k):
                if KD * b + k >= 2:
                    act.wait_ge(ssq_ready, KD * b + k - 1)
                nc.scalar.activation(sq[:, k % 2, :], hT[:, k, :], ACT.Square).then_inc(sq_ready, 1)

            def norm_tile(b, k, name):
                act.wait_ge(pm_free, FIRST_TILE[name] + k + 1)
                if b < 4:
                    nc.scalar.activation(zh[:, k, :], hT[:, k, :], ACT.Copy,
                                         scale=par[:, NORM[b] + k:NORM[b] + k + 1]).then_inc(z_hi, 1)
                else:
                    nc.scalar.activation(yf[:, k, :], hT[:, k, :], ACT.Copy, scale=par[:, P_FIN + k:P_FIN + k + 1]
                                         ).then_inc(z_hi, 1)
                square_tile(b, k)

            def norm_factor(b):
                act.wait_ge(stat_ready, b + 1)
                c = epsc[:, 0:1] if b < 4 else epsc[:, 1:2]
                nc.scalar.activation(paired(rstd[:, :]), stat, ACT.Ln, scale=WS * WS if b < 4 else 1.0, bias=c
                                     ).then_inc(ln_done, 1)
                act.wait_ge(ln_done, b + 1)
                nc.scalar.activation(rstd[:, :], rstd[:, :], ACT.Exp, scale=-0.5).then_inc(rstd_ready, 1)

            act.preload_act_table_set("natural_log_exp_and_others")
            for half in range(2):
                act.wait_ge(*((x_in, 32) if half == 0 else (x2_in, 16)))
                for k in range(4 * half, 4 * half + 4):
                    nc.scalar.activation(zh[:, k, :], hT[:, k, :], ACT.Copy, scale=par[:, NORM[0] + k:NORM[0] + k + 1]
                                         ).then_inc(z_hi, 1)
                if half == 0:
                    split_hi(0, 0, WORDS[0])
            for k in range(2):
                square_tile(0, k)
            split_hi(1, 1, WORDS[1])
            for k in range(2, KD):
                square_tile(0, k)
            act.wait_ge(consts, 1)
            norm_factor(0)
            next_split("in0", 0, 0)
            for h in range(H0):
                act.wait_ge(strip_ps, h + 1)
                nc.scalar.activation(strips[:, h, :].rearrange("p (c n) -> p c n", c=2),
                                     P[:, 6:8, 0:NB // 2] if h % 2 == 0 else P[:, 4:6, 0:NB // 2], ACT.Copy
                                     ).then_inc(strip_ready, 1)
            act.wait_ge(lam_ps, 1)
            nc.scalar.activation(lame, P[:, 6, 0:2], ACT.Exp).then_inc(act_step, 1)
            next_split("in0", 0, 1)
            for i in range(1, 4):
                for j in range(2):
                    if i + j < 4:
                        next_split("in0", i, j)

            for c in range(4):
                act.wait_ge(vt_ps, c + 1)
                nc.scalar.activation(vtok[:, c, :], P[:, 4 + c, :], ACT.Copy).then_inc(vt_done, 1)
            next_split("in0", 3, 1)

            for s in range(16):
                h, qt = divmod(s, 4)
                w = 128 * (qt + 1)
                act.wait_ge(nm_ready, s + 1)
                for m in range(2):
                    nc.scalar.activation(pr[:, m, 0:w], pr[:, m, 0:w], ACT.Exp, bias=nm[:, m:m + 1],
                                         accum_out=ls[:, m:m + 1]).then_inc(exp_done, 1)
                act.wait_ge(at_ps, s + 1)
                if s >= 1:
                    act.wait_ge(pv_done, s)
                nc.scalar.activation(aT[:, 0:w], P[:, 6, 0:w], ACT.Copy).then_inc(at_done, 1)
                if qt == 3:
                    act.wait_ge(pv_done, s + 1)
                    nc.scalar.activation(oT[:, h, 0:SEQ], P[:, 7, :], ACT.Copy).then_inc(o_evac, 1)
                if s == 8:
                    act.wait_ge(dp_ready, 1)
                    nc.scalar.activation(td[0:64, :], td[0:64, :], ACT.Exp, bias=tsm[0:64, 1:2],
                                         accum_out=tsm[0:64, 2:3]).then_inc(act_step, 1)
                if s == 10:
                    act.wait_ge(ad_ps, 1)
                    act.wait_ge(consts, 3)
                    nc.scalar.activation(aD, P[:, 0, 128:160], ACT.Copy)
                    for g in range(NPG):
                        v = apad[:, g * 256:(g + 1) * 256]
                        for h1 in range(H0):
                            ins = nc.scalar.activation(v[:, h1:h1 + 36 * 7 + 1:36], P[:, 0, g * 32 + h1:g * 32 + 32:4],
                                                       ACT.Copy)
                    ins.then_inc(ad_done, 1)
                if qt == 2:
                    g = h
                    act.wait_ge(pool_ps, g + 1)
                    nc.scalar.activation(paired(mh[:, g, :]), P[:, 2:4, 0:CH], ACT.Copy,
                                         scale=par[:, P_POOL + g:P_POOL + g + 1]).then_inc(m_hi, 1)
            act.wait_ge(kv_used, 2 * NDEC)
            nc.scalar.activation(td[0:32, 0:512], P[0:32, 1, :], ACT.Copy).then_inc(ad_done, 1)
            def mix_hi(h):
                act.wait_ge(yn_ready, h + 1)
                nc.scalar.activation(mh[:, 4 + h, :], yn[h % 2], ACT.Copy).then_inc(m_hi, 1)

            act.wait_ge(dec_o, 1)
            for h in range(H0):
                if h >= 2:
                    act.wait_ge(ostat, h - 1)
                nc.scalar.activation(sq[:, h % 2, :], oT[:, h, :], ACT.Square).then_inc(osq, 1)
            for h in range(H0):
                act.wait_ge(ostat, h + 1)
                if h >= 2:
                    act.wait_ge(yn_ready, h - 1)
                nc.scalar.activation(paired(ors[h % 2]), P[:, 4 + 2 * (h % 2):6 + 2 * (h % 2), 0:CH], ACT.Ln,
                                     bias=epsc[:, 1:2]).then_inc(oln, 1)
                act.wait_ge(oln, h + 1)
                nc.scalar.activation(ors[h % 2], ors[h % 2], ACT.Exp, scale=-0.5).then_inc(ors_ready, 1)
                if h >= 1:
                    mix_hi(h - 1)
            mix_hi(H0 - 1)

            def project_out(name, b):
                for i in range(2 if name[:3] == "out" else 4):
                    for j in range(2):
                        for k in ((4 * i + 2 * j, 4 * i + 2 * j + 1) if name[:3] == "out" else (2 * i + j,)):
                            norm_tile(b, k, name)
                        next_split(name, i, j)
                norm_factor(b)

            def ffn_up(layer):
                name = f"gu{layer}"
                act.preload_act_table(ACT.Silu)

                def body(i):
                    t = FIRST_TILE[name] + 4 * i
                    f = 2 * (11 * layer + i)
                    for j in range(2):
                        act.wait_ge(pm_free, t + j + 1)
                        nc.scalar.activation(gt[:, j, :], gt[:, j, :], ACT.Silu).then_inc(silu_done, 1)
                    next_split(name, i, 0)
                    for j in range(2):
                        act.wait_ge(prod_done, f + j + 1)
                        nc.scalar.activation(fh[:, bass.ds(2 * i + j, 1), :], gu[:, j:j + 1, :], ACT.Copy
                                             ).then_inc(f_hi, 1)
                    next_split(name, i, 1)
                with act.Fori(0, 10) as i:
                    body(i)
                body(10)
                act.preload_act_table_set("natural_log_exp_and_others")

            project_out("out0", 1)
            ffn_up(0)
            project_out("dn0", 2)

            act.wait_ge(l1_in, 16 * 5)
            nc.scalar.activation(wabh.rearrange("p k n -> p (k n)"), wabf, ACT.Copy, scale=WS).then_inc(ab_split, 1)
            nc.scalar.activation(gate[0:8, 2:3], gate[0:8, 0:1], ACT.Exp).then_inc(ab_step, 1)
            act.wait_ge(ab_step, 2)
            nc.scalar.activation(rowt[32:40, 1, :], rowt[32:40, 0, :], ACT.Exp, scale=-1.0)
            nc.scalar.activation(rowt[0:8, 1, :], rowt[0:8, 1, :], ACT.Exp).then_inc(ab_step, 1)
            act.wait_ge(ab_step, 3)
            nc.scalar.activation(rowt[0:8, 1, :], rowt[0:8, 1, :], ACT.Ln, bias=ones[0:8, 0:1]).then_inc(ab_step, 1)

            def norm_l2(h, kind):
                m = 2 * h + kind
                act.wait_ge(nstat, m + 1)
                if h >= 1:
                    act.wait_ge(nq, m - 1)
                nc.scalar.activation(paired(rs2[:, kind, :]), stat, ACT.Ln, scale=128.0 if kind == 0 else 1.0,
                                     bias=epsc[:, 2:3] if kind == 0 else epsc[:, 1:2]).then_inc(nln, 1)
                act.wait_ge(nln, m + 1)
                nc.scalar.activation(rs2[:, kind, :], rs2[:, kind, :], ACT.Exp, scale=-0.5).then_inc(nrs, 1)

            def silu_qk(h):
                act.wait_ge(convd_done, 2 * h + 1)
                for kind in range(2):
                    act.wait_ge(conv_done, 12 * h + 4 * kind + 4)
                    x = qkvc[:, h % 2, kind, :]
                    nc.scalar.activation(x, x, ACT.Silu).then_inc(csilu, 1)

            def silu_vz(h):
                act.wait_ge(pm_free, FIRST_TILE["in1"] + 4 * h + 4)
                nc.scalar.activation(sz[:, h % 2, :], sz[:, h % 2, :], ACT.Silu).then_inc(zsilu, 1)
                act.wait_ge(convd_done, 2 * h + 2)
                act.wait_ge(conv_done, 12 * h + 12)
                nc.scalar.activation(qkvc[:, h % 2, 2, :], qkvc[:, h % 2, 2, :], ACT.Silu).then_inc(csilu, 1)

            def head_square(h):
                act.wait_ge(*G("o", h + 1))
                act.wait_ge(du, h + 1)
                if h >= 1:
                    act.wait_ge(o1stat, h)
                nc.scalar.activation(ssq[:, :], oh1[:, h % 2, :], ACT.Square).then_inc(o1sq, 1)

            def head_factor(h):
                act.wait_ge(o1stat, h + 1)
                if h >= 1:
                    act.wait_ge(yo, h)
                nc.scalar.activation(paired(ors1), stat, ACT.Ln, bias=epsc[:, 1:2]).then_inc(o1ln, 1)
                act.wait_ge(o1ln, h + 1)
                nc.scalar.activation(ors1, ors1, ACT.Exp, scale=-0.5).then_inc(o1rs, 1)

            def head_hi(h):
                act.wait_ge(yz, h + 1)
                nc.scalar.activation(mh1[:, h, :], yn1, ACT.Copy).then_inc(m1_hi, 1)

            next_split("in1", 0, 0)
            act.preload_act_table(ACT.Silu)
            silu_qk(0)
            act.preload_act_table_set("natural_log_exp_and_others")
            norm_l2(0, 0)
            norm_l2(0, 1)
            act.wait_ge(tok_ps, 1)
            nc.scalar.activation(tokm, P[:, 6, 0:160].rearrange("p (c n) -> p c n", c=4), ACT.Copy
                                 ).then_inc(tok_done, 1)

            def evac(dst, bank, ready, name, h):
                act.wait_ge(*G(ready, h + 1))
                nc.scalar.activation(dst, P[:, bank, :], ACT.Copy).then_inc(S[name], 1)

            for h in range(HG):
                p, n = h + 1, h - 1
                act.wait_ge(*G("gb_ps", h + 1))
                nc.scalar.activation(gamB, P[:, 2, :], ACT.Exp).then_inc(S["gam"], 1)
                nc.scalar.activation(gD[:, h, :], P[:, 7, 0:8], ACT.Exp).then_inc(S["gd"], 1)
                if n >= 0:
                    head_factor(n)
                act.wait_ge(*G("ex", h + 1))
                nc.scalar.activation(et, et, ACT.Exp).then_inc(S["et"], 1)
                nc.scalar.activation(kd4, d4, ACT.Exp).then_inc(S["kd4"], 1)
                act.preload_act_table(ACT.Silu)
                next_split("in1", h, 1)
                silu_vz(h)
                act.wait_ge(*G("d", h + 1))
                evac(ets_nf_u, 6, "n_ps", "nf", h)
                act.wait_ge(*G("tk_ps", h + 1))
                act.wait_ge(*G("kd4", h + 1))
                for c in range(4):
                    ins = nc.scalar.activation(Kd[:, c * 128:(c + 1) * 128], P[:, 7, c * 128:(c + 1) * 128], ACT.Copy,
                                               scale=kd4[:, c:c + 1])
                ins.then_inc(S["kd"], 1)
                evac(d2_8, 2, "d2_ps", "d2", h)
                evac(dd, 6, "d4_ps", "d4", h)
                act.wait_ge(*G("y1", h + 1))
                evac(ddt, 7, "dt4_ps", "dt4", h)
                act.wait_ge(*G("tv_ps", h + 1))
                for c in range(4):
                    ins = nc.scalar.activation(bV[:, c * 128:(c + 1) * 128], P[:, 5, c * 128:(c + 1) * 128], ACT.Copy,
                                               scale=tokm[:, c, 32 + h:33 + h])
                ins.then_inc(S["bv"], 1)
                evac(d2_8, 3, "d8_ps", "d8", h)
                if n >= 0:
                    head_hi(n)
                for l in range(3):
                    act.wait_ge(*G("x_ps", 3 * h + l + 1))
                    nc.scalar.activation(dt2_x, P[:, 5, :], ACT.Copy).then_inc(S["x"], 1)
                    if l == 0:
                        act.wait_ge(kqs_ps, h + 1)
                        if h >= 1:
                            act.wait_ge(outer_ps, h)
                        nc.scalar.activation(krow[0:8, :], P[0:8, 4, 32:160], ACT.Copy).then_inc(krow_s, 1)
                    if l == 1:
                        act.wait_ge(du_ps, h + 1)
                        nc.scalar.activation(urow[0:8, :], P[0:8, 4, 160:288], ACT.Copy).then_inc(urow_s, 1)
                if p < HG:
                    next_split("in1", p, 0)
                evac(kbg_w, 4, "w_ps", "w", h)
                if p < HG:
                    silu_qk(p)
                act.preload_act_table_set("natural_log_exp_and_others")
                if p < HG:
                    norm_l2(p, 0)
                act.wait_ge(*G("o_ps", h + 1))
                if h >= 2:
                    act.wait_ge(yo, h - 1)
                nc.scalar.activation(oh1[:, h % 2, 0:SEQ], P[:, 7, :], ACT.Copy).then_inc(S["o"], 1)
                if p < HG:
                    norm_l2(p, 1)
                head_square(h)
            head_factor(HG - 1)
            head_hi(HG - 1)
            project_out("out1", 3)
            ffn_up(1)
            project_out("dn1", 4)

        @block.vector
        def _(dve):
            steps = [0]

            def link(ins):
                steps[0] += 1
                ins.then_inc(dve_step, 1)
                dve.wait_ge(dve_step, steps[0])

            def split_lo(u, j, words):
                dve.wait_ge(hi_ready, u + 1)
                nc.vector.scalar_tensor_tensor(out=wl[:, j, 0:words], in0=stage[:, j, 0:words], scalar=WS,
                                               in1=wh[:, j, 0:words], op0=MUL, op1=SUB).then_inc(lo_ready, 1)

            def next_split(name, i, j):
                base = FIRST_UNIT[name]
                if isinstance(i, int) and base + 2 * i + j + 2 >= UNITS:
                    return
                words = WORDS[base + 2 * i + j + 2] if isinstance(i, int) else WORDS[base + j + 2]
                split_lo(base + 2 * i + j + 2, j, words)

            def norm_lo(b, k):
                dve.wait_ge(z_hi, KD * b + k + 1)
                nc.vector.scalar_tensor_tensor(out=zl[:, k, :], in0=hT[:, k, :],
                                               scalar=par[:, NORM[b] + k:NORM[b] + k + 1], in1=zh[:, k, :],
                                               op0=MUL, op1=SUB).then_inc(z_lo, 1)

            for k in range(4):
                norm_lo(0, k)
            split_lo(0, 0, WORDS[0])
            for k in range(4, 8):
                norm_lo(0, k)
            split_lo(1, 1, WORDS[1])
            dve.wait_ge(c_in, 16 * 8)
            nc.vector.tensor_tensor(lpr[0:64, :], lamt[0:64, 0:2], lamt[0:64, 2:4], MUL).then_inc(lam_pr, 1)
            dve.wait_ge(rstd_ready, 1)
            for u in range(8):
                for j in range(2):
                    t = 2 * u + j
                    dve.wait_ge(mm_done, t + 1)
                    if t < 4:
                        nc.vector.tensor_tensor(paired(upad[:, t, 16:]), pm[j], paired(rstd[:, :]), MUL
                                                ).then_inc(pm_free, 1)
                    else:
                        nc.vector.scalar_tensor_tensor(out=paired(qkv[:, t - 4, :]), in0=pm[j],
                                                       scalar=HALF ** -0.5 if t < 8 else 1.0,
                                                       in1=paired(rstd[:, :]), op0=MUL, op1=MUL).then_inc(pm_free, 1)
                if u < 7:
                    next_split("in0", u // 2, u % 2)
                if u == 2:
                    dve.wait_ge(act_step, 1)
                    nc.vector.scalar_tensor_tensor(out=nlam, in0=lame[:, 1:2], scalar=-LAM0, in1=lame[:, 0:1],
                                                   op0=ADD, op1=SUB).then_inc(lam_ready, 1)
                if u == 1:
                    dve.wait_ge(pm_free, 4)
                    link(nc.vector.tensor_copy(ext[:, :, :, 15], upad[:, :, 16 + SEQ:]))
                    for g, w in enumerate(PW):
                        ins = nc.vector.tensor_reduce(out=extsum[:, g, :], in_=ext[:, g, :, 16 - w:], axis=AX.X, op=ADD)
                    link(ins)
                    dve.nop().then_inc(dext, 1)
                if u == 5:
                    dve.wait_ge(pm_free, 8)
                    dve.wait_ge(consts, 2)
                    for m in range(2):
                        part = slice(64 * m, 64 * m + 64)
                        for half in range(2):
                            for b in range(4):
                                at = 264 * b + 32 * half + m
                                nc.vector.tensor_copy(qpad[half][part, at:at + 66 * 3 + 1:66],
                                                      qkv[part, 0:4, SEQ + 4 * half + b])
            dve.wait_ge(x_in, 32)
            link(nc.vector.tensor_scalar(subw, par[:, P_SUB:P_SUB + 1], 1 - LAM0, None, MUL))
            dve.wait_ge(pm_free, 16)
            for m in range(2):
                part = slice(64 * m, 64 * m + 64)
                ins = nc.vector.tensor_tensor(qk2[part, :].rearrange("p (b h m) -> p b h m", b=NDEC, m=2)[:, :, :, m],
                                              qkv[part, 0:4, SEQ:].rearrange("p h b -> p b h"),
                                              qkv[part, 4:8, SEQ:].rearrange("p h b -> p b h"), MUL)
            link(ins)
            dve.nop().then_inc(dq_ready, 1)
            next_split("in0", 3, 1)

            def decode_softmax(s):
                if s == 7:
                    dve.wait_ge(kv_used, NDEC)
                    nc.vector.tensor_copy(td[0:64, 0:PAST], P[0:64, 0, :])
                    link(nc.vector.tensor_copy(td[0:64, PAST:PAST + 1], P[0:64, 1, 0:1]))
                    link(nc.vector.tensor_reduce(out=tsm[0:64, 0:1], in_=td[0:64, :], axis=AX.X, op=MAX))
                    nc.vector.tensor_scalar(tsm[0:64, 1:2], tsm[0:64, 0:1], -1.0, None, MUL).then_inc(dp_ready, 1)
                elif s == 9:
                    link(nc.vector.scalar_tensor_tensor(out=tsm[0:64, 3:4], in0=sel[0:64, 1:2], scalar=nlam[0:64, :],
                                                        in1=sel[0:64, 0:1], op0=MUL, op1=ADD))
                    dve.wait_ge(act_step, 2)
                    link(nc.vector.reciprocal(tsm[0:64, 4:5], tsm[0:64, 2:3]))
                    link(nc.vector.tensor_tensor(tsm[0:64, 5:6], tsm[0:64, 4:5], tsm[0:64, 3:4], MUL))
                    nc.vector.tensor_scalar(pnew[0:64, :], ones[0:64, :], td[0:64, PAST:PAST + 1], None, MUL)
                    nc.vector.tensor_scalar(comb[0:64, :], sel[0:64, 2:34], tsm[0:64, 5:6], None, MUL
                                            ).then_inc(comb_ready, 1)

            dve.wait_ge(bias_in, 16)
            for s in range(16):
                h, qt = divmod(s, 4)
                w = 128 * (qt + 1)
                if s >= 1:
                    dve.wait_ge(a_ready, s)
                for m in range(2):
                    dve.wait_ge(s_ready, 2 * s + m + 1)
                    nc.vector.tensor_tensor_reduce(out=pr[:, m, 0:w], in0=P[:, 4 + m, 0:w], in1=biasT[:, h, 512 - w:],
                                                   scale=1.0, scalar=NEG, op0=ADD, op1=MAX,
                                                   accum_out=mx[:, m:m + 1]).then_inc(s_read, 1)
                dve.wait_ge(s_read, 2 * s + 2)
                nc.vector.tensor_scalar(nm, mx, -1.0, None, MUL).then_inc(nm_ready, 1)
                dve.wait_ge(exp_done, 2 * s + 2)
                link(nc.vector.reciprocal(rl, ls))
                link(nc.vector.tensor_scalar(pr[:, 1, 0:w], pr[:, 1, 0:w], rl[:, 1:2], nlam, MUL, MUL))
                if s >= 1:
                    dve.wait_ge(at_ps, s)
                nc.vector.scalar_tensor_tensor(out=am[:, 0:w], in0=pr[:, 0, 0:w], scalar=rl[:, 0:1],
                                               in1=pr[:, 1, 0:w], op0=MUL, op1=ADD).then_inc(a_ready, 1)
                decode_softmax(s)
                if qt == 3:
                    g = h
                    dve.wait_ge(m_hi, g + 1)
                    nc.vector.scalar_tensor_tensor(out=paired(ml[:, g, :]), in0=P[:, 2:4, 0:CH],
                                                   scalar=par[:, P_POOL + g:P_POOL + g + 1], in1=paired(mh[:, g, :]),
                                                   op0=MUL, op1=SUB).then_inc(m_lo, 1)
            dve.wait_ge(ad_done, 1)
            link(nc.vector.tensor_tensor(vn.rearrange("p (b h) -> p b h", b=NDEC),
                                         aD.rearrange("p (b h) -> p b h", b=NDEC),
                                         qkv[:, 8:12, SEQ:].rearrange("p h b -> p b h"), MUL))
            dve.wait_ge(ad_ps, 2)
            dve.wait_ge(o_evac, 4)
            for h in range(H0):
                ins = nc.vector.tensor_tensor(oT[:, h, SEQ:], P[:, 4, 33 * h:32 * h + 32:4], vn[:, h:32:4], ADD)
            ins.then_inc(dec_o, 1)
            def mix_lo(h):
                dve.wait_ge(m_hi, 4 + h + 1)
                nc.vector.tensor_tensor(ml[:, 4 + h, :], yn[h % 2], mh[:, 4 + h, :], SUB).then_inc(m_lo, 1)

            for h in range(H0):
                dve.wait_ge(ors_ready, h + 1)
                if h >= 2:
                    dve.wait_ge(m_lo, 4 + h - 1)
                nc.vector.scalar_tensor_tensor(out=yn[h % 2], in0=oT[:, h, :], scalar=subw,
                                               in1=ors[h % 2], op0=MUL, op1=MUL).then_inc(yn_ready, 1)
                if h >= 1:
                    mix_lo(h - 1)
            mix_lo(H0 - 1)

            def project_out(name, b):
                pairs = name[:3] == "out"
                for i in range(2 if pairs else 4):
                    for j in range(2):
                        ks = (4 * i + 2 * j, 4 * i + 2 * j + 1) if pairs else (2 * i + j,)
                        for n, k in enumerate(ks):
                            slot = n if pairs else j
                            dve.wait_ge(mm_done, FIRST_TILE[name] + k + 1)
                            nc.vector.scalar_tensor_tensor(out=paired(hT[:, k, :]), in0=pm[slot], scalar=1 / WS,
                                                           in1=paired(hT[:, k, :]), op0=MUL, op1=ADD
                                                           ).then_inc(pm_free, 1)
                        if b < 4:
                            for k in ks:
                                norm_lo(b, k)
                        next_split(name, i, j)

            def ffn_up(layer, b):
                name = f"gu{layer}"
                dve.wait_ge(rstd_ready, b + 1)

                def body(i):
                    t = FIRST_TILE[name] + 4 * i
                    f = 2 * (11 * layer + i)
                    for part, dst in enumerate((gt, ut)):
                        for j in range(2):
                            dve.wait_ge(mm_done, t + 2 * part + j + 1)
                            if not isinstance(i, int) or i > 0:
                                dve.wait_ge(prod_done, f + j - 1)
                            nc.vector.tensor_tensor(paired(dst[:, j, :]), pm[j], paired(rstd[:, :]), MUL
                                                    ).then_inc(pm_free, 1)
                        next_split(name, i, part)
                body(0)
                with dve.Fori(1, 10) as i:
                    body(i)
                body(10)

            project_out("out0", 1)
            ffn_up(0, 1)
            project_out("dn0", 2)

            def leave(h, kind):
                t = FIRST_TILE["in1"] + 4 * h + kind
                acc = pm[kind % 2] if h == 0 else pm[0]
                dve.wait_ge(mm_done, t + 1)
                if kind == 3:
                    if h >= 2:
                        dve.wait_ge(yz, h - 1)
                    dst = sz[:, h % 2, :]
                else:
                    e = 3 * h + kind
                    if e >= 2:
                        dve.wait_ge(tail_done, e - 1)
                    dst = pre[:, e % 2, 3:3 + T]
                nc.vector.tensor_tensor(paired(dst), acc, paired(rstd[:, :]), MUL).then_inc(pm_free, 1)

            dve.wait_ge(l1_free, 1)
            dve.wait_ge(ab_split, 1)
            nc.vector.scalar_tensor_tensor(out=wabl.rearrange("p k n -> p (k n)"), in0=wabf, scalar=WS,
                                           in1=wabh.rearrange("p k n -> p (k n)"), op0=MUL, op1=SUB
                                           ).then_inc(ab_split, 1)
            dve.wait_ge(rstd_ready, 3)
            leave(0, 0)
            dve.wait_ge(ab_ps, 1)
            link(nc.vector.tensor_tensor(paired(rowt[0:40, 0, :]), P[0:40, 4:6, 0:CH], paired(rstd[0:40, :]), MUL))
            link(nc.vector.tensor_scalar(rowt[0:8, 2, :], rowt[0:8, 0, :], gate[0:8, 1:2], 0.0, ADD, MAX))
            link(nc.vector.tensor_scalar(rowt[0:8, 3, :], rowt[0:8, 0, :], gate[0:8, 1:2], 0.0, ADD, MIN))
            nc.vector.tensor_tensor(rowt[0:8, 1, :], rowt[0:8, 3, :], rowt[0:8, 2, :], SUB).then_inc(ab_step, 1)
            def convolve(h, kind, i):
                a, e = 8 * kind + h, 3 * h + kind
                x, c = pre[:, e % 2, :], qkvc[:, h % 2, kind, 0:SEQ]
                if i == 0:
                    dve.wait_ge(pm_free, FIRST_TILE["in1"] + 4 * h + kind + 1)
                    ins = nc.vector.tensor_scalar(c, x[:, 0:SEQ], cw[:, 0, a:a + 1], None, MUL)
                else:
                    dve.wait_ge(conv_done, 4 * e + i)
                    ins = nc.vector.scalar_tensor_tensor(out=c, in0=x[:, i:i + SEQ], scalar=cw[:, i, a:a + 1], in1=c,
                                                         op0=MUL, op1=ADD)
                ins.then_inc(conv_done, 1)

            leave(0, 1)
            for kind in range(2):
                for i in range(4):
                    convolve(0, kind, i)
            leave(0, 2)
            dve.wait_ge(ab_step, 4)
            link(nc.vector.tensor_tensor(rowt[0:8, 2, :], rowt[0:8, 2, :], rowt[0:8, 1, :], ADD))
            link(nc.vector.tensor_scalar(rowt[0:8, 2, :], rowt[0:8, 2, :], gate[0:8, 2:3], -1.0, MUL, MUL))
            for c in range(4):
                nc.vector.tensor_tensor_scan(rows[0:8, c * 128:(c + 1) * 128], ones[0:8, :],
                                             rowt[0:8, 2, c * 128:(c + 1) * 128], 0.0, MUL, ADD)
            nc.vector.tensor_copy(rows[0:8, SEQ:], rowt[0:8, 2, SEQ:])
            leave(0, 3)
            link(nc.vector.tensor_scalar(rowt[32:40, 1, :], rowt[32:40, 1, :], 1.0, None, ADD))
            nc.vector.reciprocal(rows[32:40, :], rowt[32:40, 1, :]).then_inc(rows_ready, 1)
            next_split("in1", 0, 0)

            def split_quarter(u, j, c):
                q = slice(c * UQ, (c + 1) * UQ)
                dve.wait_ge(hi_ready, u + 1)
                ins = nc.vector.scalar_tensor_tensor(out=wl[:, j, q], in0=stage[:, j, q], scalar=WS,
                                                     in1=wh[:, j, q], op0=MUL, op1=SUB)
                if c == 3:
                    ins.then_inc(lo_ready, 1)

            def four(ap):
                return ap.rearrange("p (c n) -> p c n", c=4)

            def mask(i):
                return msk[:, i, :].unsqueeze(1).to_broadcast([128, 4, 128])

            def add(dst, bank, src, ready, name, count, op=ADD):
                dve.wait_ge(*G(ready, count))
                if op == ADD:
                    nc.vector.tensor_tensor(dst, P[:, bank, :], src, ADD).then_inc(S[name], 1)
                else:
                    nc.vector.tensor_tensor(dst, src, P[:, bank, :], SUB).then_inc(S[name], 1)

            def head_scale(h):
                dve.wait_ge(o1rs, h + 1)
                if h >= 1:
                    dve.wait_ge(m1_lo, h)
                nc.vector.scalar_tensor_tensor(out=yn1, in0=oh1[:, h % 2, :], scalar=par[:, P_ONORM:P_ONORM + 1],
                                               in1=ors1, op0=MUL, op1=MUL).then_inc(yo, 1)

            def decode_update(h):
                dve.wait_ge(kqs_ps, h + 1)
                dve.wait_ge(krow_s, h + 1)
                dve.wait_ge(csilu, 3 * h + 3)
                kqS = P[:, 4, 0:16].rearrange("p (b m) -> p b m", m=2)
                g = gD[:, h, :]
                nc.vector.tensor_tensor(od, kqS[:, :, 0], g, MUL)
                link(nc.vector.tensor_tensor(t8, kqS[:, :, 1], g, MUL))
                link(nc.vector.tensor_tensor(t8, qkvc[:, h % 2, 2, SEQ:], t8, SUB))
                link(nc.vector.tensor_tensor(ud, t8, bD[:, h, :], MUL))
                link(nc.vector.tensor_tensor(t8, ud, P[:, 4, 16:24], MUL))
                nc.vector.tensor_tensor(oh1[:, h % 2, SEQ:], od, t8, ADD).then_inc(du, 1)

            def decode_rows(h):
                dve.wait_ge(urow_s, h + 1)
                nc.vector.tensor_tensor(um[0:8, :].rearrange("p (b n) -> p b n", b=NDEC),
                                        urow[0:8, :].unsqueeze(1).to_broadcast([8, NDEC, 128]),
                                        ident[0:8, 0:8].unsqueeze(2).to_broadcast([8, NDEC, 128]), MUL
                                        ).then_inc(um_s, 1)

            def decode_state(h):
                dve.wait_ge(outer_ps, h + 1)
                dve.wait_ge(sdec, h + 1)
                v = dS[:, h % 2, :].rearrange("p (c n) -> p c n", c=2)
                nc.vector.tensor_tensor(v, P[:, 2:4, :], v, ADD).then_inc(snew, 1)

            dve.wait_ge(tok_done, 1)
            for h in range(HG):
                p, n = h + 1, h - 1
                k = qkvc[:, h % 2, 1, 0:SEQ]
                dve.wait_ge(*G("gd", h + 1))
                for c in range(4):
                    nc.vector.tensor_scalar(et[:, c * 128:(c + 1) * 128], P[:, 2, c * 128:(c + 1) * 128],
                                            tokm[:, c, h:h + 1], 0.0, SUB, MIN)
                nc.vector.tensor_tensor(d4, P[:, 2, :].rearrange("p (c n) -> p c n", c=4)[:, :, 127],
                                        tokm[:, :, h], SUB).then_inc(S["ex"], 1)
                nc.vector.tensor_copy(bD[:, h, :], P[:, 7, 8:16]).then_inc(S["bd"], 1)
                dve.wait_ge(nq, 2 * h + 2)
                nc.vector.tensor_tensor(kbg_w, P[:, 3, :], k, MUL).then_inc(S["kb"], 1)
                for i in range(4):
                    convolve(h, 2, i)
                dve.wait_ge(*G("ets", h + 1))
                dve.wait_ge(*G("kk_ps", h + 1))
                nc.vector.tensor_tensor(nt_z, P[:, 4, :], ets_nf_u, MUL).then_inc(S["nt"], 1)
                dve.wait_ge(*G("nt", h + 1))
                nc.vector.tensor_tensor(four(ddt), four(nt_z), mask(2), MUL).then_inc(S["dt"], 1)
                dve.wait_ge(*G("eti", h + 1))
                dve.wait_ge(*G("qk_ps", h + 1))
                nc.vector.tensor_tensor(At, P[:, 5, :], et, MUL).then_inc(S["at"], 1)
                dve.wait_ge(*G("n_ps", h + 1))
                nc.vector.tensor_tensor(four(dd), four(P[:, 6, :]), mask(2), MUL).then_inc(S["d"], 1)
                if p < HG:
                    leave(p, 0)
                else:
                    leave(h, 3)
                dve.wait_ge(*G("dt", h + 1))
                nc.vector.scalar_tensor_tensor(out=four(ya), in0=four(ddt), scalar=-1.0,
                                               in1=ident[:, :].unsqueeze(1).to_broadcast([128, 4, 128]),
                                               op0=MUL, op1=ADD).then_inc(S["y1"], 1)
                if n >= 0:
                    head_scale(n)
                if p < HG:
                    convolve(p, 0, 0)
                    convolve(p, 0, 1)
                dve.wait_ge(*G("dt2_ps", h + 1))
                nc.vector.tensor_copy(dt2_x, P[:, 3, :]).then_inc(S["dt2"], 1)
                dve.wait_ge(*G("tkb_ps", h + 1))
                nc.vector.tensor_copy(Kp, P[:, 4, :]).then_inc(S["kp"], 1)
                for c in range(4):
                    split_quarter(FIRST_UNIT["in1"] + 2 * h + 3, 1, c)
                dve.wait_ge(*G("y1", h + 1))
                add(yb, 2, ya, "y2_ps", "y2", h + 1)
                if p < HG:
                    convolve(p, 0, 2)
                    convolve(p, 0, 3)
                dve.wait_ge(*G("y2", h + 1))
                add(ya, 4, yb, "y3_ps", "y3", h + 1)
                dve.wait_ge(*G("y3", h + 1))
                if p < HG:
                    leave(p, 1)
                    convolve(p, 1, 0)
                add(yb, 6, ya, "y4_ps", "xt", h + 1)
                if p < HG:
                    for i in range(1, 4):
                        convolve(p, 1, i)
                for l in range(3):
                    src, dst = (yb, ya) if l % 2 == 0 else (ya, yb)
                    dve.wait_ge(*G("z_ps", 3 * h + l + 1))
                    nc.vector.tensor_copy(nt_z, P[:, 7, :]).then_inc(S["z"], 1)
                    if p < HG and l == 2:
                        leave(p, 2)
                    dve.wait_ge(*G("xt", 4 * h + l + 1))
                    add(dst, 6, src, "v_ps", "xt", 3 * h + l + 1, SUB)
                    if l == 0:
                        decode_update(h)
                    elif l == 1:
                        decode_rows(h)
                    else:
                        decode_state(h)
                dve.wait_ge(*G("u_ps", h + 1))
                nc.vector.tensor_copy(ets_nf_u, P[:, 5, :]).then_inc(S["u"], 1)
                for c in range(4):
                    cc = slice(c * 128, (c + 1) * 128)
                    if c > 0:
                        dve.wait_ge(*G("ws_ps", 3 * h + c))
                        dve.wait_ge(*G("u", 4 * h + c))
                        nc.vector.tensor_tensor(ets_nf_u[:, cc], ets_nf_u[:, cc], P[:, 2, cc], SUB).then_inc(S["u"], 1)
                    dve.wait_ge(*G("ds_ps", 4 * h + c + 1))
                    dst = sall[:, h, :] if c == 3 else sping[:, c % 2, :]
                    if c == 0:
                        nc.vector.tensor_copy(dst, P[:, 3, cc]).then_inc(S["s"], 1)
                    else:
                        dve.wait_ge(*G("s", 4 * h + c))
                        nc.vector.scalar_tensor_tensor(out=dst, in0=sping[:, (c - 1) % 2, :],
                                                       scalar=gamB[:, c * 128 + 127:c * 128 + 128], in1=P[:, 3, cc],
                                                       op0=MUL, op1=ADD).then_inc(S["s"], 1)
                    if p < HG:
                        split_quarter(FIRST_UNIT["in1"] + 2 * p + 2, 0, c)
                if p < HG - 1:
                    leave(p, 3)
            head_scale(HG - 1)
            project_out("out1", 3)
            ffn_up(1, 3)
            project_out("dn1", 4)

            dve.wait_ge(rstd_ready, 5)
            dve.wait_ge(z_hi, 5 * KD)
            for k in range(KD):
                if k % 3 < 2:
                    nc.vector.tensor_tensor(yf[:, k, :], yf[:, k, :], rstd[:, :], MUL).then_inc(y_dve, 1)

        @block.tensor
        def _(pe):
            def product(j, wslot, woff, xh, xl, nk, stride, ks=None, ready=None):
                for k in range(nk) if ks is None else ks:
                    if ready is not None:
                        ready(k)
                    o = woff + k * stride
                    for w, x in ((wh, xh), (wh, xl), (wl, xh)):
                        for c in range(2):
                            mm = nc.tensor.matmul(pm[j][:, c, :], w[:, wslot, o:o + 128],
                                                  x[:, k, c * CH:(c + 1) * CH],
                                                  start=(k == 0 and w is wh and x is xh),
                                                  stop=(k == nk - 1 and w is wl))
                return mm

            def unit(name, i, j, xh, xl, ready=None, between=None):
                base, per, words = FIRST_UNIT[name], *[(p, w) for a, _, p, w in PHASES if a == name][0]
                pe.wait_ge(hi_ready, base + 2 * i + j + 1)
                pe.wait_ge(lo_ready, base + 2 * i + j + 1)
                nk = KF if per == 1 else KD
                for n in range(per):
                    slot = n if per == 2 else j
                    t = FIRST_TILE[name] + per * (2 * i + j) + n
                    if not isinstance(t, int) or t >= 2:
                        pe.wait_ge(pm_free, t - 1)
                    product(slot, j, 128 * n, xh, xl, nk, words // nk, ready=ready if n == 0 else None
                            ).then_inc(mm_done, 1)
                    if n == 0 and between is not None:
                        between()

            def phase(name, xh, xl, ready=None, between=None, first=0):
                n = [c for a, c, _, _ in PHASES if a == name][0] // 2
                if first == 0:
                    unit(name, 0, 0, xh, xl, ready, between)
                    unit(name, 0, 1, xh, xl)
                with pe.Fori(max(first, 1), n) as i:
                    for j in range(2):
                        unit(name, i, j, xh, xl)

            def phase_in_two(name, xh, xl, early, done, mid, ready):
                base, t = FIRST_UNIT[name], FIRST_TILE[name]
                pe.wait_ge(hi_ready, base + 1)
                pe.wait_ge(lo_ready, base + 1)
                pe.wait_ge(pm_free, t - 1)
                if done < early:
                    product(0, 0, 0, xh, xl, KD, 256, range(done, early), ready)
                mid()
                pe.wait_ge(pm_free, t)
                product(1, 0, 128, xh, xl, KD, 256, range(early), ready)
                for n in range(2):
                    product(n, 0, 128 * n, xh, xl, KD, 256, range(early, KD), ready).then_inc(mm_done, 1)
                unit(name, 0, 1, xh, xl)
                phase(name, xh, xl, first=1)

            def z_ready(b):
                def wait(k):
                    pe.wait_ge(z_lo, KD * b + k + 1)
                return wait

            def statistics(b):
                pe.wait_ge(ssq_ready, KD * (b + 1))
                if b > 0:
                    pe.wait_ge(rstd_ready, b)
                for c in range(2):
                    mm = nc.tensor.matmul(stat[:, c, :], onesD[:, :], ssq[:, c * CH:(c + 1) * CH], start=True, stop=True)
                mm.then_inc(stat_ready, 1)

            unit("in0", 0, 0, zh, zl, z_ready(0))
            pe.wait_ge(consts, 1)
            statistics(0)
            pe.wait_ge(tabB_ready, 1)
            pe.wait_ge(c_in, 16 * 8)
            for h in range(H0):
                if h == 1:
                    pe.wait_ge(rstd_ready, 1)
                if h >= 2:
                    pe.wait_ge(strip_ready, h - 1)
                for c in range(2):
                    mm = nc.tensor.matmul(P[:, (6 if h % 2 == 0 else 4) + c, 0:NB // 2], tabB[0:33, h, :],
                                          oh[0:33, c * NB // 2:(c + 1) * NB // 2], start=True, stop=True)
                mm.then_inc(strip_ps, 1)
            pe.wait_ge(lam_pr, 1)
            pe.wait_ge(strip_ready, H0)
            nc.tensor.matmul(P[:, 6, 0:2], ones[0:64, :], lpr[0:64, :], start=True, stop=True).then_inc(lam_ps, 1)
            unit("in0", 0, 1, zh, zl)
            phase("in0", zh, zl, first=1)

            pe.wait_ge(pm_free, 16)
            pe.wait_ge(rstd_ready, 1)
            pe.wait_ge(lam_ready, 1)
            for c in range(4):
                for h in range(H0):
                    mm = nc.tensor.transpose(P[:, 4 + c, h * 128:(h + 1) * 128], qkv[:, 8 + h, c * 128:(c + 1) * 128],
                                             ident[:, :])
                mm.then_inc(vt_ps, 1)
            pe.wait_ge(dq_ready, 1)
            nc.tensor.matmul(P[0:64, 0, :], tab64[0:33, :], oh[0:33, NB:NB + PAST], start=True, stop=False)
            nc.tensor.matmul(P[0:64, 1, 0:1], tab64[0:33, :], oh[0:33, NB + PAST:NB + PAST + 1], start=True, stop=False)
            nc.tensor.matmul(P[0:64, 1, 0:1], qk2, ones[:, 0:1], start=False, stop=True)

            def decode_scores(i):
                b, h = bh(i)
                if h == 0:
                    pe.wait_ge(kv_in[b % NKV], 16 * NPG * (b // NKV + 1))
                mm = nc.tensor.matmul(P[0:64, 0, :], qpad[i // 16][:, i % 16 * 64:i % 16 * 64 + 64],
                                      kv[:, b % NKV, :, h * 128:(h + 1) * 128], start=False, stop=(i == 31))
                if h == 3:
                    mm.then_inc(kv_used, 1)

            def decode_probs():
                pe.wait_ge(comb_ready, 1)
                for g in range(NPG + 1):
                    lhs = td[0:64, g * 128:(g + 1) * 128] if g < NPG else pnew[0:64, :]
                    mm = nc.tensor.matmul(P[:, 0, g * 32:(g + 1) * 32], lhs, comb[0:64, :], start=True, stop=True)
                mm.then_inc(ad_ps, 1)

            def decode_values(b):
                n = NDEC + b
                if b == 0:
                    pe.wait_ge(ad_done, 1)
                pe.wait_ge(kv_in[n % NKV], 16 * NPG * (n // NKV + 1))
                for g in range(NPG):
                    mm = nc.tensor.matmul(P[0:32, 1, :], apad[:, g * 256 + b * 32:g * 256 + b * 32 + 32],
                                          kv[:, n % NKV, g, :], start=(b == 0 and g == 0),
                                          stop=(b == NDEC - 1 and g == NPG - 1))
                mm.then_inc(kv_used, 1)

            def attend(s):
                h, qt = divmod(s, 4)
                pe.wait_ge(at_done, s + 1)
                if s >= 4 and qt == 0:
                    pe.wait_ge(o_evac, h)
                for c in range(qt + 1):
                    mm = nc.tensor.matmul(P[:, 7, qt * 128:(qt + 1) * 128], vtok[:, c, h * 128:(h + 1) * 128],
                                          aT[:, c * 128:(c + 1) * 128], start=(c == 0), stop=(c == qt))
                mm.then_inc(pv_done, 1)

            def scores(s):
                h, qt = divmod(s, 4)
                w = 128 * (qt + 1)
                for m in range(2):
                    if s >= 1:
                        pe.wait_ge(s_read, 2 * s - 1 + m)
                    part = slice(64 * m, 64 * m + 64)
                    nc.tensor.matmul(P[:, 4 + m, 0:w], qkv[part, h, qt * 128:(qt + 1) * 128], qkv[part, 4 + h, 0:w],
                                     start=True, stop=True).then_inc(s_ready, 1)

            pe.wait_ge(vt_done, 4)
            scores(0)
            for s in range(16):
                h, qt = divmod(s, 4)
                if s < NDEC:
                    decode_scores(4 * s)
                    decode_scores(4 * s + 1)
                elif s == 10:
                    decode_probs()
                elif s > 10:
                    decode_values((0, 1, 2, 4, 6)[s - 11])
                if s >= 1:
                    attend(s - 1)
                if qt == 2:
                    pe.wait_ge(d_ready, h + 1)
                    if h >= 1:
                        pe.wait_ge(m_lo, h)
                    for c in range(2):
                        mm = nc.tensor.matmul(P[:, 2 + c, 0:CH], poolw[:, h, :], dT[:, c * CH:(c + 1) * CH],
                                              start=True, stop=True)
                    mm.then_inc(pool_ps, 1)
                if s < NDEC:
                    decode_scores(4 * s + 2)
                    decode_scores(4 * s + 3)
                elif s > 12:
                    decode_values((3, 5, 7)[s - 13])
                if s < 15:
                    scores(s + 1)
                pe.wait_ge(a_ready, s + 1)
                if s >= 1:
                    pe.wait_ge(at_done, s)
                for c in range(qt + 1):
                    mm = nc.tensor.transpose(P[:, 6, c * 128:(c + 1) * 128], am[:, c * 128:(c + 1) * 128], ident[:, :])
                mm.then_inc(at_ps, 1)
            attend(15)

            pe.wait_ge(ad_done, 2)
            for h in range(H0):
                mm = nc.tensor.transpose(P[:, 4, h * 32:(h + 1) * 32], td[0:32, h * 128:(h + 1) * 128],
                                         ident[0:32, 0:32])
            mm.then_inc(ad_ps, 1)
            pe.wait_ge(m_lo, 4)
            def head_stats(h):
                pe.wait_ge(osq, h + 1)
                if h >= 2:
                    pe.wait_ge(oln, h - 1)
                for c in range(2):
                    mm = nc.tensor.matmul(P[:, 4 + 2 * (h % 2) + c, 0:CH], onesH[:, :],
                                          sq[:, h % 2, c * CH:(c + 1) * CH], start=True, stop=True)
                mm.then_inc(ostat, 1)

            def out0_mid():
                for h in range(H0):
                    head_stats(h)

            phase_in_two("out0", mh, ml, 4, 0, out0_mid, lambda k: pe.wait_ge(m_lo, k + 1))

            def f_ready(layer):
                def wait(k):
                    pe.wait_ge(f_lo, KF * layer + k + 1)
                return wait

            phase("gu0", zh, zl, z_ready(1), lambda: statistics(1))
            phase("dn0", fh, fl, f_ready(0))
            unit("in1", 0, 0, zh, zl, z_ready(2), lambda: statistics(2))

            pe.wait_ge(ab_split, 2)
            pe.wait_ge(rstd_ready, 3)
            for k in range(KD):
                for w, x in ((wabh, zh), (wabh, zl), (wabl, zh)):
                    for c in range(2):
                        mm = nc.tensor.matmul(P[0:40, 4 + c, 0:CH], w[:, k, :], x[:, k, c * CH:(c + 1) * CH],
                                              start=(k == 0 and w is wabh and x is zh),
                                              stop=(k == KD - 1 and w is wabl))
            mm.then_inc(ab_ps, 1)

            unit("in1", 0, 1, zh, zl)
            def stat_l2(h, kind):
                pe.wait_ge(nsq, 2 * h + kind + 1)
                if kind == 1:
                    pe.wait_ge(nln, 2 * h + 1)
                for c in range(2):
                    mm = nc.tensor.matmul(stat[:, c, :], ones[:, :], sq[:, kind, c * CH:(c + 1) * CH],
                                          start=True, stop=True)
                mm.then_inc(nstat, 1)

            def stat_head(h):
                pe.wait_ge(o1sq, h + 1)
                for c in range(2):
                    mm = nc.tensor.matmul(stat[:, c, :], onesH[:, :], ssq[:, c * CH:(c + 1) * CH],
                                          start=True, stop=True)
                mm.then_inc(o1stat, 1)

            def project_part(h, part):
                kind, k = divmod(part, KD)
                u, n = 2 * h + kind // 2, kind % 2
                if k == 0:
                    pe.wait_ge(hi_ready, FIRST_UNIT["in1"] + u + 1)
                    pe.wait_ge(lo_ready, FIRST_UNIT["in1"] + u + 1)
                    pe.wait_ge(pm_free, FIRST_TILE["in1"] + 4 * h + kind)
                o = 128 * n + 256 * k
                for w, x in ((wh, zh), (wh, zl), (wl, zh)):
                    for c in range(2):
                        mm = nc.tensor.matmul(pm[0][:, c, :], w[:, u % 2, o:o + 128], x[:, k, c * CH:(c + 1) * CH],
                                              start=(k == 0 and w is wh and x is zh), stop=(k == KD - 1 and w is wl))
                if k == KD - 1:
                    mm.then_inc(mm_done, 1)

            def chunks(bank, lhs, rhs, name):
                for c in range(4):
                    cc = slice(c * 128, (c + 1) * 128)
                    mm = nc.tensor.matmul(P[:, bank, cc], lhs[:, cc], rhs[:, cc], start=True, stop=True)
                mm.then_inc(S[name], 1)

            def turn(bank, src, name):
                for c in range(4):
                    cc = slice(c * 128, (c + 1) * 128)
                    mm = nc.tensor.transpose(P[:, bank, cc], src[:, cc], ident[:, :])
                mm.then_inc(S[name], 1)

            def ready(h, *names):
                for n in names:
                    pe.wait_ge(*G(n, h + 1))

            stat_l2(0, 0)
            stat_l2(0, 1)
            pe.wait_ge(rows_ready, 1)
            for c in range(4):
                mm = nc.tensor.transpose(P[:, 6, 40 * c:40 * c + 40], rows[0:40, c * 128:(c + 1) * 128],
                                         ident[0:40, 0:40])
            mm.then_inc(tok_ps, 1)
            def output_part(k):
                if k == 0:
                    pe.wait_ge(hi_ready, FIRST_UNIT["out1"] + 1)
                    pe.wait_ge(lo_ready, FIRST_UNIT["out1"] + 1)
                    pe.wait_ge(pm_free, FIRST_TILE["out1"])
                pe.wait_ge(m1_lo, k + 1)
                product(0, 0, 0, mh1, ml1, KD, 256, (k,))

            pe.wait_ge(pm_free, FIRST_TILE["in1"] + 4)
            pe.wait_ge(tok_done, 1)
            for h in range(HG):
                q, k, v = (qkvc[:, h % 2, i, 0:SEQ] for i in range(3))
                done, calls = [0], [0]

                def fill(n):
                    first = 28 if h == HG - 1 else 0
                    last = 28 if h == HG - 2 else 32
                    for part in range(first + done[0], min(first + done[0] + n, last)):
                        project_part(min(h + 1, HG - 1), part)
                        done[0] += 1
                    if h == HG - 1 and done[0] >= 4:
                        calls[0] += 1
                        if calls[0] in OUT1_CALLS:
                            output_part(OUT1_CALLS.index(calls[0]))

                ready(h, "selb")
                if h >= 1:
                    pe.wait_ge(*G("s", 4 * h))
                    ready(h - 1, "o")
                nc.tensor.matmul(P[:, 2, :], selb[0:40, h % 2, 0, :], rows[0:40, 0:SEQ], start=True, stop=True)
                nc.tensor.matmul(P[:, 3, :], selb[0:40, h % 2, 1, :], rows[0:40, 0:SEQ], start=True, stop=True)
                nc.tensor.matmul(P[:, 7, 0:8], selb[0:40, h % 2, 0, :], rows[0:40, SEQ:], start=True, stop=True)
                nc.tensor.matmul(P[:, 7, 8:16], selb[0:40, h % 2, 1, :], rows[0:40, SEQ:], start=True, stop=True
                                 ).then_inc(S["gb_ps"], 1)
                if h >= 1:
                    pe.wait_ge(nln, 2 * h + 2)
                    stat_head(h - 1)
                fill(2)
                pe.wait_ge(nq, 2 * h + 2)
                if h >= 1:
                    pe.wait_ge(o1ln, h)
                chunks(5, k, q, "qk_ps")
                ready(h, "kb")
                chunks(4, k, kbg_w, "kk_ps")
                ready(h, "gd", "bd")
                turn(7, k, "tk_ps")
                fill(3)
                ready(h, "nt")
                turn(6, nt_z, "n_ps")
                fill(2)
                ready(h, "kbg")
                turn(4, kbg_w, "tkb_ps")
                fill(1)
                ready(h, "d", "dt", "gam")
                chunks(2, ddt, dd, "d2_ps")
                chunks(3, dd, ddt, "dt2_ps")
                fill(3)
                ready(h, "d2", "dt2", "nf", "kd")
                chunks(6, dt2_x, d2_8, "d4_ps")
                chunks(7, d2_8, dt2_x, "dt4_ps")
                ready(h, "y1")
                chunks(2, d2_8, ya, "y2_ps")
                ready(h, "at")
                pe.wait_ge(csilu, 3 * h + 3)
                turn(5, v, "tv_ps")
                fill(3)
                ready(h, "d4", "dt4", "y2", "kp")
                chunks(3, ddt, dd, "d8_ps")
                chunks(4, dd, yb, "y3_ps")
                fill(2)
                ready(h, "d8", "y3")
                chunks(6, d2_8, ya, "y4_ps")
                fill(3)
                pe.wait_ge(st_in[h % 2], 16 * (h // 2 + 1))
                pe.wait_ge(dprep, h + 1)
                for b in range(NDEC):
                    nc.tensor.matmul(P[:, 4, 2 * b:2 * b + 2], dS[:, h % 2, b * 128:(b + 1) * 128],
                                     qkvc[:, h % 2, 0:2, SEQ + b], start=True, stop=True)
                nc.tensor.matmul(P[:, 4, 16:24], ones[:, :], qkp, start=True, stop=True)
                nc.tensor.transpose(P[0:8, 4, 32:160], qkvc[:, h % 2, 1, SEQ:], ident[:, :]).then_inc(kqs_ps, 1)
                ready(h, "bv")
                for l in range(3):
                    src = yb if l % 2 == 0 else ya
                    pe.wait_ge(*G("xt", 4 * h + l + 1))
                    turn(5, src, "x_ps")
                    pe.wait_ge(*G("om", 3 * h + l + 1))
                    chunks(7, offs[l], src, "z_ps")
                    fill(1)
                    if l == 2:
                        pe.wait_ge(um_s, h + 1)
                        for c in range(2):
                            mm = nc.tensor.matmul(P[:, 2 + c, :], krow[0:8, :], um[0:8, c * 512:(c + 1) * 512],
                                                  start=True, stop=True)
                        mm.then_inc(outer_ps, 1)
                    pe.wait_ge(*G("x", 3 * h + l + 1))
                    pe.wait_ge(*G("z", 3 * h + l + 1))
                    chunks(6, dt2_x, nt_z, "v_ps")
                    fill(1)
                    if l == 1:
                        pe.wait_ge(du, h + 1)
                        pe.wait_ge(krow_s, h + 1)
                        nc.tensor.transpose(P[0:8, 4, 160:288], ud, ident[:, :]).then_inc(du_ps, 1)
                pe.wait_ge(*G("xt", 4 * h + 4))
                pe.wait_ge(urow_s, h + 1)
                chunks(4, Kp, ya, "w_ps")
                chunks(5, ya, bV, "u_ps")
                fill(1)
                pe.wait_ge(snew, h + 1)
                for c in range(4):
                    cc = slice(c * 128, (c + 1) * 128)
                    s_prev = sping[:, (c - 1) % 2, :]
                    if c == 1:
                        ready(h, "w", "qd")
                    if c > 0:
                        pe.wait_ge(*G("s", 4 * h + c))
                        nc.tensor.matmul(P[:, 2, cc], kbg_w[:, cc], s_prev, start=True, stop=True
                                         ).then_inc(S["ws_ps"], 1)
                        nc.tensor.matmul(P[:, 7, cc], s_prev, q[:, cc], start=True, stop=False)
                    if c == 1:
                        fill(1)
                    elif c > 1 and h + 1 < HG:
                        stat_l2(h + 1, c - 2)
                    pe.wait_ge(*G("u", 4 * h + c + 1))
                    nc.tensor.matmul(P[:, 3, cc], Kd[:, cc], ets_nf_u[:, cc], start=True, stop=True
                                     ).then_inc(S["ds_ps"], 1)
                    mm = nc.tensor.matmul(P[:, 7, cc], ets_nf_u[:, cc], At[:, cc], start=(c == 0), stop=True)
                    if c == 0:
                        fill(1)
                mm.then_inc(S["o_ps"], 1)
                fill(4)

            def out1_mid():
                pe.wait_ge(*G("s", 4 * HG))
                stat_head(HG - 1)

            phase_in_two("out1", mh1, ml1, HG - 1, len(OUT1_CALLS), out1_mid, lambda k: pe.wait_ge(m1_lo, k + 1))
            phase("gu1", zh, zl, z_ready(3), lambda: statistics(3))
            phase("dn1", fh, fl, f_ready(1))
            statistics(4)


NORM = (P_MIX, P_FFN, P_MIX + 8, P_FFN + 8)


def kernel(**inputs):
    import numpy as np
    import concourse.bacc as bacc
    from concourse.bass_utils import run_bass_kernel_spmd
    a = {k: np.asarray(v) for k, v in inputs.items()}
    f = np.float32

    def units(w, width):
        k, n = w.shape
        return np.ascontiguousarray(w.reshape(k // 128, 128, n // width, width).transpose(2, 1, 0, 3)
                                    ).reshape(n // width, 128, -1)

    def rows(v):
        return v.reshape(-1, 128).T

    def gate_up(w):
        g, u = units(w[:, :DFF], 256), units(w[:, DFF:], 256)
        return np.stack([g, u], 1).reshape(22, 128, -1)

    x = np.concatenate([a["x_prompt"][0], a["x_sample"][:, 0]])
    pool_pages = a["cache_k"].shape[0]
    n = np.arange(0, PAST + 1)
    large = 16 + (np.log(np.maximum(n, 1).astype(f) / f(16)) / f(np.log(8.0)) * f(16)).astype(np.int32)
    bucket = np.where(n < 16, n, np.minimum(large, 31))
    onehot = np.zeros((33, NB + PAST + 1), f)
    for m in range(NB):
        d = SEQ - 1 - m
        onehot[bucket[d] if d >= 0 else 32, m] = 1
    for t in range(PAST + 1):
        onehot[bucket[PAST - t], NB + t] = 1
    sel64 = np.zeros((64, 34), f)
    for r in range(64):
        sel64[r, r % 2] = 1
        sel64[r, 2 + r // 2] = 1
    p, n = np.arange(128)[:, None], np.arange(128)[None]
    masks = np.stack([p <= n, p < n, p // 16 == n // 16] +
                     [(p // (2 * s) == n // (2 * s)) & (p // s > n // s) for s in (16, 32, 64)], 1).astype(f)
    wab = np.zeros((128, KD, 40), f)
    w2 = a["w_in_odd"][0][:, 4096:].reshape(KD, 128, 16).transpose(1, 0, 2)
    wab[:, :, 0:8], wab[:, :, 32:40] = w2[:, :, 0:8], w2[:, :, 8:16]
    arrays = {
        "xT": np.ascontiguousarray(x.T.reshape(KD, 128, T).transpose(1, 0, 2)),
        "w_in0": units(a["w_in_even"][0], 256), "w_out0": units(a["w_out_even"][0], 256),
        "w_gu": np.stack([gate_up(w) for w in a["w_gate_up"]]),
        "w_dn": np.stack([units(w, 128) for w in a["w_down"]]),
        "w_in1": units(a["w_in_odd"][0][:, :4096].reshape(D, 4, HG, 128).transpose(0, 2, 1, 3).reshape(D, 4096), 256), "w_out1": units(a["w_out_odd"][0], 256),
        "params": np.ascontiguousarray(np.concatenate(
            [rows(a[k]) for k in ("norm_mix", "norm_ffn", "norm_final", "pool_scale", "subln_w", "o_norm")], 1)),
        "convw": np.ascontiguousarray(rows(a["conv_w"][0])),
        "wab": wab,
        "gates": np.ascontiguousarray(np.concatenate([a["a_log"], a["dt_bias"]]).T),
        "cache_k": np.ascontiguousarray(a["cache_k"][:, 0].transpose(0, 3, 2, 1)).reshape(pool_pages, 128, 512),
        "cache_v": np.ascontiguousarray(a["cache_v"][:, 0]).reshape(pool_pages, 128, 512),
        "pages": a["page_table"].reshape(1, -1),
        "pool_w": np.ascontiguousarray(a["pool_w"][0].transpose(1, 0, 2)),
        "pool_state": np.pad(a["state_pool"][0].reshape(NDEC, 15, 4, 128).transpose(3, 2, 0, 1),
                             ((0, 0), (0, 0), (0, 0), (0, 1))),
        "conv_state": np.pad(a["state_conv"][0].reshape(NDEC, 3, 24, 128).transpose(3, 2, 0, 1),
                             ((0, 0), (0, 0), (0, 0), (0, 1))),
        "delta_state": np.ascontiguousarray(a["state_delta"][0].transpose(1, 2, 0, 3)).reshape(HG, 128, NDEC * 128),
        "rel_tab": np.concatenate([a["rel_bias"], np.full((1, 4), NEG, f)]),
        "onehot": onehot,
        "lam_vec": np.ascontiguousarray(np.stack([a[k][0] for k in ("lambda_q1", "lambda_q2", "lambda_k1",
                                                                   "lambda_k2")], 1)),
        "sel64": sel64,
        "invcnt": np.ascontiguousarray(np.broadcast_to((1 / np.arange(1, 16)).astype(f), (128, 15))),
        "masks": np.ascontiguousarray(masks),
    }
    outs = {"o_y": (128, KD, T), "o_k": (128, 4, T), "o_v": (128, 4, T), "o_pp": (128, 4, 15),
            "o_ps": (128, 4, NDEC, 16), "o_ct": (128, 24, 11), "o_cs": (128, 24, NDEC, 4),
            "o_dp": (128, HG, 128), "o_ds": (HG, 128, NDEC * 128)}
    nc = bacc.Bacc("TRN2", target_bir_lowering=False, num_devices=1)
    aps = [nc.dram_tensor(k, v.shape, mybir.dt.from_np(v.dtype), kind="ExternalInput").ap() for k, v in arrays.items()]
    aps += [nc.dram_tensor(k, s, mybir.dt.float32, kind="ExternalOutput").ap() for k, s in outs.items()]
    hybrid_trunk(nc, *aps)
    r = run_bass_kernel_spmd(nc, [arrays], core_ids=[0]).results[0]
    feat = {k: r[k].transpose(2, 1, 0).reshape(T, -1) for k in ("o_y", "o_k", "o_v")}
    k, v = (feat[n].reshape(T, 4, 128) for n in ("o_k", "o_v"))
    return (feat["o_y"][None, :SEQ], feat["o_y"][SEQ:, None], k[None, None, :SEQ], v[None, None, :SEQ],
            k[SEQ:, None, None], v[SEQ:, None, None],
            r["o_pp"].transpose(2, 1, 0).reshape(1, 1, 15, 512),
            r["o_ps"][:, :, :, 1:].transpose(2, 3, 1, 0).reshape(1, NDEC, 15, 512),
            r["o_ct"][:, :, :3].transpose(2, 1, 0).reshape(1, 1, 3, 3072),
            r["o_cs"][:, :, :, 1:].transpose(2, 3, 1, 0).reshape(1, NDEC, 3, 3072),
            r["o_dp"].transpose(1, 0, 2)[None, None],
            r["o_ds"].reshape(HG, 128, NDEC, 128).transpose(2, 0, 1, 3)[None])
```
